# Optimizing a Trainium2 kernel written in Bass

```python
import jax, jax.numpy as jnp
from jax import lax
import numpy as np

D_MODEL = 1024
BATCH = 1
SEQ = 512
DEPTH = 1
DEC_BATCH = 1
DEC_SEQ = 32
PAST_LEN = 512

CHUNK = 64
N_META = 16
Q_BLOCK = 128
HEAD_DIM = 64
SB_HEADS = 8
DSA_HEADS = 8
DSA_KV_HEADS = 2
DSA_GROUP = DSA_HEADS // DSA_KV_HEADS
IDX_HEADS = 8
IDX_DIM = 64
TOPK_MAX = 256
ROPE_THETA = 10000.0
N_GROUPS = 4
EXPERTS_PER_GROUP = 8
N_EXPERTS = N_GROUPS * EXPERTS_PER_GROUP
EXPERT_TOPK = 2
EXPERT_DIM = 256
EPS = 1e-6

SB_WIDTH = SB_HEADS * HEAD_DIM
DSA_WIDTH = DSA_HEADS * HEAD_DIM
DSA_KV_WIDTH = DSA_KV_HEADS * HEAD_DIM
SB_SCALE = HEAD_DIM ** -0.5
ATTN_SCALE = HEAD_DIM ** -0.5
IDX_SCALE = IDX_DIM ** -0.5
IDX_W_SCALE = IDX_HEADS ** -0.5
IN_SPLIT_SIZES = (SB_WIDTH, SB_WIDTH, SB_WIDTH, DSA_WIDTH, DSA_KV_WIDTH, DSA_KV_WIDTH,
                  IDX_HEADS * IDX_DIM, IDX_DIM, IDX_HEADS, D_MODEL, D_MODEL)
IN_SPLITS = tuple(sum(IN_SPLIT_SIZES[:i + 1]) for i in range(len(IN_SPLIT_SIZES) - 1))
IN_COLS = sum(IN_SPLIT_SIZES)

kernel_name = 'chunk_stream_sb_dsa_hmoe_step'

def rms_norm(x, g):
    xf = x.astype(jnp.float32)
    y = xf * lax.rsqrt(jnp.mean(xf * xf, axis=-1, keepdims=True) + EPS)
    return (y * g.astype(jnp.float32)).astype(x.dtype)

def rope(x, pos):
    half = x.shape[-1] // 2
    freqs = ROPE_THETA ** (-jnp.arange(half, dtype=jnp.float32) / half)
    ang = pos.astype(jnp.float32)[:, None] * freqs[None, :]
    cos = jnp.cos(ang)[None, :, None, :]
    sin = jnp.sin(ang)[None, :, None, :]
    xf = x.astype(jnp.float32)
    x1, x2 = xf[..., :half], xf[..., half:]
    return jnp.concatenate([x1 * cos - x2 * sin, x2 * cos + x1 * sin], axis=-1).astype(x.dtype)

def prompt_chunk_id(pos):
    return jnp.where(pos < N_META, 0, (pos - N_META) // CHUNK + 1)

def project(x, pos, norm1_g, w_in, q_norm_g, k_norm_g):
    B, L, _ = x.shape
    xn = rms_norm(x, norm1_g)
    sq, sk, sv, dq, dk, dv, iq, ik, iw, g_sb, g_dsa = jnp.split(xn @ w_in, IN_SPLITS, axis=-1)
    sq = sq.reshape(B, L, SB_HEADS, HEAD_DIM)
    sk = sk.reshape(B, L, SB_HEADS, HEAD_DIM)
    sv = sv.reshape(B, L, SB_HEADS, HEAD_DIM)
    dq = rope(rms_norm(dq.reshape(B, L, DSA_HEADS, HEAD_DIM), q_norm_g), pos)
    dk = rope(rms_norm(dk.reshape(B, L, DSA_KV_HEADS, HEAD_DIM), k_norm_g), pos)
    dv = dv.reshape(B, L, DSA_KV_HEADS, HEAD_DIM)
    iq = rope(iq.reshape(B, L, IDX_HEADS, IDX_DIM), pos)
    ik = rope(ik[:, :, None, :], pos)[:, :, 0, :]
    return (sq, sk, sv, dq, dk, dv, iq, ik, iw, jax.nn.sigmoid(g_sb), jax.nn.sigmoid(g_dsa))

def sb_attend(q, k, v, q_pos, k_pos):
    z = jnp.einsum('bqhd,bkhd->bhqk', q, k).astype(jnp.float32) * SB_SCALE
    visible = (k_pos[None, :] < q_pos[:, None])[None, None]
    log_skip = jnp.where(visible, jax.nn.log_sigmoid(-z), 0.0)
    between = lax.cumsum(log_skip, axis=3, reverse=True) - log_skip
    weight = jnp.where(visible, jnp.exp(jax.nn.log_sigmoid(z) + between), 0.0)
    return jnp.einsum('bhqk,bkhd->bqhd', weight.astype(v.dtype), v)

def dsa_attend(q, iq, iw, q_chunk, k, v, ik, k_chunk, n_sel):
    B, Tq = q.shape[:2]
    iscore = jnp.einsum('bqhd,bkd->bqhk', iq, ik).astype(jnp.float32) * IDX_SCALE
    score = jnp.einsum('bqhk,bqh->bqk', jax.nn.relu(iscore), iw.astype(jnp.float32)) * IDX_W_SCALE
    admissible = k_chunk[None, :] <= q_chunk[:, None]
    score = jnp.where(admissible[None], score, -jnp.inf)
    _, sel = lax.top_k(score, n_sel)
    sel_ok = k_chunk[sel] <= q_chunk[None, :, None]
    k_sel = jax.vmap(lambda kb, ib: kb[ib])(k, sel)
    v_sel = jax.vmap(lambda vb, ib: vb[ib])(v, sel)
    qg = q.reshape(B, Tq, DSA_KV_HEADS, DSA_GROUP, HEAD_DIM)
    logits = jnp.einsum('bqhgd,bqkhd->bqhgk', qg, k_sel).astype(jnp.float32) * ATTN_SCALE
    logits = jnp.where(sel_ok[:, :, None, None, :], logits, -jnp.inf)
    p = jax.nn.softmax(logits, axis=-1).astype(v.dtype)
    out = jnp.einsum('bqhgk,bqkhd->bqhgd', p, v_sel)
    return out.reshape(B, Tq, DSA_HEADS, HEAD_DIM)

def pad_seq(a, length):
    return jnp.pad(a, [(0, 0), (0, length - a.shape[1])] + [(0, 0)] * (a.ndim - 2))

def to_blocks(a):
    B, Lp = a.shape[:2]
    return jnp.moveaxis(a.reshape((B, Lp // Q_BLOCK, Q_BLOCK) + a.shape[2:]), 1, 0)

def from_blocks(a):
    a = jnp.moveaxis(a, 0, 1)
    return a.reshape((a.shape[0], -1) + a.shape[3:])

def hier_moe(h, w_group, w_router, w_gate, w_up, w_down):
    B, L, D = h.shape
    xt = h.reshape(-1, D)
    group_probs = jax.nn.softmax((xt @ w_group).astype(jnp.float32), axis=-1)
    gp, gi = lax.top_k(group_probs, 1)
    elog = (xt @ w_router).astype(jnp.float32).reshape(-1, N_GROUPS, EXPERTS_PER_GROUP)
    elog = jnp.take_along_axis(elog, gi[:, :, None], axis=1)[:, 0]
    ev, ei = lax.top_k(elog, EXPERT_TOPK)
    ew = jax.nn.softmax(ev, axis=-1) * gp
    gid = gi * EXPERTS_PER_GROUP + ei
    comb = jnp.sum(jax.nn.one_hot(gid, N_EXPERTS, dtype=jnp.float32) * ew[..., None], axis=1).astype(h.dtype)
    y = jnp.zeros_like(xt)
    for g in range(N_GROUPS):
        sl = slice(g * EXPERTS_PER_GROUP, (g + 1) * EXPERTS_PER_GROUP)
        a = jnp.einsum('nd,edf->nef', xt, w_gate[sl])
        b = jnp.einsum('nd,edf->nef', xt, w_up[sl])
        hh = jax.nn.silu(a) * b * comb[:, sl, None]
        y = y + jnp.einsum('nef,efd->nd', hh, w_down[sl])
    return y.reshape(B, L, D)

def layer_tail(x, o_sb, o_dsa, g_sb, g_dsa, w_sb_branch, w_dsa_branch, w_out, norm2_g,
               w_group, w_router, w_gate, w_up, w_down):
    B, L, _ = x.shape
    merged = (g_sb * (o_sb.reshape(B, L, SB_WIDTH) @ w_sb_branch)
              + g_dsa * (o_dsa.reshape(B, L, DSA_WIDTH) @ w_dsa_branch))
    h = x + merged @ w_out
    return h + hier_moe(rms_norm(h, norm2_g), w_group, w_router, w_gate, w_up, w_down)

def setup_inputs(seed: int = 0) -> dict:
    key = jax.random.key(seed)
    ks = jax.random.split(key, 24)
    f32 = jnp.float32
    nrm = lambda k, shape, scale: scale * jax.random.normal(k, shape, f32)
    return {
        'x_prompt': nrm(ks[0], (BATCH, SEQ, D_MODEL), 1.0),
        'x_sample': nrm(ks[1], (DEC_BATCH, DEC_SEQ, D_MODEL), 1.0),
        'cache_sb_k': nrm(ks[2], (DEPTH, DEC_BATCH, PAST_LEN, SB_HEADS, HEAD_DIM), 1.0),
        'cache_sb_v': nrm(ks[3], (DEPTH, DEC_BATCH, PAST_LEN, SB_HEADS, HEAD_DIM), 1.0),
        'cache_dsa_k': nrm(ks[4], (DEPTH, DEC_BATCH, PAST_LEN, DSA_KV_HEADS, HEAD_DIM), 1.0),
        'cache_dsa_v': nrm(ks[5], (DEPTH, DEC_BATCH, PAST_LEN, DSA_KV_HEADS, HEAD_DIM), 1.0),
        'cache_idx_k': nrm(ks[6], (DEPTH, DEC_BATCH, PAST_LEN, IDX_DIM), 1.0),
        'meta_tokens': nrm(ks[7], (N_META, D_MODEL), 1.0),
        'norm1_g': 1.0 + nrm(ks[8], (DEPTH, D_MODEL), 0.02),
        'w_in': nrm(ks[9], (DEPTH, D_MODEL, IN_COLS), D_MODEL ** -0.5),
        'dsa_q_norm_g': 1.0 + nrm(ks[10], (DEPTH, HEAD_DIM), 0.02),
        'dsa_k_norm_g': 1.0 + nrm(ks[11], (DEPTH, HEAD_DIM), 0.02),
        'w_sb_branch': nrm(ks[12], (DEPTH, SB_WIDTH, D_MODEL), SB_WIDTH ** -0.5),
        'w_dsa_branch': nrm(ks[13], (DEPTH, DSA_WIDTH, D_MODEL), DSA_WIDTH ** -0.5),
        'w_out': nrm(ks[14], (DEPTH, D_MODEL, D_MODEL), D_MODEL ** -0.5),
        'norm2_g': 1.0 + nrm(ks[15], (DEPTH, D_MODEL), 0.02),
        'w_group': nrm(ks[16], (DEPTH, D_MODEL, N_GROUPS), D_MODEL ** -0.5),
        'w_router': nrm(ks[17], (DEPTH, D_MODEL, N_EXPERTS), D_MODEL ** -0.5),
        'w_gate': nrm(ks[18], (DEPTH, N_EXPERTS, D_MODEL, EXPERT_DIM), D_MODEL ** -0.5),
        'w_up': nrm(ks[19], (DEPTH, N_EXPERTS, D_MODEL, EXPERT_DIM), D_MODEL ** -0.5),
        'w_down': nrm(ks[20], (DEPTH, N_EXPERTS, EXPERT_DIM, D_MODEL), EXPERT_DIM ** -0.5),
    }

def reference(x_prompt, x_sample, cache_sb_k, cache_sb_v, cache_dsa_k, cache_dsa_v, cache_idx_k,
              meta_tokens, norm1_g, w_in, dsa_q_norm_g, dsa_k_norm_g, w_sb_branch, w_dsa_branch,
              w_out, norm2_g, w_group, w_router, w_gate, w_up, w_down):
    B = x_prompt.shape[0]
    meta = jnp.broadcast_to(meta_tokens[None].astype(x_prompt.dtype), (B, N_META, D_MODEL))
    xp = jnp.concatenate([meta, x_prompt], axis=1)
    Lr = xp.shape[1]
    Lp = -(-Lr // Q_BLOCK) * Q_BLOCK
    pos_p = jnp.arange(Lp, dtype=jnp.int32)
    chunk_p = prompt_chunk_id(pos_p)
    n_sel_p = min(TOPK_MAX, x_prompt.shape[1] // 4)
    xs = x_sample
    T = xs.shape[1]
    pos_s = PAST_LEN + jnp.arange(T, dtype=jnp.int32)
    chunk_s = pos_s // CHUNK
    kpos_s = jnp.arange(PAST_LEN + T, dtype=jnp.int32)
    kchunk_s = kpos_s // CHUNK
    n_sel_s = min(TOPK_MAX, (PAST_LEN + T) // 4)

    p_sbk, p_sbv, p_dk, p_dv, p_ik = [], [], [], [], []
    s_sbk, s_sbv, s_dk, s_dv, s_ik = [], [], [], [], []
    for layer in range(DEPTH):
        proj_w = (norm1_g[layer], w_in[layer], dsa_q_norm_g[layer], dsa_k_norm_g[layer])
        tail_w = (w_sb_branch[layer], w_dsa_branch[layer], w_out[layer], norm2_g[layer],
                  w_group[layer], w_router[layer], w_gate[layer], w_up[layer], w_down[layer])

        sq, sk, sv, dq, dk, dv, iq, ik, iw, g_sb, g_dsa = project(xp, pos_p[:Lr], *proj_w)
        skp, svp, dkp, dvp, ikp = (pad_seq(a, Lp) for a in (sk, sv, dk, dv, ik))
        o_sb = from_blocks(lax.map(
            lambda blk: sb_attend(blk[0], skp, svp, blk[1], pos_p),
            (to_blocks(pad_seq(sq, Lp)), pos_p.reshape(-1, Q_BLOCK))))[:, :Lr]
        o_dsa = from_blocks(lax.map(
            lambda blk: dsa_attend(blk[0], blk[1], blk[2], blk[3], dkp, dvp, ikp, chunk_p, n_sel_p),
            (to_blocks(pad_seq(dq, Lp)), to_blocks(pad_seq(iq, Lp)), to_blocks(pad_seq(iw, Lp)),
             chunk_p.reshape(-1, Q_BLOCK))))[:, :Lr]
        xp = layer_tail(xp, o_sb, o_dsa, g_sb, g_dsa, *tail_w)
        p_sbk.append(sk); p_sbv.append(sv); p_dk.append(dk); p_dv.append(dv); p_ik.append(ik)

        dt = xs.dtype
        tq, tk, tv, tdq, tdk, tdv, tiq, tik, tiw, tg_sb, tg_dsa = project(xs, pos_s, *proj_w)
        k_sb = jnp.concatenate([cache_sb_k[layer].astype(dt), tk], axis=1)
        v_sb = jnp.concatenate([cache_sb_v[layer].astype(dt), tv], axis=1)
        k_ds = jnp.concatenate([cache_dsa_k[layer].astype(dt), tdk], axis=1)
        v_ds = jnp.concatenate([cache_dsa_v[layer].astype(dt), tdv], axis=1)
        k_ix = jnp.concatenate([cache_idx_k[layer].astype(dt), tik], axis=1)
        o_sb_s = sb_attend(tq, k_sb, v_sb, pos_s, kpos_s)
        o_dsa_s = dsa_attend(tdq, tiq, tiw, chunk_s, k_ds, v_ds, k_ix, kchunk_s, n_sel_s)
        xs = layer_tail(xs, o_sb_s, o_dsa_s, tg_sb, tg_dsa, *tail_w)
        s_sbk.append(tk); s_sbv.append(tv); s_dk.append(tdk); s_dv.append(tdv); s_ik.append(tik)

    y_prompt = xp[:, N_META:]
    y_sample = xs
    return (y_prompt, y_sample,
            jnp.stack(p_sbk), jnp.stack(p_sbv), jnp.stack(p_dk), jnp.stack(p_dv), jnp.stack(p_ik),
            jnp.stack(s_sbk), jnp.stack(s_sbv), jnp.stack(s_dk), jnp.stack(s_dv), jnp.stack(s_ik))


_drawn_inputs = setup_inputs


def setup_inputs(seed=0):
    import zlib

    import numpy as np

    out = dict(_drawn_inputs(seed))
    spreads = {}
    factors = {'dsa_q_norm_g': 4.143, 'dsa_k_norm_g': 2.784}
    for name, (base, spread) in spreads.items():
        noise = np.random.default_rng([zlib.crc32(name.encode()), seed]).standard_normal(out[name].shape)
        drawn = base * np.exp(spread * noise) if base else spread * noise
        out[name] = __import__('jax').numpy.asarray(drawn.astype(out[name].dtype))
    for name, factor in factors.items():
        out[name] = (out[name] * factor).astype(out[name].dtype)
    return out
```

```python
from contextlib import ExitStack

import numpy as np

import concourse.bass as bass
from concourse import mybir

F32 = mybir.dt.float32
I32 = mybir.dt.int32
ACT = mybir.ActivationFunctionType
ALU = mybir.AluOpType
AX = mybir.AxisListType

P = 128
D = 1024
KT = D // P
HD = 64
HALF = HD // 2
NH = 8
NPAIR = NH // 2
N_META, SEQ, DEC, PAST, CHUNK = 16, 512, 32, 512, 64
N_PROMPT = N_META + SEQ
N_ROWS = N_PROMPT + DEC
OFF = [0, 80, 208, 336, 464]
ROWS = [80, 128, 128, 128, 96]
NT = len(OFF)
KEYS = [80, 208, 336, 464, PAST + DEC]
KEY_ROWS = [80, 128, 128, 128, 64]
NCB = PAST // P
SEL_PROMPT = min(256, SEQ // 4)
SEL_SAMPLE = min(256, (PAST + DEC) // 4)
EPS = 1e-6
NG, EPG, NE, FE = 4, 8, 32, 256
CAP = 64
MAX_OVER = (2 * N_ROWS) // CAP
NBLK = NE + MAX_OVER
N_SLOTS = NBLK * CAP
BIG = 1.0e30
HIDDEN = float(np.float32(-3.0e38))
Z_CAP = 30.0
TAKEN = float(np.float32(-3.2e38))

C_SQ, C_SK, C_SV, C_DQ, C_DK, C_IQ, C_IK, C_GSB, C_GDSA = 0, 512, 1024, 1536, 2048, 2304, 2816, 2888, 3912
N_SMALL1, N_SMALL2 = 72, 256

K_ID, K_NTRI, K_NONE, K_STRI, K_COS, K_SIN, K_IOTA, K_THR, K_VALID, K_RID = (
    0, 128, 256, 384, 512, 832, 1152, 1184, 1192, 1197)
K_COLS = 1202


def constants():
    c = np.zeros((P, K_COLS), np.float32)
    i = np.arange(P)
    c[:, K_ID:K_ID + P] = np.eye(P)
    c[:, K_NTRI:K_NTRI + P] = -(i[:, None] >= i[None, :]).astype(np.float32)
    c[:, K_NONE:K_NONE + P] = -1.0
    c[:, K_STRI:K_STRI + P] = (i[:, None] < i[None, :])
    freqs = np.float32(10000.0) ** (-np.arange(HALF, dtype=np.float32) / np.float32(HALF))
    for t in range(NT):
        pos = OFF[t] + i
        if t == NT - 1:
            pos = np.where(i < 64, pos, PAST + i - 64)
        ang = (pos.astype(np.float32)[:, None] * freqs[None, :].astype(np.float32)).astype(np.float64)
        c[:, K_COS + t * HD:K_COS + (t + 1) * HD] = np.concatenate([np.cos(ang), np.cos(ang)], 1)
        c[:, K_SIN + t * HD:K_SIN + (t + 1) * HD] = np.concatenate([-np.sin(ang), np.sin(ang)], 1)
        c[:ROWS[t], K_VALID + t] = 1.0
        c[:, K_RID + t] = OFF[t] + i
    c[:, K_IOTA:K_IOTA + NE] = np.arange(NE)
    c[:, K_THR:K_THR + 8] = CAP * (1 + np.arange(8))
    return c


def row_pieces(t):
    if t == 0:
        return [(0, N_META, "meta", 0), (N_META, ROWS[0], "prompt", 0)]
    if t == NT - 1:
        return [(0, 64, "prompt", OFF[t] - N_META), (64, 96, "sample", 0)]
    return [(0, P, "prompt", OFF[t] - N_META)]


GROUPS = [(208, N_PROMPT, [4, 3, 2, 1, 0]), (0, 208, [1, 0])]


def sb_steps():
    steps = []
    for pair in range(NPAIR):
        for g, (lo, hi, blocks) in enumerate(GROUPS):
            for n, j in enumerate(blocks):
                for half in range(2):
                    q0 = max(OFF[j], lo)
                    steps.append(dict(kind="prompt", pair=pair, g=g, half=half, j=j, lo=lo, hi=hi, q0=q0,
                                      n=hi - q0, nk=KEY_ROWS[j], diag=OFF[j] >= lo, first=n == 0,
                                      last=n == len(blocks) - 1, stream=2 * (g % 2) + half,
                                      cover0=max(OFF[blocks[n - 1]], lo) if n else hi,
                                      acc=2 * pair + g))
    for n, j in enumerate([NCB] + list(range(NCB - 1, -1, -1))):
        for half in range(2):
            steps.append(dict(kind="sample", half=half, j=j, n=NPAIR * DEC, nk=DEC if j == NCB else P,
                              diag=j == NCB, first=n == 0, last=j == 0, stream=half, acc=2 * NPAIR))
    return steps


STEPS = sb_steps()
NSTEP = len(STEPS)
ZR, SPR, WR = 6, 6, 3
TRI_LAG, PV_LAG = 3, 5


def build(nc, a, out):
    ctx = ExitStack()
    with ctx:
        def sem(name):
            return ctx.enter_context(nc.semaphore(name))

        def sems(name, n):
            return [sem(f"{name}{i}") for i in range(n)]

        def sb(name, cols, dt=F32, rows=P):
            return ctx.enter_context(nc.sbuf_tensor(name, [rows, cols], dt))

        SLOT = 3 * 2048
        arena = sb("arena", 4 * SLOT + KT * N_ROWS)
        xnT = sb("xnT", KT * N_ROWS)
        ring_w = sb("ring_w", 2 * 4096)
        hreg = sb("hreg", NT * D)
        cst = sb("cst", K_COLS)
        g1 = sb("g1", KT)
        gqk = sb("gqk", 4 * HD)
        tabs = sb("tabs", 4 * NT * HD)
        small = sb("small", 1400)

        at = [0]

        def carve(cols):
            s = arena[:, at[0]:at[0] + cols]
            at[0] += cols
            assert at[0] <= 4 * SLOT + KT * N_ROWS, at[0]
            return s

        sqT = carve(NPAIR * N_ROWS).rearrange("p (b r) -> p b r", b=NPAIR)
        skT = carve(NPAIR * N_ROWS).rearrange("p (b r) -> p b r", b=NPAIR)
        ksT = carve(NPAIR * PAST).rearrange("p (b r) -> p b r", b=NPAIR)
        svP = carve(NT * 512).rearrange("p (t c) -> p t c", t=NT)
        svC = carve(NCB * 512).rearrange("p (t c) -> p t c", t=NCB)
        svN = carve(512)
        dqT = carve(NPAIR * N_ROWS).rearrange("p (b r) -> p b r", b=NPAIR)
        dkiT = carve(3 * N_ROWS).rearrange("p (b r) -> p b r", b=3)
        dkiC = carve(3 * PAST).rearrange("p (b r) -> p b r", b=3)
        dvP = carve(NT * 128).rearrange("p (t c) -> p t c", t=NT)
        dvC = carve(NCB * 128).rearrange("p (t c) -> p t c", t=NCB)
        dvN = carve(128)
        sc0 = at[0]
        SC = [carve(k) for k in KEYS]
        natD = arena[:, sc0:sc0 + NCB * 384].rearrange("p (t b u c) -> p t b u c", t=NCB, b=3, u=2)
        rb = carve(2 * 512).rearrange("p (i c) -> p i c", i=2)
        mark = at[0]
        ropeA = carve(2 * 512).rearrange("p (i c) -> p i c", i=2)
        ropeB = carve(2 * 512).rearrange("p (i c) -> p i c", i=2)
        ropeQ = carve(2 * 512).rearrange("p (i c) -> p i c", i=2)
        kd = carve(NT * 384).rearrange("p (t b u c) -> p t b u c", t=NT, b=3, u=2)
        natS = carve(NCB * 512).rearrange("p (t c) -> p t c", t=NCB)
        skR = natS
        skR4 = carve(512)
        at[0] = mark
        spb = carve(SPR * 320).rearrange("p (i c) -> p i c", i=SPR)
        wtb = carve(WR * 320).rearrange("p (i c) -> p i c", i=WR)
        sufb = carve(4 * 320).rearrange("p (i c) -> p i c", i=4)
        Lb = carve(2 * 544).rearrange("p (i c) -> p i c", i=2)
        pb = carve(2 * 544).rearrange("p (i c) -> p i c", i=2)
        pTb = carve(2 * 512).rearrange("p (i c) -> p i c", i=2)
        oN = carve(512)
        merged = arena[:, 4 * SLOT:].rearrange("p (k r) -> p k r", k=KT)
        xT = xnT[:, :].rearrange("p (k r) -> p k r", k=KT)
        X = hreg[:, :].rearrange("p (t d) -> p t d", t=NT)
        osbT = hreg[:, 0:NPAIR * N_ROWS].rearrange("p (b r) -> p b r", b=NPAIR)
        odsaT = hreg[:, NPAIR * N_ROWS:2 * NPAIR * N_ROWS].rearrange("p (b r) -> p b r", b=NPAIR)
        zeros = hreg[:, 2 * NPAIR * N_ROWS:2 * NPAIR * N_ROWS + 512]
        iqT = odsaT
        wslot = [ring_w[:, s * 4096:(s + 1) * 4096] for s in range(2)]
        moe_w = [arena[:, s * SLOT:(s + 1) * SLOT] for s in range(4)]
        wslot_extra = moe_w[3][:, 0:4096]
        Xg = ring_w[0:CAP, 0:2 * D].rearrange("p (i d) -> p i d", i=2)
        Yb = ring_w[0:CAP, 2 * D:4 * D].rearrange("p (i d) -> p i d", i=2)
        xgT = ring_w[:, 4 * D:5 * D].rearrange("p (i k s) -> p i k s", i=2, k=KT)
        hidT = ring_w[:, 5 * D:5 * D + 512].rearrange("p (i g f s) -> p i g f s", i=2, g=2, f=2)
        x2row = arena[:, 4 * SLOT:4 * SLOT + 2 * D].rearrange("p (i d) -> p i d", i=2)
        g2b = arena[:, 4 * SLOT + 2 * D:4 * SLOT + 3 * D]

        so = [0]

        def sm(cols):
            s = small[:, so[0]:so[0] + cols]
            so[0] += cols
            assert so[0] <= 1400
            return s

        ss = sm(NT)
        rstd = sm(NT)
        ssq = sm(2 * NH).rearrange("p (i h) -> p i h", i=2)
        rq = sm(2 * NH).rearrange("p (i h) -> p i h", i=2)
        iws = sm(NT * NH).rearrange("p (t h) -> p t h", t=NT)
        top8 = sm(8)
        mhalf = sm(NH)
        mx = sm(2)
        nbias = sm(2)
        rsum = sm(2 * NH).rearrange("p (i h) -> p i h", i=2)
        rinv = sm(NH)
        wr = sm(KT * 36).rearrange("p (k c) -> p k c", k=KT)
        rl = sm(NT * 36).rearrange("p (t c) -> p t c", t=NT)
        oh = [sm(NT * NE).rearrange("p (t e) -> p t e", t=NT) for _ in range(2)]
        gx = sm(64)
        ew = [sm(NT) for _ in range(2)]
        elg = sm(NT * 8).rearrange("p (t e) -> p t e", t=NT)
        v_max, v_rest, v_base, v_gp, v_p, v_o = (sm(NT) for _ in range(6))
        v_top = [sm(NT) for _ in range(2)]
        v_e = [sm(NT) for _ in range(2)]
        g_eq = sm(NT * NG).rearrange("p (t g) -> p t g", t=NT)
        elm = sm(NT * EPG).rearrange("p (t e) -> p t e", t=NT)
        elx = sm(NT * EPG).rearrange("p (t e) -> p t e", t=NT)
        rt = sb("rt", NT * NE * 3 + 400)
        slot_i = [sb(f"slot_i{c}", NT, I32) for c in range(2)]
        rid_i = sb("rid_i", NT, I32)
        zero_i = sb("zero_i", CAP, I32, NBLK)
        idxs = sb("idxs", NBLK, I32, CAP)
        idx_now = sb("idx_now", 2, I32, CAP)
        over_i = sb("over_i", MAX_OVER + 1, I32, 1)

        ident = cst[:, K_ID:K_ID + P]
        ntri = cst[:, K_NTRI:K_NTRI + P]
        nones = cst[:, K_NONE:K_NONE + P]
        stri = cst[:, K_STRI:K_STRI + P]
        cos = cst[:, K_COS:K_COS + NT * HD].rearrange("p (t c) -> p t c", t=NT)
        sin = cst[:, K_SIN:K_SIN + NT * HD].rearrange("p (t c) -> p t c", t=NT)
        iota = cst[:, K_IOTA:K_IOTA + NE]
        thr = cst[:, K_THR:K_THR + 8]
        valid = cst[:, K_VALID:K_VALID + NT]
        rid = cst[:, K_RID:K_RID + NT]
        tab = tabs[:, :].rearrange("p (w t c) -> p w t c", w=4, t=NT)

        pair01 = ctx.enter_context(nc.psum_tensor("pair01", [P, 1024], F32))
        pair23 = ctx.enter_context(nc.psum_tensor("pair23", [P, 1024], F32))
        pair45 = ctx.enter_context(nc.psum_tensor("pair45", [P, 1024], F32))
        pair67 = ctx.enter_context(nc.psum_tensor("pair67", [P, 1024], F32))
        pairs = [pair01, pair23, pair45, pair67]
        bank = [p[:, s * 512:(s + 1) * 512] for p in pairs for s in range(2)]

        xn2_d = nc.dram_tensor("xn2_d", [N_ROWS, D], F32).ap()
        slot_row_d = nc.dram_tensor("slot_row_d", [N_SLOTS, 1], I32).ap()
        y_d = nc.dram_tensor("y_d", [N_SLOTS, D], F32).ap()

        const_in = sem("const_in")
        gains_in = sem("gains_in")
        x_in = sems("x_in", NT)
        cache_k_in = sem("cache_k_in")
        cache_v_in = sem("cache_v_in")
        chunk_in = sems("chunk_in", 14)
        ss_ready = sem("ss_ready")
        rstd_ready = sem("rstd_ready")
        rstd2_ready = sem("rstd2_ready")
        xs_ready = sem("xs_ready")
        tr_ready = sem("tr_ready")
        tr_free_act = sem("tr_free_act")
        tr_free_dve = sem("tr_free_dve")
        pj_ready = sem("pj_ready")
        pj_free_act = sem("pj_free_act")
        pj_free_dve = sem("pj_free_dve")
        tables_ready = sem("tables_ready")
        rope_parts = sem("rope_parts")
        squares = sem("squares")
        rows_ready = sem("rows_ready")
        ix_ready = sem("ix_ready")
        relu_ready = sem("relu_ready")
        relu_used = sem("relu_used")
        topk_done = sem("topk_done")
        vnew_in = sem("vnew_in")
        keys_out = sem("keys_out")
        sk_rows = sem("sk_rows")
        sv_rows = sem("sv_rows")
        small_rows = sem("small_rows")
        z_ready = sem("z_ready")
        cap_ready = sem("cap_ready")
        ln_ready = sem("ln_ready")
        sp_ready = sem("sp_ready")
        sp_masked = sem("sp_masked")
        suf_ready = sem("suf_ready")
        logw_ready = sem("logw_ready")
        w_ready = sem("w_ready")
        w_masked = sem("w_masked")
        pv_done = sem("pv_done")
        acc_ready = sem("acc_ready")
        acc_free = sem("acc_free")
        lg_ready = sem("lg_ready")
        lb_ready = sem("lb_ready")
        p_ready = sem("p_ready")
        pT_ready = sem("pT_ready")
        pT_copied = sem("pT_copied")
        o_ready = sem("o_ready")
        on_ready = sem("on_ready")
        oT_ready = sem("oT_ready")
        oT_copied = sem("oT_copied")
        pvd_done = sem("pvd_done")
        gate_ready = sem("gate_ready")
        half_merged = sem("half_merged")
        merged_ready = sem("merged_ready")
        xres_in = sem("xres_in")
        wr_in = sem("wr_in")
        g2_in = sem("g2_in")
        h_ready = sem("h_ready")
        ss2_ready = sem("ss2_ready")
        x2_ready = sem("x2_ready")
        x2_stored = sems("x2_stored", NT)
        logits_ready = sem("logits_ready")
        rexp_ready = sem("rexp_ready")
        rvals_ready = sem("rvals_ready")
        gvals_ready = sem("gvals_ready")
        onehot_ready = sem("onehot_ready")
        pos_ready = sem("pos_ready")
        slots_ready = sem("slots_ready")
        table_zero = sem("table_zero")
        table_done = sem("table_done")
        idx_in = sem("idx_in")
        mw_in = sems("mw_in", 4)
        idx_now_ready = sem("idx_now_ready")
        gath = sems("gath", 2)
        xgp_ready = sems("xgp_ready", 2)
        xgT_ready = sem("xgT_ready")
        gu_ready = sem("gu_ready")
        silu_ready = sem("silu_ready")
        hid_ready = sem("hid_ready")
        y_done = sems("y_done", 4)
        y_copied_act = sems("y_copied_act", 2)
        y_copied_dve = sems("y_copied_dve", 2)
        y_out = sems("y_out", 2)
        o_w = sem("o_w")
        o_idx = sem("o_idx")
        o_g = sem("o_g")
        o_step = sem("o_step")
        comb_in = sems("comb_in", 4)
        comb_used = sem("comb_used")
        final_ready = sem("final_ready")
        y_final_out = sem("y_final_out")
        pe_turns = sem("pe_turns")
        pool_turns = sem("pool_turns")
        zero_ready = sem("zero_ready")
        y_zeroed = sem("y_zeroed")
        act_chain = sem("act_chain")
        dve_chain = sem("dve_chain")
        pool_chain = sem("pool_chain")

        slots = [0, 1, 0, 1, 0, 1, 0, 1, 0, 1, 0, 2, 1, 0]
        chunk_at = [wslot_extra if s == 2 else wslot[s] for s in slots]

        used_at = [5, 10, 15, 20, 28, 36, 44, 52, 68, 100, 84, 100, 110, 110]

        def free_before(n):
            return max([used_at[m] for m in range(n) if slots[m] == slots[n]], default=0)

        win = a["w_in"].rearrange("(p k) c -> p k c", k=KT)

        def load_chunk(eng, n):
            if slots[n] != 2 and free_before(n):
                eng.wait_ge(pj_ready, free_before(n))
            v = chunk_at[n]
            if n == 1:
                v = v[:, 0:KT * 328].rearrange("p (k c) -> p k c", k=KT)
                eng.dma_start(v[:, :, 0:N_SMALL1], win[:, :, C_IK:C_IK + N_SMALL1]).then_inc(chunk_in[n], 16)
                eng.dma_start(v[:, :, N_SMALL1:328], win[:, :, C_DK:C_DK + N_SMALL2]).then_inc(chunk_in[n], 16)
                return
            v8 = v.rearrange("p (k c) -> p k c", k=KT)
            col = {0: C_IQ, 2: C_DQ, 3: C_SV, 4: C_SK, 5: C_SQ, 6: C_GSB, 7: C_GSB + 512,
                   10: C_GDSA, 11: C_GDSA + 512}
            if n in col:
                src, v = win[:, :, col[n]:col[n] + 512], v8
            elif n in (8, 9):
                src = a["w_sb_branch" if n == 8 else "w_dsa_branch"].rearrange("(k p) c -> p k c", p=P)
                v = v.rearrange("p (k c) -> p k c", k=4)
            else:
                src = a["w_out"].rearrange("(k p) c -> p k c", p=P)[:, :, (n - 12) * 512:(n - 11) * 512]
                v = v8
            eng.dma_start(v, src).then_inc(chunk_in[n], 16)

        def chunk_arrived(eng, n):
            eng.wait_ge(chunk_in[n], 32 if n == 1 else 16)

        PJ = (["dve"] * 15 + ["act"] * (NT + 16) + ["act"] * 16 + ["dve"] * 16 + ["act", "dve"] * 16
              + ["dve"] * 10 + ["act"] * NT)
        J_IQ, J_SM, J_DQ, J_SV, J_SK, J_SQ = 0, 5, 10, 15, 20, 28
        J_GSB, J_A, J_GB, J_WO, J_RT = 36, 52, 68, 100, 110
        TR = ["dve"] * 10 + ["act"] * 8 + ["act"] * 20 + ["act"] * 10
        T_X, T_C, T_IQ, T_SM, T_DQ, T_SK, T_X2 = 0, 10, 18, 23, 28, 33, 38

        def emptied(order, who, n):
            return sum(w == who for w in order[:n + 1])

        def pj_wait_free(eng, n):
            if n >= 4:
                who = PJ[n - 4]
                eng.wait_ge(pj_free_act if who == "act" else pj_free_dve, emptied(PJ, who, n - 4))

        def tr_wait_free(eng, n):
            if n >= 2:
                who = TR[n - 2]
                eng.wait_ge(tr_free_act if who == "act" else tr_free_dve, emptied(TR, who, n - 2))

        FG = [(0, 280), (280, 560)]
        IX = []
        for t in range(1, NT):
            for h in range(NH):
                IX += [(t, h, 0, 272), (t, h, 272, 544)] if t == NT - 1 else [(t, h, 0, KEYS[t])]

        block = ctx.enter_context(nc.Block())

        @block.sync
        def _(sp):
            sp.dma_start(X[0:N_META, 0, :], a["meta_tokens"]).then_inc(x_in[0], 16)
            sp.dma_start(X[N_META:ROWS[0], 0, :], a["x_prompt"][0:ROWS[0] - N_META, :]).then_inc(x_in[0], 16)
            sp.dma_start(cst[:, :], a["consts"]).then_inc(const_in, 16)
            sp.dma_start(g1[:, :], a["norm1_g"].rearrange("(p k) -> p k", k=KT)).then_inc(gains_in, 16)
            for t in range(1, NT):
                for p0, p1, which, r0 in row_pieces(t):
                    sp.dma_start(X[p0:p1, t, :], a["x_" + which][r0:r0 + p1 - p0, :]).then_inc(x_in[t], 16)
            load_chunk(sp, 0)
            for w, name in enumerate(("dsa_q_norm_g", "dsa_k_norm_g")):
                g = a[name].rearrange("(o c) -> o c", o=1)
                q = gqk[:, 2 * w * HD:2 * (w + 1) * HD]
                sp.dma_start(q[:, 0:HD], g.broadcast_to([P, HD])).then_inc(gains_in, 16)
                sp.dma_start(q[:, HD:HD + HALF], g[:, HALF:HD].broadcast_to([P, HALF])).then_inc(gains_in, 16)
                sp.dma_start(q[:, HD + HALF:2 * HD], g[:, 0:HALF].broadcast_to([P, HALF])).then_inc(gains_in, 16)
            sp.dma_start(natS, a["cache_sb_k"].rearrange("(t p) c -> p t c", p=P)).then_inc(cache_k_in, 16)
            for u in range(2):
                for b in range(2):
                    sp.dma_start(natD[:, :, b, u, :],
                                 a["cache_dsa_k"][:, b, :].rearrange("(t p) c -> p t c", p=P)).then_inc(cache_k_in, 16)
                sp.dma_start(natD[:, :, 2, u, :],
                             a["cache_idx_k"].rearrange("(t p) c -> p t c", p=P)).then_inc(cache_k_in, 16)
            load_chunk(sp, 1)
            sp.dma_start(svC, a["cache_sb_v"].rearrange("(t p) c -> p t c", p=P)).then_inc(cache_v_in, 16)
            sp.dma_start(dvC, a["cache_dsa_v"].rearrange("(t p) c -> p t c", p=P)).then_inc(cache_v_in, 16)
            load_chunk(sp, 2)

            def store_rows(src, dst_prompt, dst_sample, t):
                n = KEY_ROWS[t]
                sp.dma_start(dst_prompt[OFF[t]:OFF[t] + n, :], src[0:n]).then_inc(keys_out, 16)
                if t == NT - 1:
                    sp.dma_start(dst_sample[:, :], src[64:96]).then_inc(keys_out, 16)

            load_chunk(sp, 3)
            for t in range(NT):
                sp.wait_ge(small_rows, t + 1)
                for b in range(2):
                    store_rows(kd[:, t, b, 0, :], out["dk_p"][:, b, :], out["dk_s"][:, b, :], t)
                store_rows(kd[:, t, 2, 0, :], out["ik_p"], out["ik_s"], t)
                store_rows(dvP[:, t, :], out["dv_p"], out["dv_s"], t)
            sp.dma_start(dvN[0:DEC, :], dvP[64:96, NT - 1, :]).then_inc(vnew_in, 16)
            load_chunk(sp, 4)
            load_chunk(sp, 5)
            for t in range(NT):
                sp.wait_ge(sv_rows, t + 1)
                store_rows(svP[:, t, :], out["sv_p"], out["sv_s"], t)
            sp.dma_start(svN[0:DEC, :], svP[64:96, NT - 1, :]).then_inc(vnew_in, 16)
            load_chunk(sp, 6)
            load_chunk(sp, 7)
            for t in range(NT):
                sp.wait_ge(sk_rows, t + 1)
                store_rows(skR4 if t == NT - 1 else skR[:, t, :], out["sk_p"], out["sk_s"], t)
            wg = a["w_gate"].rearrange("e (p k) f -> (e p) (k f)", k=KT)
            wu = a["w_up"].rearrange("e (p k) f -> (e p) (k f)", k=KT)
            wd = a["w_down"].rearrange("e (p j) c -> (e p) (j c)", j=2)
            sp.wait_ge(oT_copied, NT)
            sp.wait_ge(acc_free, 2 * NPAIR + 1)
            sp.wait_ge(vnew_in, 32)
            with sp.Fori(0, NE // 4) as i:
                for s in range(4):
                    if s == 3:
                        sp.wait_ge(pj_ready, used_at[11])
                    sp.wait_ge(y_done[s], i)
                    for n, w in enumerate((wg, wu, wd)):
                        sp.dma_start(moe_w[s][:, n * 2048:(n + 1) * 2048],
                                     w[bass.ds((i * 4 + s) * P, P), :]).then_inc(mw_in[s], 16)
            over = sp.value_load(over_i[0:1, MAX_OVER:MAX_OVER + 1], min_val=0, max_val=MAX_OVER)
            with sp.If(over > 0):
                with sp.Fori(0, MAX_OVER) as b:
                    sp.wait_ge(o_step, b * 8)
                    e = sp.value_load(over_i[0:1, bass.ds(b, 1)], min_val=0, max_val=NE - 1)
                    for n, w in enumerate((wg, wu, wd)):
                        sp.dma_start(moe_w[0][:, n * 2048:(n + 1) * 2048],
                                     w[bass.ds(e * P, P), :]).then_inc(o_w, 16)
            for t in range(NT):
                sp.wait_ge(final_ready, t + 1)
                for p0, p1, which, r0 in row_pieces(t):
                    if which != "meta":
                        sp.dma_start(out["y_" + which][r0:r0 + p1 - p0, :], X[p0:p1, t, :]).then_inc(y_final_out, 16)
            sp.wait_ge(y_final_out, 16 * (NT + 1))
            sp.wait_ge(keys_out, 16 * 6 * (NT + 1))

        @block.tensor
        def _(pe):
            tr = [0]
            pj = [0]

            def tr_job(items, n):
                tr_wait_free(pe, tr[0])
                b = bank[4 + tr[0] % 2]
                for i, (src, idn) in enumerate(items):
                    cols = src.shape[1]
                    last = nc.tensor.transpose(b[0:cols, i * n:i * n + src.shape[0]], src, idn)
                last.then_inc(tr_ready, 1)
                tr[0] += 1

            def pj_job(mms, view):
                pj_wait_free(pe, pj[0])
                o = view(bank[pj[0] % 4])
                for i, (l, r) in enumerate(mms):
                    last = nc.tensor.matmul(o, l, r, start=i == 0, stop=i == len(mms) - 1)
                last.then_inc(pj_ready, 1)
                pj[0] += 1

            pe.wait_ge(const_in, 16)
            for t in range(NT):
                pe.wait_ge(xs_ready, t + 1)
                xk = X[0:ROWS[t], t, :].rearrange("p (c k) -> p k c", k=KT)
                for q in range(2):
                    tr_job([(xk[:, 4 * q + i, :], ident[0:ROWS[t], 0:ROWS[t]]) for i in range(4)], ROWS[t])
            pe.wait_ge(cache_k_in, 16 * 7)
            for c in range(NCB):
                tr_job([(natS[:, c, P * i:P * (i + 1)], ident) for i in range(4)], P)
                tr_job([(natD[:, c, i].rearrange("p u c -> p (u c)"), ident) for i in range(3)], P)

            def by_rows(n, t, cols):
                v = chunk_at[n][:, 0:KT * cols].rearrange("p (k c) -> p k c", k=KT)
                pj_job([(xT[:, k, OFF[t]:OFF[t] + ROWS[t]], v[:, k, :]) for k in range(KT)],
                       lambda b: b[0:ROWS[t], 0:cols])

            def roped_chunk(n, cols, rows_before, tile):
                chunk_arrived(pe, n)
                for t in range(NT + 1):
                    if t < NT:
                        by_rows(n, t, cols)
                    if t:
                        pe.wait_ge(rows_ready, rows_before + t)
                        tr_job(tile(t - 1), ROWS[t - 1])

            pe.wait_ge(tr_free_dve, 10)
            tile4 = lambda t: [(ropeA[0:ROWS[t], t % 2, P * i:P * (i + 1)], ident[0:ROWS[t], 0:ROWS[t]])
                               for i in range(4)]
            roped_chunk(0, 512, 0, tile4)
            roped_chunk(1, 328, NT, lambda t: [(kd[0:ROWS[t], t, i].rearrange("p u c -> p (u c)"),
                                                ident[0:ROWS[t], 0:ROWS[t]]) for i in range(3)])

            pe.wait_ge(tr_free_act, emptied(TR, "act", T_DQ - 1))
            for i, (t, h, k0, k1) in enumerate(IX):
                if i >= 2:
                    pe.wait_ge(relu_ready, i - 1)
                b = bank[6 + i % 2]
                hp = slice(64 * (h % 2), 64 * (h % 2) + 64)
                n = KEY_ROWS[t]
                last = nc.tensor.matmul(b[0:n, 0:k1 - k0], iqT[hp, h // 2, OFF[t]:OFF[t] + n], dkiT[hp, 2, k0:k1],
                                        start=True, stop=True)
                if t == NT - 1:
                    q = iqT[hp, h // 2, N_PROMPT:N_ROWS]
                    last = nc.tensor.matmul(b[64:96, 0:min(k1, PAST) - k0], q, dkiC[hp, 2, k0:min(k1, PAST)],
                                            start=True, stop=True)
                    if k1 > PAST:
                        last = nc.tensor.matmul(b[64:96, PAST - k0:k1 - k0], q, dkiT[hp, 2, N_PROMPT:N_ROWS],
                                                start=True, stop=True)
                last.then_inc(ix_ready, 1)

            roped_chunk(2, 512, 2 * NT, tile4)
            chunk_arrived(pe, 3)
            for t in range(NT):
                by_rows(3, t, 512)

            def by_width(v, rhs, cb, g):
                lo, hi = FG[g]
                kt = v.shape[1]
                pj_job([(v[:, k, P * cb:P * (cb + 1)], rhs[:, k, lo:hi]) for k in range(kt)],
                       lambda b: b[:, 0:hi - lo])

            def chunk8(n):
                return chunk_at[n].rearrange("p (k c) -> p k c", k=KT)

            for n in (4, 5):
                chunk_arrived(pe, n)
                for cb in range(4):
                    for g in range(2):
                        by_width(chunk8(n), xT, cb, g)
            for t in range(NT):
                tr_job([(skT[:, i, OFF[t]:OFF[t] + ROWS[t]], ident) for i in range(4)], P)

            pe.wait_ge(pj_free_act, emptied(PJ, "act", J_GSB - 1))
            pe.wait_ge(pj_free_dve, emptied(PJ, "dve", J_GSB - 1))
            pe.wait_ge(tr_free_act, emptied(TR, "act", T_X2 - 1))
            pe.wait_ge(relu_ready, len(IX))
            pe.wait_ge(cache_v_in, 32)
            pe.wait_ge(vnew_in, 32)
            for i in range(NSTEP + PV_LAG):
                if i < NSTEP:
                    s = STEPS[i]
                    if i >= ZR:
                        pe.wait_ge(w_ready, i - ZR + 1)
                    z = bank[2 + i % ZR]
                    if s["kind"] == "prompt":
                        hp = slice(64 * s["half"], 64 * s["half"] + 64)
                        last = nc.tensor.matmul(z[0:s["nk"], 0:s["n"]],
                                                skT[hp, s["pair"], OFF[s["j"]]:OFF[s["j"]] + s["nk"]],
                                                sqT[hp, s["pair"], s["q0"]:s["hi"]], start=True, stop=True,
                                                skip_group_check=True)
                    else:
                        hp = slice(64 * s["half"], 64 * s["half"] + 64)
                        for b in range(NPAIR):
                            k = (skT[hp, b, N_PROMPT:N_ROWS] if s["diag"]
                                 else ksT[hp, b, P * s["j"]:P * (s["j"] + 1)])
                            last = nc.tensor.matmul(z[0:s["nk"], b * DEC:(b + 1) * DEC], k,
                                                    sqT[hp, b, N_PROMPT:N_ROWS], start=b == 0, stop=True,
                                                    skip_group_check=True)
                    last.then_inc(z_ready, 1)
                m = i - TRI_LAG
                if 0 <= m < NSTEP:
                    s = STEPS[m]
                    z = bank[2 + m % ZR]
                    pe.wait_ge(sp_masked, m + 1)
                    last = nc.tensor.matmul(z[0:s["nk"], 0:s["n"]], ntri[0:s["nk"], 0:s["nk"]],
                                            spb[0:s["nk"], m % SPR, 0:s["n"]], start=False, stop=True,
                                            skip_group_check=True)
                    if not s["first"]:
                        pe.wait_ge(suf_ready, m - 1)
                        c0 = s["cover0"] - s["q0"] if s["kind"] == "prompt" else 0
                        o0 = s["cover0"] - s["lo"] if s["kind"] == "prompt" else 0
                        last = nc.tensor.matmul(z[0:s["nk"], c0:s["n"]], nones[:, 0:s["nk"]],
                                                sufb[:, s["stream"], o0:o0 + s["n"] - c0], start=False, stop=True,
                                                skip_group_check=True)
                    last.then_inc(logw_ready, 1)
                m = i - PV_LAG
                if 0 <= m < NSTEP:
                    s = STEPS[m]
                    pe.wait_ge(w_masked, m + 1)
                    acc = bank[s["acc"] % 2]
                    if s["first"] and s["acc"] >= 2:
                        pe.wait_ge(acc_free, s["acc"] - 1)
                    if s["kind"] == "prompt":
                        h = 2 * s["pair"] + s["half"]
                        o = acc[64 * s["half"]:64 * s["half"] + 64, s["q0"] - s["lo"]:s["hi"] - s["lo"]]
                        last = nc.tensor.matmul(o, svP[0:s["nk"], s["j"], 64 * h:64 * h + 64],
                                                wtb[0:s["nk"], m % WR, 0:s["n"]], start=s["first"], stop=s["last"],
                                                skip_group_check=True)
                    else:
                        for b in range(NPAIR):
                            h = 2 * b + s["half"]
                            v = svN[0:DEC, 64 * h:64 * h + 64] if s["diag"] else svC[:, s["j"], 64 * h:64 * h + 64]
                            o = acc[64 * s["half"]:64 * s["half"] + 64, DEC * b:DEC * (b + 1)]
                            last = nc.tensor.matmul(o, v, wtb[0:s["nk"], m % WR, b * DEC:(b + 1) * DEC],
                                                    start=s["first"] and b == 0, stop=True, skip_group_check=True)
                    last.then_inc(pv_done, 1)

            pe.wait_ge(acc_free, 2 * NPAIR + 1)
            jobs = [(t, h) for t in range(NT) for h in range(NH)]

            def out_T(t):
                pe.wait_ge(on_ready, t + 1)
                b = bank[4]
                pe.wait_ge(pT_copied, min(NH * (t + 1) + 1, NT * NH))
                for q in range(4):
                    last = nc.tensor.transpose(b[:, q * ROWS[t]:(q + 1) * ROWS[t]], oN[0:ROWS[t], P * q:P * (q + 1)],
                                               ident[0:ROWS[t], 0:ROWS[t]])
                last.then_inc(oT_ready, 1)

            for i in range(len(jobs) + 3):
                if i < len(jobs):
                    t, h = jobs[i]
                    if i >= 2:
                        pe.wait_ge(lb_ready, i - 1)
                    pr = pairs[i % 2]
                    hp = slice(64 * (h % 2), 64 * (h % 2) + 64)
                    kv = h // 4
                    n = KEY_ROWS[t]
                    q = dqT[hp, h // 2, OFF[t]:OFF[t] + n]
                    if t < NT - 1:
                        last = nc.tensor.matmul(pr[0:n, 0:KEYS[t]], q, dkiT[hp, kv, 0:KEYS[t]], start=True, stop=True)
                    else:
                        qs = dqT[hp, h // 2, N_PROMPT:N_ROWS]
                        for b in range(2):
                            k0, k1 = 272 * b, 272 * (b + 1)
                            o = pr[:, 512 * b:512 * b + 272]
                            nc.tensor.matmul(o[0:64, :], q, dkiT[hp, kv, k0:k1], start=True, stop=True)
                            last = nc.tensor.matmul(o[64:96, 0:min(k1, PAST) - k0], qs, dkiC[hp, kv, k0:min(k1, PAST)],
                                                    start=True, stop=True)
                        last = nc.tensor.matmul(o[64:96, PAST - k0:272], qs, dkiT[hp, kv, N_PROMPT:N_ROWS],
                                                start=True, stop=True)
                    last.then_inc(lg_ready, 1)
                m = i - 1
                if 0 <= m < len(jobs):
                    t, h = jobs[m]
                    pe.wait_ge(p_ready, m + 1)
                    if m >= 2:
                        pe.wait_ge(pT_copied, m - 1)
                    if h == 2 and t:
                        pe.wait_ge(oT_copied, t)
                    b = bank[4 + m % 2]
                    r = ROWS[t]
                    for kb in range(t + 1):
                        nk = KEY_ROWS[kb]
                        n = KEY_ROWS[t]
                        last = nc.tensor.transpose(b[0:nk, kb * r:kb * r + n], pb[0:n, m % 2, OFF[kb]:OFF[kb] + nk],
                                                   ident[0:n, 0:n])
                    if t == NT - 1:
                        for kb in range(NCB + 1):
                            nk = P if kb < NCB else DEC
                            last = nc.tensor.transpose(b[0:nk, kb * r + 64:kb * r + 96],
                                                       pb[64:96, m % 2, P * kb:P * kb + nk], ident[64:96, 64:96])
                    last.then_inc(pT_ready, 1)
                m = i - 2
                if 0 <= m < len(jobs):
                    t, h = jobs[m]
                    pe.wait_ge(pT_copied, m + 1)
                    if h == 0 and t >= 2:
                        pe.wait_ge(on_ready, t - 1)
                    b = bank[6 + t % 2]
                    kv = h // 4
                    r = ROWS[t]
                    n = KEY_ROWS[t]
                    for kb in range(t + 1):
                        nk = KEY_ROWS[kb]
                        last = nc.tensor.matmul(b[0:n, 64 * h:64 * h + 64], pTb[0:nk, m % 2, kb * r:kb * r + n],
                                                dvP[0:nk, kb, 64 * kv:64 * kv + 64], start=kb == 0, stop=kb == t)
                    if t == NT - 1:
                        for kb in range(NCB + 1):
                            nk = P if kb < NCB else DEC
                            v = dvC[:, kb] if kb < NCB else dvN[0:DEC]
                            last = nc.tensor.matmul(b[64:96, 64 * h:64 * h + 64],
                                                    pTb[0:nk, m % 2, kb * r + 64:kb * r + 96],
                                                    v[:, 64 * kv:64 * kv + 64], start=kb == 0, stop=kb == NCB)
                    last.then_inc(pvd_done, 1)
                m = i - 3
                if 0 <= m < len(jobs) and jobs[m][1] == NH - 1:
                    out_T(jobs[m][0])

            pe.wait_ge(oT_copied, NT)
            for n in (6, 7):
                chunk_arrived(pe, n)
                for cb in range(4):
                    for g in range(2):
                        by_width(chunk8(n), xT, cb, g)
            chunk_arrived(pe, 8)
            for cb in range(8):
                for g in range(2):
                    by_width(chunk_at[8].rearrange("p (k c) -> p k c", k=4), osbT, cb, g)
            chunk_arrived(pe, 9)
            for cb in range(8):
                chunk_arrived(pe, 10 + cb // 4)
                for g in range(2):
                    by_width(chunk8(10 + cb // 4), xT, cb % 4, g)
                    by_width(chunk_at[9].rearrange("p (k c) -> p k c", k=4), odsaT, cb, g)
            pe.wait_ge(merged_ready, 16)
            chunk_arrived(pe, 12)
            chunk_arrived(pe, 13)
            for t in range(NT):
                for c in range(2):
                    pj_job([(merged[:, k, OFF[t]:OFF[t] + ROWS[t]], chunk8(12 + c)[:, k, :]) for k in range(KT)],
                           lambda b: b[0:ROWS[t], :])
            pe.wait_ge(wr_in, 32)
            for t in range(NT):
                pe.wait_ge(x2_ready, t + 1)
                xk = x2row[0:ROWS[t], t % 2, :].rearrange("p (c k) -> p k c", k=KT)
                for q in range(2):
                    tr_job([(xk[:, 4 * q + i, :], ident[0:ROWS[t], 0:ROWS[t]]) for i in range(4)], ROWS[t])
            for t in range(NT):
                pe.wait_ge(tr_free_act, emptied(TR, "act", T_X2 + 2 * t + 1))
                pj_job([(xT[:, k, OFF[t]:OFF[t] + ROWS[t]], wr[:, k, :]) for k in range(KT)],
                       lambda b: b[0:ROWS[t], 0:36])
            pe.wait_ge(onehot_ready, 1)
            M = rt[:, 0:NT * NE].rearrange("p (t e) -> p t e", t=NT)
            b = bank[0]
            pe.wait_ge(pj_free_act, emptied(PJ, "act", len(PJ) - 1))
            for t in range(NT):
                for u in range(t + 1):
                    last = nc.tensor.matmul(b[:, NE * t:NE * (t + 1)], stri if u == t else nones, M[:, u, :] if u == t
                                            else rt[:, NT * NE + u * NE:NT * NE + (u + 1) * NE],
                                            start=u == 0, stop=u == t)
            for u in range(NT):
                last = nc.tensor.matmul(b[:, NE * NT:NE * (NT + 1)], nones,
                                        rt[:, NT * NE + u * NE:NT * NE + (u + 1) * NE], start=u == 0, stop=u == NT - 1)
            last.then_inc(pos_ready, 1)

            def expert(x, xp, xt, gu, hid, y, w, waits, incs):
                waits("x")
                for k in range(KT):
                    last = nc.tensor.transpose(xp[:, k * CAP:(k + 1) * CAP],
                                               x.rearrange("p (c k) -> p k c", k=KT)[:, k, :], ident[0:CAP, 0:CAP])
                incs("xp", last)
                waits("xt")
                for g in range(2):
                    wv = w[:, g * 2048:(g + 1) * 2048].rearrange("p (k c j) -> p k j c", k=KT, j=2)
                    for f in range(2):
                        for k in range(KT):
                            last = nc.tensor.matmul(gu[:, (2 * g + f) * CAP:(2 * g + f + 1) * CAP], wv[:, k, f, :],
                                                    xt[:, k, :], start=k == 0, stop=k == KT - 1)
                incs("gu", last)
                waits("hid")
                wv = w[:, 4096:6144].rearrange("p (j c) -> p j c", j=2)
                for c in range(2):
                    for f in range(2):
                        last = nc.tensor.matmul(y[0:CAP, 512 * c:512 * (c + 1)], hid[:, f, :],
                                                wv[:, f, 512 * c:512 * (c + 1)], start=f == 0, stop=f == 1)
                incs("y", last)

            pe.wait_ge(slots_ready, 1)
            with pe.Fori(0, NE // 4) as i:
                for s in range(4):
                    q = s % 2

                    def waits(what):
                        if what == "x":
                            pe.wait_ge(gath[q], (i * 2 + s // 2 + 1) * 16)
                            nc.tensor.sem_inc(pe_turns, 1)
                        elif what == "xt":
                            pe.wait_ge(xgT_ready, i * 4 + s + 1)
                            pe.wait_ge(mw_in[s], i * 48 + 48)
                        else:
                            pe.wait_ge(hid_ready, i * 4 + s + 1)
                            pe.wait_ge(y_copied_act[q], i * 2 + s // 2)
                            pe.wait_ge(y_copied_dve[q], i * 2 + s // 2)

                    def incs(what, ins):
                        if what == "xp":
                            ins.then_inc(xgp_ready[q], 1)
                        elif what == "gu":
                            ins.then_inc(gu_ready, 1)
                        else:
                            ins.then_inc(y_done[s], 1)

                    expert(Xg[:, q, :], bank[4 * q], xgT[:, q], bank[4 * q + 1], hidT[:, q, 0], pairs[2 * q + 1],
                           moe_w[s], waits, incs)
            over = pe.value_load(over_i[0:1, MAX_OVER:MAX_OVER + 1], min_val=0, max_val=MAX_OVER)
            with pe.If(over > 0):
                with pe.Fori(0, MAX_OVER) as b:
                    def waits(what):
                        if what == "x":
                            pe.wait_ge(o_g, b * 16 + 16)
                            pe.wait_ge(o_w, b * 48 + 48)
                            nc.tensor.sem_inc(pe_turns, 1)
                        else:
                            pe.wait_ge(o_step, b * 8 + {"xt": 2, "hid": 5}[what])

                    def incs(what, ins):
                        ins.then_inc(o_step, 1)

                    expert(Xg[:, 0, :], bank[0], xgT[:, 0], bank[1], hidT[:, 0, 0], pairs[1], moe_w[0], waits, incs)

        @block.scalar
        def _(act):
            tr = [0]
            chain = [0]

            def link(ins):
                chain[0] += 1
                ins.then_inc(act_chain, 1)
                act.wait_ge(act_chain, chain[0])

            for t in range(NT):
                r = ROWS[t]
                act.wait_ge(x_in[t], 16 * len(row_pieces(t)))
                link(nc.scalar.activation(arena[0:r, 0:D], X[0:r, t, :], ACT.Square, scale=1.0 / 32.0,
                                          accum_out=ss[0:r, t:t + 1]))
                nc.scalar.sem_inc(ss_ready, 1)
            tr[0] = 10

            def tr_copy(dst, n, cols, rows=P):
                act.wait_ge(tr_ready, tr[0] + 1)
                b = bank[4 + tr[0] % 2]
                nc.scalar.activation(dst, b[0:rows, 0:n * cols].rearrange("p (i c) -> p i c", i=n), ACT.Copy)\
                    .then_inc(tr_free_act, 1)
                tr[0] += 1

            for c in range(NCB):
                tr_copy(ksT[:, :, P * c:P * (c + 1)], 4, P)
                tr_copy(dkiC[:, :, P * c:P * (c + 1)], 3, P)
            act.wait_ge(xs_ready, NT)
            act.wait_ge(tr_ready, 10)
            for t in range(NT):
                tr_copy(iqT[:, :, OFF[t]:OFF[t] + ROWS[t]], 4, ROWS[t])

            def pj_copy(n, dst, src, func=ACT.Copy, scale=1.0, also=None):
                act.wait_ge(pj_ready, n + 1)
                ins = nc.scalar.activation(dst, src(bank[n % 4]), func, scale=scale)
                ins.then_inc(pj_free_act, 1)

            def squares_of(n, t, i, c0, cols):
                act.wait_ge(pj_ready, n + t + 1)
                if i >= 2:
                    act.wait_ge(rope_parts, i - 1 + NT)
                r = ROWS[t]
                nc.scalar.activation(ropeQ[0:r, i % 2, 0:cols], bank[(n + t) % 4][0:r, c0:c0 + cols],
                                     ACT.Square, scale=1.0 / 8.0).then_inc(squares, 1)

            for t in range(NT + 1):
                if t < NT:
                    squares_of(J_SM, t, t, N_SMALL1, 128)
                if t:
                    tr_copy(dkiT[:, :, OFF[t - 1]:OFF[t - 1] + ROWS[t - 1]], 3, ROWS[t - 1])
            for i, (t, h, k0, k1) in enumerate(IX):
                r = ROWS[t]
                act.wait_ge(ix_ready, i + 1)
                if i >= 2:
                    act.wait_ge(relu_used, i - 1)
                nc.scalar.activation(rb[0:r, i % 2, 0:k1 - k0], bank[6 + i % 2][0:r, 0:k1 - k0], ACT.Relu)\
                    .then_inc(relu_ready, 1)
            for t in range(NT + 1):
                if t < NT:
                    squares_of(J_DQ, t, NT + t, 0, 512)
                if t:
                    tr_copy(dqT[:, :, OFF[t - 1]:OFF[t - 1] + ROWS[t - 1]], 4, ROWS[t - 1])
            for t in range(NT):
                r = ROWS[t]
                act.wait_ge(pj_ready, J_SV + t + 1)
                link(nc.scalar.activation(svP[0:r, t, :], bank[(J_SV + t) % 4][0:r, :], ACT.Copy))
                nc.scalar.sem_inc(pj_free_act, 1)
                nc.scalar.sem_inc(sv_rows, 1)
            for n0, dst, scale in ((J_SK, skT, 1.0), (J_SQ, sqT, HD ** -0.5)):
                for cb in range(4):
                    for g in range(2):
                        lo, hi = FG[g]
                        pj_copy(n0 + 2 * cb + g, dst[:, cb, lo:hi], lambda b: b[:, 0:hi - lo], scale=scale)
            for t in range(NT):
                r = ROWS[t]
                act.wait_ge(tr_ready, tr[0] + 1)
                dst = skR4 if t == NT - 1 else skR[:, t, :]
                link(nc.scalar.activation(dst[0:r, :], bank[4 + tr[0] % 2][0:r, :], ACT.Copy))
                nc.scalar.sem_inc(tr_free_act, 1)
                nc.scalar.sem_inc(sk_rows, 1)
                tr[0] += 1

            for i in range(NSTEP + TRI_LAG):
                if i < NSTEP:
                    s = STEPS[i]
                    act.wait_ge(cap_ready, i + 1)
                    v = spb[0:s["nk"], i % SPR, 0:s["n"]]
                    link(nc.scalar.activation(v, v, ACT.Exp))
                    nc.scalar.activation(v, v, ACT.Ln, bias=1.0).then_inc(ln_ready, 1)
                m = i - TRI_LAG
                if 0 <= m < NSTEP:
                    s = STEPS[m]
                    act.wait_ge(logw_ready, m + 1)
                    if m >= WR:
                        act.wait_ge(pv_done, m - WR + 1)
                    nc.scalar.activation(wtb[0:s["nk"], m % WR, 0:s["n"]], bank[2 + m % ZR][0:s["nk"], 0:s["n"]],
                                         ACT.Exp).then_inc(w_ready, 1)
                e = i - TRI_LAG - 2
                if 0 <= e < NSTEP and e + 1 < NSTEP and STEPS[e]["acc"] != STEPS[e + 1]["acc"]:
                    s = STEPS[e]
                    act.wait_ge(pv_done, e + 1)
                    nc.scalar.activation(osbT[:, s["pair"], s["lo"]:s["hi"]], bank[s["acc"] % 2][:, 0:s["hi"] - s["lo"]],
                                         ACT.Copy).then_inc(acc_free, 1)
            act.wait_ge(pv_done, NSTEP)
            nc.scalar.activation(osbT[:, :, N_PROMPT:N_ROWS],
                                 bank[0][:, 0:NPAIR * DEC].rearrange("p (b q) -> p b q", b=NPAIR),
                                 ACT.Copy).then_inc(acc_free, 1)

            jobs = [(t, h) for t in range(NT) for h in range(NH)]
            for i in range(len(jobs) + 2):
                if i < len(jobs):
                    t, h = jobs[i]
                    r, w = ROWS[t], KEYS[t]
                    act.wait_ge(lb_ready, i + 1)
                    if i >= 2:
                        act.wait_ge(pT_ready, i - 1)
                    if h == 0 and t >= 2:
                        act.wait_ge(on_ready, t - 1)
                    nc.scalar.activation(pb[0:r, i % 2, 0:w], Lb[0:r, i % 2, 0:w], ACT.Exp, scale=HD ** -0.5,
                                         bias=nbias[0:r, i % 2:i % 2 + 1],
                                         accum_out=rsum[0:r, t % 2, h:h + 1]).then_inc(p_ready, 1)
                m = i - 1
                if 0 <= m < len(jobs):
                    t, h = jobs[m]
                    act.wait_ge(pT_ready, m + 1)
                    if m >= 2:
                        act.wait_ge(pvd_done, m - 1)
                    n = (t + 1) * ROWS[t]
                    nc.scalar.activation(pTb[:, m % 2, 0:n], bank[4 + m % 2][:, 0:n], ACT.Copy).then_inc(pT_copied, 1)
                if i % NH == 2 and i > NH and i < len(jobs):
                    t = i // NH - 1
                    act.wait_ge(oT_ready, t + 1)
                    nc.scalar.activation(odsaT[:, :, OFF[t]:OFF[t] + ROWS[t]],
                                         bank[4][:, 0:4 * ROWS[t]].rearrange("p (i c) -> p i c", i=4), ACT.Copy)\
                        .then_inc(oT_copied, 1)
            act.wait_ge(oT_ready, NT)
            nc.scalar.activation(odsaT[:, :, OFF[4]:OFF[4] + ROWS[4]],
                                 bank[4][:, 0:4 * ROWS[4]].rearrange("p (i c) -> p i c", i=4), ACT.Copy)\
                .then_inc(oT_copied, 1)

            for cb in range(8):
                for g in range(2):
                    lo, hi = FG[g]
                    n = J_GSB + 2 * cb + g
                    act.wait_ge(pj_ready, n + 1)
                    link(nc.scalar.activation(merged[:, cb, lo:hi], bank[n % 4][:, 0:hi - lo], ACT.Sigmoid))
                    nc.scalar.sem_inc(pj_free_act, 1)
                    nc.scalar.sem_inc(gate_ready, 1)
            for j in range(16):
                cb, g = j // 2, j % 2
                lo, hi = FG[g]
                n = J_GB + 2 * j
                act.wait_ge(pj_ready, n + 1)
                if j >= 2:
                    act.wait_ge(half_merged, j - 1)
                link(nc.scalar.activation(tabs[:, (j % 2) * 280:(j % 2) * 280 + hi - lo], bank[n % 4][:, 0:hi - lo],
                                          ACT.Sigmoid))
                nc.scalar.sem_inc(pj_free_act, 1)
                nc.scalar.sem_inc(gate_ready, 1)
            for t in range(NT):
                r = ROWS[t]
                act.wait_ge(h_ready, t + 1)
                if t == 0:
                    act.wait_ge(pj_ready, used_at[13])
                link(nc.scalar.activation(arena[0:r, 4 * SLOT + 3 * D:4 * SLOT + 4 * D], X[0:r, t, :], ACT.Square,
                                          scale=1.0 / 32.0, accum_out=ss[0:r, t:t + 1]))
                nc.scalar.sem_inc(ss2_ready, 1)
            for t in range(NT):
                for q in range(2):
                    tr_copy(xT[:, 4 * q:4 * q + 4, OFF[t]:OFF[t] + ROWS[t]], 4, ROWS[t])
            for t in range(NT):
                n = J_RT + t
                r = ROWS[t]
                act.wait_ge(pj_ready, n + 1)
                link(nc.scalar.activation(rl[0:r, t, :], bank[n % 4][0:r, 0:36], ACT.Copy))
                nc.scalar.sem_inc(pj_free_act, 1)
                nc.scalar.sem_inc(logits_ready, 1)
            act.wait_ge(rvals_ready, 1)
            link(nc.scalar.activation(gx[:, 0:4 * NT], gx[:, 0:4 * NT], ACT.Exp))
            nc.scalar.sem_inc(rexp_ready, 1)
            act.wait_ge(rvals_ready, 2)
            link(nc.scalar.activation(gx[:, 40:40 + NT], gx[:, 40:40 + NT], ACT.Exp))
            nc.scalar.sem_inc(rexp_ready, 1)

            with act.Fori(0, NE // 4) as i:
                for s in range(4):
                    q = s % 2
                    act.wait_ge(xgp_ready[q], i * 2 + s // 2 + 1)
                    nc.scalar.activation(xgT[:, q], bank[4 * q].rearrange("p (k s) -> p k s", k=KT), ACT.Copy)\
                        .then_inc(xgT_ready, 1)
                    act.wait_ge(gu_ready, i * 4 + s + 1)
                    nc.scalar.activation(hidT[:, q, 1], bank[4 * q + 1][:, 0:2 * CAP].rearrange("p (f s) -> p f s", f=2),
                                         ACT.Silu).then_inc(silu_ready, 1)
                    act.wait_ge(y_done[s], i + 1)
                    act.wait_ge(y_out[q], (i * 2 + s // 2) * 16)
                    nc.scalar.activation(Yb[:, q, 0:512], pairs[2 * q + 1][0:CAP, 0:512], ACT.Copy)\
                        .then_inc(y_copied_act[q], 1)
                    act.wait_ge(y_copied_act[q], i * 2 + s // 2 + 1)
                    act.wait_ge(y_copied_dve[q], i * 2 + s // 2 + 1)
                    act.dma_start(y_d[bass.ds((i * 4 + s) * CAP, CAP), :], Yb[:, q, :]).then_inc(y_out[q], 16)
            act.wait_ge(y_out[0], NE // 2 * 16)
            act.wait_ge(y_out[1], NE // 2 * 16)
            over = act.value_load(over_i[0:1, MAX_OVER:MAX_OVER + 1], min_val=0, max_val=MAX_OVER)
            with act.If(over > 0):
                with act.Fori(0, MAX_OVER) as b:
                    act.wait_ge(o_step, b * 8 + 1)
                    nc.scalar.activation(xgT[:, 0], bank[0].rearrange("p (k s) -> p k s", k=KT), ACT.Copy)\
                        .then_inc(o_step, 1)
                    act.wait_ge(o_step, b * 8 + 3)
                    nc.scalar.activation(hidT[:, 0, 1], bank[1][:, 0:2 * CAP].rearrange("p (f s) -> p f s", f=2),
                                         ACT.Silu).then_inc(o_step, 1)
                    act.wait_ge(o_step, b * 8 + 6)
                    nc.scalar.activation(Yb[:, 0, :], pairs[1][0:CAP, :], ACT.Copy).then_inc(o_step, 1)
                    act.wait_ge(o_step, b * 8 + 7)
                    act.dma_start(y_d[bass.ds((b + NE) * CAP, CAP), :], Yb[:, 0, :]).then_inc(y_out[0], 16)
                    act.wait_ge(y_out[0], (b + NE // 2 + 1) * 16)
                    nc.scalar.sem_inc(o_step, 1)
            nc.scalar.sem_inc(comb_used, 1)

        @block.gpsimd
        def _(pool):
            chain = [0]

            def link(ins):
                chain[0] += 1
                ins.then_inc(pool_chain, 1)
                pool.wait_ge(pool_chain, chain[0])

            def inverse_roots(ready, done):
                for t in range(NT):
                    r = ROWS[t]
                    pool.wait_ge(ready, t + 1)
                    link(nc.gpsimd.tensor_scalar(rstd[0:r, t:t + 1], ss[0:r, t:t + 1], EPS, None, ALU.add))
                    nc.gpsimd.tensor_tensor(rstd[0:r, t:t + 1], rstd[0:r, t:t + 1], mhalf[0:r, 0:1], ALU.pow)\
                        .then_inc(done, 1)


            link(nc.gpsimd.memset(mhalf, -0.5))
            inverse_roots(ss_ready, rstd_ready)
            pool.wait_ge(const_in, 16)
            pool.wait_ge(gains_in, 16 * 7)
            for w in range(2):
                for v, base in ((0, cos), (1, sin)):
                    g = gqk[:, (2 * w + v) * HD:(2 * w + v + 1) * HD].rearrange("p (o c) -> p o c", o=1)
                    link(nc.gpsimd.tensor_tensor(tab[:, 2 * w + v], base, g.broadcast_to([P, NT, HD]), ALU.mult))
            link(nc.gpsimd.tensor_copy(rid_i[:, :], rid))
            link(nc.gpsimd.memset(zero_i[:, :], 0))
            nc.gpsimd.sem_inc(tables_ready, 1)
            pool.dma_start(slot_row_d.rearrange("(b s) o -> b (s o)", s=CAP), zero_i[:, :]).then_inc(table_zero, 16)
            pool.wait_ge(zero_ready, 1)
            pool.dma_start(y_d[NE * CAP:, :].rearrange("(p a) (b c) -> p a b c", p=64, b=2)
                           .rearrange("p a b c -> p (a b) c"),
                           zeros[0:64, :].rearrange("p (o c) -> p o c", o=1).broadcast_to([64, 2 * MAX_OVER, 512]))\
                .then_inc(y_zeroed, 16)
            for n in range(3 * NT):
                t, kind = n % NT, n // NT
                r = ROWS[t]
                pool.wait_ge(rope_parts, n + 1)
                if kind:
                    hs = 2 if kind == 1 else NH
                    f = rq[0:r, n % 2, 0:hs]
                    link(nc.gpsimd.tensor_scalar(f, ssq[0:r, n % 2, 0:hs], EPS, None, ALU.add))
                    link(nc.gpsimd.tensor_tensor(f, f, mhalf[0:r, 0:hs], ALU.pow))
                if kind == 1:
                    d = kd[0:r, t, :, 0, :]
                    link(nc.gpsimd.tensor_tensor(d, d, ropeB[0:r, n % 2, 0:192].rearrange("p (b c) -> p b c", b=3),
                                                 ALU.add))
                    link(nc.gpsimd.tensor_tensor(d[:, 0:2], d[:, 0:2],
                                                 rq[0:r, n % 2, 0:2].rearrange("p (h o) -> p h o", o=1)
                                                 .broadcast_to([r, 2, HD]), ALU.mult))
                    link(nc.gpsimd.tensor_copy(kd[0:r, t, :, 1, :], d))
                    nc.gpsimd.sem_inc(small_rows, 1)
                else:
                    A = ropeA[0:r, t % 2, :]
                    link(nc.gpsimd.tensor_tensor(A, A, ropeB[0:r, n % 2, :], ALU.add))
                    if kind == 2:
                        A3 = A.rearrange("p (h c) -> p h c", h=NH)
                        link(nc.gpsimd.tensor_tensor(A3, A3, rq[0:r, n % 2, :].rearrange("p (h o) -> p h o", o=1)
                                                     .broadcast_to([r, NH, HD]), ALU.mult))
                nc.gpsimd.sem_inc(rows_ready, 1)

            pool.wait_ge(keys_out, 16 * 6 * (NT + 1))
            for i in range(NSTEP + PV_LAG):
                m = i - 1
                if 0 <= m < NSTEP:
                    s = STEPS[m]
                    if s["first"]:
                        prev = [k for k in range(m) if STEPS[k]["stream"] == s["stream"]]
                        if prev:
                            pool.wait_ge(logw_ready, prev[-1] + 1)
                        link(nc.gpsimd.memset(sufb[:, s["stream"], :], 0.0))
                    pool.wait_ge(sp_ready, m + 1)
                    v = spb[0:s["nk"], m % SPR, 0:s["n"]]
                    if s["diag"]:
                        if s["kind"] == "prompt":
                            w = min(s["nk"], s["n"])
                            v = v[:, 0:w]
                            link(nc.gpsimd.affine_select(out=v, in_=v, compare_op=ALU.is_gt, fill=0.0, base=0,
                                                         pattern=[[1, w]], channel_multiplier=-1))
                        else:
                            v3 = v.rearrange("p (b q) -> p b q", b=NPAIR)
                            link(nc.gpsimd.affine_select(out=v3, in_=v3, compare_op=ALU.is_gt, fill=0.0, base=0,
                                                         pattern=[[0, NPAIR], [1, DEC]], channel_multiplier=-1))
                    nc.gpsimd.sem_inc(sp_masked, 1)
                m = i - TRI_LAG
                if 0 <= m < NSTEP:
                    s = STEPS[m]
                    if not s["last"]:
                        pool.wait_ge(logw_ready, m + 1)
                        o0 = s["q0"] - s["lo"] if s["kind"] == "prompt" else 0
                        v = sufb[0:s["nk"], s["stream"], o0:o0 + s["n"]]
                        link(nc.gpsimd.tensor_tensor(v, v, spb[0:s["nk"], m % SPR, 0:s["n"]], ALU.add))
                    nc.gpsimd.sem_inc(suf_ready, 1)
                m = i - TRI_LAG - 1
                if 0 <= m < NSTEP:
                    s = STEPS[m]
                    pool.wait_ge(w_ready, m + 1)
                    if s["diag"]:
                        if s["kind"] == "prompt":
                            w = min(s["nk"], s["n"])
                            v = wtb[0:s["nk"], m % WR, 0:w]
                            link(nc.gpsimd.affine_select(out=v, in_=v, compare_op=ALU.is_gt, fill=0.0, base=0,
                                                         pattern=[[1, w]], channel_multiplier=-1))
                        else:
                            v3 = wtb[0:s["nk"], m % WR, 0:s["n"]].rearrange("p (b q) -> p b q", b=NPAIR)
                            link(nc.gpsimd.affine_select(out=v3, in_=v3, compare_op=ALU.is_gt, fill=0.0, base=0,
                                                         pattern=[[0, NPAIR], [1, DEC]], channel_multiplier=-1))
                    nc.gpsimd.sem_inc(w_masked, 1)

            pool.wait_ge(oT_copied, NT)
            load_chunk(pool, 8)
            load_chunk(pool, 9)
            load_chunk(pool, 10)
            load_chunk(pool, 11)
            pool.dma_start(wr[:, :, 0:4], a["w_group"].rearrange("(p k) c -> p k c", k=KT)).then_inc(wr_in, 16)
            pool.dma_start(wr[:, :, 4:36], a["w_router"].rearrange("(p k) c -> p k c", k=KT)).then_inc(wr_in, 16)
            load_chunk(pool, 12)
            load_chunk(pool, 13)
            pool.wait_ge(y_zeroed, 16)
            pool.wait_ge(pj_ready, used_at[11])
            for t in range(NT):
                for p0, p1, which, r0 in row_pieces(t):
                    src = a["meta_tokens"] if which == "meta" else a["x_" + which]
                    pool.dma_start(X[p0:p1, t, :], src[r0:r0 + p1 - p0, :]).then_inc(xres_in, 16)
            pool.wait_ge(pj_ready, used_at[13])
            pool.dma_start(g2b, a["norm2_g"].rearrange("(o c) -> o c", o=1).broadcast_to([P, D])).then_inc(g2_in, 16)
            inverse_roots(ss2_ready, rstd2_ready)
            for t in range(NT):
                pool.wait_ge(x2_ready, t + 1)
                pool.dma_start(xn2_d[OFF[t]:OFF[t] + ROWS[t], :], x2row[0:ROWS[t], t % 2, :]).then_inc(x2_stored[t], 16)
            pool.wait_ge(table_zero, 16)
            pool.wait_ge(slots_ready, 1)
            for c in range(2):
                for t in range(NT):
                    pool.indirect_dma_start(slot_row_d, bass.IndirectOffsetOnAxis(ap=slot_i[c][0:ROWS[t], t:t + 1], axis=0),
                                            rid_i[0:ROWS[t], t:t + 1], None).then_inc(table_done, 16)
            pool.wait_ge(table_done, 16 * 2 * NT)
            pool.dma_start(idxs[:, :], slot_row_d.rearrange("(b s) o -> s (b o)", s=CAP),
                           allow_slow_non_contiguous=True).then_inc(idx_in, 16)
            pool.wait_ge(idx_in, 16)
            for t in range(NT):
                pool.wait_ge(x2_stored[t], 16)
            with pool.Fori(0, NE // 4) as i:
                for s in range(4):
                    q = s % 2
                    pool.wait_ge(xgp_ready[q], i * 2 + s // 2)
                    pool.wait_ge(gath[q], (i * 2 + s // 2) * 16)
                    nc.gpsimd.tensor_copy(idx_now[:, q:q + 1], idxs[:, bass.ds(i * 4 + s, 1)]).then_inc(idx_now_ready, 1)
                    pool.wait_ge(idx_now_ready, i * 4 + s + 1)
                    nc.gpsimd.sem_inc(pool_turns, 1)
                    pool.indirect_dma_start(Xg[:, q, :], None, xn2_d,
                                            bass.IndirectOffsetOnAxis(ap=idx_now[:, q:q + 1], axis=0)).then_inc(gath[q], 16)
            over = pool.value_load(over_i[0:1, MAX_OVER:MAX_OVER + 1], min_val=0, max_val=MAX_OVER)
            with pool.If(over > 0):
                pool.wait_ge(xgp_ready[0], NE // 2)
                with pool.Fori(0, MAX_OVER) as b:
                    pool.wait_ge(o_step, b * 8)
                    nc.gpsimd.tensor_copy(idx_now[:, 0:1], idxs[:, bass.ds(b + NE, 1)]).then_inc(o_idx, 1)
                    pool.wait_ge(o_idx, b + 1)
                    nc.gpsimd.sem_inc(pool_turns, 1)
                    pool.indirect_dma_start(Xg[:, 0, :], None, xn2_d,
                                            bass.IndirectOffsetOnAxis(ap=idx_now[:, 0:1], axis=0)).then_inc(o_g, 16)
            pool.wait_ge(comb_used, 1)
            for t in range(NT):
                for c in range(2):
                    n = 2 * t + c
                    if n >= 4:
                        pool.wait_ge(comb_used, n - 2)
                    pool.indirect_dma_start(moe_w[n % 4][0:ROWS[t], 0:D], None, y_d,
                                            bass.IndirectOffsetOnAxis(ap=slot_i[c][0:ROWS[t], t:t + 1], axis=0))\
                        .then_inc(comb_in[n % 4], 16)

        @block.vector
        def _(dve):
            chain = [0]

            def link(ins):
                chain[0] += 1
                ins.then_inc(dve_chain, 1)
                dve.wait_ge(dve_chain, chain[0])
                return ins

            for p in pairs:
                link(nc.vector.memset(p[:, :], 0.0))
            link(nc.vector.memset(rl, 0.0))

            def norm_rows(t, ready, out_ap):
                r = ROWS[t]
                dve.wait_ge(ready, t + 1)
                link(nc.vector.tensor_scalar(out_ap, X[0:r, t, :], rstd[0:r, t:t + 1], None, ALU.mult))

            for t in range(NT):
                norm_rows(t, rstd_ready, X[0:ROWS[t], t, :])
                nc.vector.sem_inc(xs_ready, 1)
            dve.wait_ge(gains_in, 16 * 7)
            for n in range(2 * NT):
                t, q = n // 2, n % 2
                r = ROWS[t]
                dve.wait_ge(tr_ready, n + 1)
                nc.vector.tensor_tensor(xT[:, 4 * q:4 * q + 4, OFF[t]:OFF[t] + r],
                                        bank[4 + n % 2][:, 0:4 * r].rearrange("p (i c) -> p i c", i=4),
                                        g1[:, 4 * q:4 * q + 4].rearrange("p (k o) -> p k o", o=1)
                                        .broadcast_to([P, 4, r]), ALU.mult).then_inc(tr_free_dve, 1)

            def rope(src, A, B, ct, st, r, heads):
                def bc(v, w):
                    return v.rearrange("p (o c) -> p o c", o=1).broadcast_to([r, heads, w])
                nc.vector.tensor_tensor(A, src, bc(ct, HD), ALU.mult)
                nc.vector.tensor_tensor(B[:, :, 0:HALF], src[:, :, HALF:HD], bc(st[:, 0:HALF], HALF), ALU.mult)
                return nc.vector.tensor_tensor(B[:, :, HALF:HD], src[:, :, 0:HALF], bc(st[:, HALF:HD], HALF), ALU.mult)

            def wait_rope_buffers(n):
                if n >= 2:
                    dve.wait_ge(rows_ready, n - 1)

            nc.vector.memset(zeros, 0.0).then_inc(zero_ready, 1)
            dve.wait_ge(tables_ready, 1)
            for t in range(NT):
                r = ROWS[t]
                n = J_IQ + t
                dve.wait_ge(pj_ready, n + 1)
                wait_rope_buffers(t)
                if t >= 2:
                    dve.wait_ge(tr_ready, T_IQ + t - 1)
                src = bank[n % 4][0:r, :].rearrange("p (h c) -> p h c", h=NH)
                link(rope(src, ropeA[0:r, t % 2, :].rearrange("p (h c) -> p h c", h=NH),
                          ropeB[0:r, t % 2, :].rearrange("p (h c) -> p h c", h=NH), cos[0:r, t], sin[0:r, t], r, NH))
                nc.vector.sem_inc(pj_free_dve, 1)
                nc.vector.sem_inc(rope_parts, 1)
            for t in range(NT):
                r = ROWS[t]
                n = J_SM + t
                m = NT + t
                b = bank[n % 4][0:r, :]
                dve.wait_ge(squares, t + 1)
                wait_rope_buffers(m)
                nc.vector.tensor_scalar(iws[0:r, t, :], b[:, HD:HD + NH], HD ** -0.5 * NH ** -0.5, None, ALU.mult)
                nc.vector.tensor_copy(dvP[0:r, t, :], b[:, N_SMALL1 + 128:328])
                B = ropeB[0:r, m % 2, 0:192].rearrange("p (b c) -> p b c", b=3)
                rope(b[:, 0:HD].rearrange("p (h c) -> p h c", h=1), kd[0:r, t, 2:3, 0, :], B[:, 2:3], cos[0:r, t],
                     sin[0:r, t], r, 1)
                rope(b[:, N_SMALL1:N_SMALL1 + 128].rearrange("p (h c) -> p h c", h=2), kd[0:r, t, 0:2, 0, :],
                     B[:, 0:2], tab[0:r, 2, t], tab[0:r, 3, t], r, 2)
                link(nc.vector.tensor_reduce(ssq[0:r, m % 2, 0:2],
                                             ropeQ[0:r, t % 2, 0:128].rearrange("p (h c) -> p h c", h=2), AX.X, ALU.add))
                nc.vector.sem_inc(pj_free_dve, 1)
                nc.vector.sem_inc(rope_parts, 1)
            for i, (t, h, k0, k1) in enumerate(IX):
                r = ROWS[t]
                dve.wait_ge(relu_ready, i + 1)
                s = SC[t][0:r, k0:k1]
                if h == 0:
                    link(nc.vector.tensor_scalar(s, rb[0:r, i % 2, 0:k1 - k0], iws[0:r, t, 0:1], None, ALU.mult))
                else:
                    link(nc.vector.scalar_tensor_tensor(s, rb[0:r, i % 2, 0:k1 - k0], iws[0:r, t, h:h + 1], s,
                                                        ALU.mult, ALU.add))
                nc.vector.sem_inc(relu_used, 1)
            for t in range(NT):
                r = ROWS[t]
                n = J_DQ + t
                m = 2 * NT + t
                dve.wait_ge(squares, NT + t + 1)
                wait_rope_buffers(m)
                if t >= 2:
                    dve.wait_ge(tr_ready, T_DQ + t - 1)
                src = bank[n % 4][0:r, :].rearrange("p (h c) -> p h c", h=NH)
                rope(src, ropeA[0:r, t % 2, :].rearrange("p (h c) -> p h c", h=NH),
                     ropeB[0:r, m % 2, :].rearrange("p (h c) -> p h c", h=NH), tab[0:r, 0, t], tab[0:r, 1, t], r, NH)
                link(nc.vector.tensor_reduce(ssq[0:r, m % 2, :],
                                             ropeQ[0:r, (NT + t) % 2, :].rearrange("p (h c) -> p h c", h=NH),
                                             AX.X, ALU.add))
                nc.vector.sem_inc(pj_free_dve, 1)
                nc.vector.sem_inc(rope_parts, 1)
            link(nc.vector.memset(SC[0][0:ROWS[0], :], 0.0))
            link(nc.vector.memset(SC[0][0:N_META, N_META:KEYS[0]], -BIG))
            for t in range(1, NT):
                r = ROWS[t]
                w = KEYS[t]
                hide = w - CHUNK if t < NT - 1 else N_PROMPT
                link(nc.vector.memset(SC[t][0:64, hide:w], HIDDEN))
                for n in range(SEL_PROMPT // 8):
                    link(nc.vector.max(top8[0:r, :], SC[t][0:r, :]))
                    link(nc.vector.match_replace(SC[t][0:r, :], top8[0:r, :], SC[t][0:r, :], TAKEN))
                if t == NT - 1:
                    for n in range((SEL_SAMPLE - SEL_PROMPT) // 8):
                        link(nc.vector.max(top8[64:96, :], SC[t][64:96, :]))
                        link(nc.vector.match_replace(SC[t][64:96, :], top8[64:96, :], SC[t][64:96, :], TAKEN))
                link(nc.vector.tensor_scalar(SC[t][0:r, :], SC[t][0:r, :], TAKEN, -BIG, ALU.not_equal, ALU.mult))

            dve.wait_ge(keys_out, 16 * 6 * (NT + 1))
            for i in range(NSTEP + 1):
                if i < NSTEP:
                    s = STEPS[i]
                    dve.wait_ge(z_ready, i + 1)
                    if i >= SPR:
                        dve.wait_ge(logw_ready, i - SPR + 1)
                        dve.wait_ge(suf_ready, i - SPR + 1)
                    nc.vector.tensor_scalar(spb[0:s["nk"], i % SPR, 0:s["n"]], bank[2 + i % ZR][0:s["nk"], 0:s["n"]],
                                            Z_CAP, None, ALU.min).then_inc(cap_ready, 1)
                m = i - 1
                if m >= 0:
                    s = STEPS[m]
                    dve.wait_ge(ln_ready, m + 1)
                    v = spb[0:s["nk"], m % SPR, 0:s["n"]]
                    nc.vector.tensor_tensor(v, bank[2 + m % ZR][0:s["nk"], 0:s["n"]], v, ALU.max)\
                        .then_inc(sp_ready, 1)

            jobs = [(t, h) for t in range(NT) for h in range(NH)]

            def norm_out(t):
                r = ROWS[t]
                dve.wait_ge(pvd_done, NH * (t + 1))
                link(nc.vector.reciprocal(rinv[0:r, :], rsum[0:r, t % 2, :]))
                if t >= 1:
                    dve.wait_ge(oT_ready, t)
                link(nc.vector.tensor_tensor(oN[0:r, :].rearrange("p (h c) -> p h c", h=NH),
                                             bank[6 + t % 2][0:r, :].rearrange("p (h c) -> p h c", h=NH),
                                             rinv[0:r, :].rearrange("p (h o) -> p h o", o=1)
                                             .broadcast_to([r, NH, HD]), ALU.mult))
                nc.vector.sem_inc(on_ready, 1)

            for i, (t, h) in enumerate(jobs):
                r, w = ROWS[t], KEYS[t]
                dve.wait_ge(lg_ready, i + 1)
                if i >= 2:
                    dve.wait_ge(p_ready, i - 1)
                pr = pairs[i % 2]
                if t < NT - 1:
                    src, bias, dst = pr[0:r, 0:w], SC[t][0:r, :], Lb[0:r, i % 2, 0:w]
                else:
                    src = pr[0:r, :].rearrange("p (b c) -> p b c", b=2)[:, :, 0:272]
                    bias = SC[t][0:r, :].rearrange("p (b c) -> p b c", b=2)
                    dst = Lb[0:r, i % 2, 0:w].rearrange("p (b c) -> p b c", b=2)
                link(nc.vector.tensor_tensor_reduce(out=dst, in0=src, in1=bias, scale=1.0, scalar=HIDDEN,
                                                    op0=ALU.add, op1=ALU.max, accum_out=mx[0:r, i % 2:i % 2 + 1]))
                link(nc.vector.tensor_scalar(nbias[0:r, i % 2:i % 2 + 1], mx[0:r, i % 2:i % 2 + 1], -HD ** -0.5, None,
                                             ALU.mult))
                nc.vector.sem_inc(lb_ready, 1)
                if h == 2 and t:
                    norm_out(t - 1)
            norm_out(NT - 1)

            for j in range(16):
                cb, g = j // 2, j % 2
                lo, hi = FG[g]
                n = J_A + j
                dve.wait_ge(pj_ready, n + 1)
                dve.wait_ge(gate_ready, j + 1)
                link(nc.vector.tensor_tensor(merged[:, cb, lo:hi], bank[n % 4][:, 0:hi - lo], merged[:, cb, lo:hi],
                                             ALU.mult))
                nc.vector.sem_inc(pj_free_dve, 1)
            for j in range(16):
                cb, g = j // 2, j % 2
                lo, hi = FG[g]
                n = J_GB + 2 * j + 1
                dve.wait_ge(pj_ready, n + 1)
                dve.wait_ge(gate_ready, 17 + j)
                gt = tabs[:, (j % 2) * 280:(j % 2) * 280 + hi - lo]
                link(nc.vector.tensor_tensor(gt, bank[n % 4][:, 0:hi - lo], gt, ALU.mult))
                nc.vector.sem_inc(pj_free_dve, 1)
                link(nc.vector.tensor_tensor(merged[:, cb, lo:hi], merged[:, cb, lo:hi], gt, ALU.add))
                nc.vector.sem_inc(half_merged, 1)
                nc.vector.sem_inc(merged_ready, 1)
            dve.wait_ge(xres_in, 16 * (NT + 2))
            for t in range(NT):
                r = ROWS[t]
                for c in range(2):
                    n = J_WO + 2 * t + c
                    dve.wait_ge(pj_ready, n + 1)
                    v = X[0:r, t, 512 * c:512 * (c + 1)]
                    link(nc.vector.tensor_tensor(v, bank[n % 4][0:r, :], v, ALU.add))
                    nc.vector.sem_inc(pj_free_dve, 1)
                nc.vector.sem_inc(h_ready, 1)
            dve.wait_ge(g2_in, 16)
            for t in range(NT):
                r = ROWS[t]
                if t >= 2:
                    dve.wait_ge(x2_stored[t - 2], 16)
                    dve.wait_ge(tr_ready, T_X2 + 2 * (t - 2) + 2)
                norm_rows(t, rstd2_ready, x2row[0:r, t % 2, :])
                link(nc.vector.tensor_tensor(x2row[0:r, t % 2, :], x2row[0:r, t % 2, :], g2b[0:r, :], ALU.mult))
                nc.vector.sem_inc(x2_ready, 1)

            dve.wait_ge(logits_ready, NT)
            def per_row(v, n):
                return v.rearrange("p (t o) -> p t o", o=1).broadcast_to([P, NT, n])

            def tt(o, x, y, op):
                link(nc.vector.tensor_tensor(o, x, y, op))

            def ts(o, x, c1, c2, op0, op1=None):
                if op1 is None:
                    link(nc.vector.tensor_scalar(o, x, c1, None, op0))
                else:
                    link(nc.vector.tensor_scalar(o, x, c1, c2, op0, op1))

            def red(o, x, op):
                link(nc.vector.tensor_reduce(o, x, AX.X, op))

            g = rl[:, :, 0:NG]
            d = gx[:, 0:NG * NT].rearrange("p (t g) -> p t g", t=NT)
            red(v_max, g, ALU.max)
            tt(d, g, per_row(v_max, NG), ALU.subtract)
            nc.vector.sem_inc(rvals_ready, 1)
            tt(g_eq, g, per_row(v_max, NG), ALU.is_equal)
            ts(v_rest, v_max, 0.0, 1.0, ALU.mult, ALU.add)
            for k in range(NG):
                if k:
                    tt(v_rest, v_rest, g_eq[:, :, k - 1], ALU.subtract)
                tt(g_eq[:, :, k], g_eq[:, :, k], v_rest, ALU.mult)
            for k in range(NG):
                el = rl[:, :, NG + EPG * k:NG + EPG * (k + 1)]
                tt(elm if k else elg, el, g_eq[:, :, k:k + 1].broadcast_to([P, NT, EPG]), ALU.mult)
                if k:
                    tt(elg, elg, elm, ALU.add)
            ts(v_base, g_eq[:, :, 1], float(EPG), None, ALU.mult)
            for k in range(2, NG):
                link(nc.vector.scalar_tensor_tensor(v_base, g_eq[:, :, k], float(EPG * k), v_base, ALU.mult, ALU.add))
            dve.wait_ge(rexp_ready, 1)
            red(v_gp, d, ALU.add)
            link(nc.vector.reciprocal(v_gp, v_gp))
            iota8 = iota[:, 0:EPG].rearrange("p (o e) -> p o e", o=1).broadcast_to([P, NT, EPG])
            for c in range(2):
                red(v_top[c], elg, ALU.max)
                tt(elm, elg, per_row(v_top[c], EPG), ALU.is_equal)
                ts(elx, iota8, -100.0, None, ALU.add)
                tt(elx, elx, elm, ALU.mult)
                red(v_e[c], elx, ALU.min)
                ts(v_e[c], v_e[c], 100.0, None, ALU.add)
                if c == 0:
                    tt(elm, iota8, per_row(v_e[c], EPG), ALU.is_equal)
                    link(nc.vector.scalar_tensor_tensor(elg, elm, -BIG, elg, ALU.mult, ALU.add))
                tt(v_e[c], v_e[c], v_base, ALU.add)
            ex = gx[:, 40:40 + NT]
            tt(ex, v_top[1], v_top[0], ALU.subtract)
            nc.vector.sem_inc(rvals_ready, 1)
            iota32 = iota.rearrange("p (o e) -> p o e", o=1).broadcast_to([P, NT, NE])
            for c in range(2):
                tt(oh[c], iota32, per_row(v_e[c], NE), ALU.is_equal)
                tt(oh[c], oh[c], per_row(valid, NE), ALU.mult)
            W = NT * NE
            M = rt[:, 0:W].rearrange("p (t e) -> p t e", t=NT)
            tt(M, oh[0], oh[1], ALU.add)
            ts(rt[:, W:2 * W], rt[:, 0:W], -1.0, None, ALU.mult)
            nc.vector.sem_inc(onehot_ready, 1)
            dve.wait_ge(rexp_ready, 2)
            ts(ew[0], ex, 1.0, None, ALU.add)
            link(nc.vector.reciprocal(ew[0], ew[0]))
            tt(ew[0], ew[0], v_gp, ALU.mult)
            tt(ew[1], ew[0], ex, ALU.mult)
            pos = rt[:, 2 * W:3 * W].rearrange("p (t e) -> p t e", t=NT)
            cnt = rt[:, 3 * W:3 * W + NE]
            blocks = rt[:, 3 * W + NE:3 * W + 2 * NE]
            upto = rt[:, 3 * W + 2 * NE:3 * W + 3 * NE]
            before = rt[:, 3 * W + 3 * NE:3 * W + 4 * NE]
            ones = rt[:, 3 * W + 4 * NE:3 * W + 5 * NE]
            cmp = tabs[:, 0:8 * NE].rearrange("p (e k) -> p e k", k=8)
            dve.wait_ge(pos_ready, 1)
            link(nc.vector.tensor_copy(rt[:, 2 * W:3 * W + NE], bank[0][:, 0:W + NE]))
            tt(cmp, cnt.rearrange("p (e o) -> p e o", o=1).broadcast_to([P, NE, 8]),
               thr.rearrange("p (o k) -> p o k", o=1).broadcast_to([P, NE, 8]), ALU.is_gt)
            red(blocks, cmp, ALU.add)
            link(nc.vector.memset(ones, 1.0))
            link(nc.vector.tensor_tensor_scan(upto, ones, blocks, 0.0, ALU.mult, ALU.add))
            tt(before, upto, blocks, ALU.subtract)
            for c in range(2):
                tmp = tabs[:, 0:W].rearrange("p (t e) -> p t e", t=NT)
                tt(tmp, oh[c], pos, ALU.mult)
                red(v_p, tmp, ALU.add)
                tt(tmp, oh[c], before.rearrange("p (o e) -> p o e", o=1).broadcast_to([P, NT, NE]), ALU.mult)
                red(v_o, tmp, ALU.add)
                tt(v_o, v_o, v_e[c], ALU.subtract)
                ts(v_o, v_o, float(CAP), float(NE * CAP - CAP), ALU.mult, ALU.add)
                ts(v_rest, v_p, float(CAP), None, ALU.is_ge)
                tt(v_o, v_o, v_rest, ALU.mult)
                tt(v_o, v_o, v_p, ALU.add)
                link(nc.vector.scalar_tensor_tensor(v_o, v_e[c], float(CAP), v_o, ALU.mult, ALU.add))
                link(nc.vector.tensor_copy(slot_i[c][:, :], v_o))
            m17 = tabs[0:1, 0:MAX_OVER * NE].rearrange("p (b e) -> p b e", b=MAX_OVER)
            tt(m17, upto[0:1].rearrange("p (o e) -> p o e", o=1).broadcast_to([1, MAX_OVER, NE]),
               iota[0:1, 0:MAX_OVER].rearrange("p (b o) -> p b o", o=1).broadcast_to([1, MAX_OVER, NE]), ALU.is_le)
            o17 = tabs[0:1, 600:600 + MAX_OVER]
            red(o17, m17, ALU.add)
            ts(o17, o17, float(NE - 1), None, ALU.min)
            link(nc.vector.tensor_copy(over_i[0:1, 0:MAX_OVER], o17))
            link(nc.vector.tensor_copy(over_i[0:1, MAX_OVER:MAX_OVER + 1], upto[0:1, NE - 1:NE]))
            nc.vector.sem_inc(slots_ready, 1)

            with dve.Fori(0, NE // 4) as i:
                for s in range(4):
                    q = s % 2
                    dve.wait_ge(silu_ready, i * 4 + s + 1)
                    nc.vector.tensor_tensor(hidT[:, q, 0], hidT[:, q, 1],
                                            bank[4 * q + 1][:, 2 * CAP:4 * CAP].rearrange("p (f s) -> p f s", f=2),
                                            ALU.mult).then_inc(hid_ready, 1)
                    dve.wait_ge(y_done[s], i + 1)
                    dve.wait_ge(y_out[q], (i * 2 + s // 2) * 16)
                    nc.vector.tensor_copy(Yb[:, q, 512:1024], pairs[2 * q + 1][0:CAP, 512:1024])\
                        .then_inc(y_copied_dve[q], 1)
            over = dve.value_load(over_i[0:1, MAX_OVER:MAX_OVER + 1], min_val=0, max_val=MAX_OVER)
            with dve.If(over > 0):
                with dve.Fori(0, MAX_OVER) as b:
                    dve.wait_ge(o_step, b * 8 + 4)
                    nc.vector.tensor_tensor(hidT[:, 0, 0], hidT[:, 0, 1],
                                            bank[1][:, 2 * CAP:4 * CAP].rearrange("p (f s) -> p f s", f=2),
                                            ALU.mult).then_inc(o_step, 1)
            for t in range(NT):
                r = ROWS[t]
                for c in range(2):
                    n = 2 * t + c
                    dve.wait_ge(comb_in[n % 4], 16 * (n // 4 + 1))
                    link(nc.vector.scalar_tensor_tensor(X[0:r, t, :], moe_w[n % 4][0:r, 0:D], ew[c][0:r, t:t + 1],
                                                        X[0:r, t, :], ALU.mult, ALU.add))
                    nc.vector.sem_inc(comb_used, 1)
                nc.vector.sem_inc(final_ready, 1)


_SHAPES = {
    "y_prompt": [SEQ, D], "y_sample": [DEC, D],
    "sk_p": [N_PROMPT, 512], "sv_p": [N_PROMPT, 512], "dk_p": [N_PROMPT, 2, HD], "dv_p": [N_PROMPT, 128],
    "ik_p": [N_PROMPT, HD],
    "sk_s": [DEC, 512], "sv_s": [DEC, 512], "dk_s": [DEC, 2, HD], "dv_s": [DEC, 128], "ik_s": [DEC, HD],
}
_RETURNED = [
    (1, SEQ, D), (1, DEC, D),
    (1, 1, N_PROMPT, NH, HD), (1, 1, N_PROMPT, NH, HD), (1, 1, N_PROMPT, 2, HD), (1, 1, N_PROMPT, 2, HD),
    (1, 1, N_PROMPT, HD),
    (1, 1, DEC, NH, HD), (1, 1, DEC, NH, HD), (1, 1, DEC, 2, HD), (1, 1, DEC, 2, HD), (1, 1, DEC, HD),
]


def kernel(**inputs):
    import numpy as _np
    import concourse.bacc as _bacc
    from concourse import mybir as _mybir
    from concourse.bass_utils import run_bass_kernel_spmd as _run

    shapes = {
        "x_prompt": (SEQ, D), "x_sample": (DEC, D), "cache_sb_k": (PAST, 512), "cache_sb_v": (PAST, 512),
        "cache_dsa_k": (PAST, 2, HD), "cache_dsa_v": (PAST, 128), "cache_idx_k": (PAST, HD),
        "meta_tokens": (N_META, D), "norm1_g": (D,), "w_in": (D, 4936), "dsa_q_norm_g": (HD,),
        "dsa_k_norm_g": (HD,), "w_sb_branch": (512, D), "w_dsa_branch": (512, D), "w_out": (D, D),
        "norm2_g": (D,), "w_group": (D, NG), "w_router": (D, NE), "w_gate": (NE, D, FE), "w_up": (NE, D, FE),
        "w_down": (NE, FE, D),
    }
    nc = _bacc.Bacc("TRN2", target_bir_lowering=False, num_devices=1)
    arrays = {n: _np.ascontiguousarray(inputs[n]).reshape(s) for n, s in shapes.items()}
    arrays["consts"] = constants()
    arrays = {f"in_{n}": v for n, v in arrays.items()}
    args = {n[3:]: nc.dram_tensor(n, v.shape, _mybir.dt.from_np(v.dtype), kind="ExternalInput").ap()
            for n, v in arrays.items()}
    outs = {n: nc.dram_tensor(f"out_{n}", s, _mybir.dt.float32, kind="ExternalOutput").ap()
            for n, s in _SHAPES.items()}
    build(nc, args, outs)
    r = _run(nc, [arrays], core_ids=[0])
    return tuple(r.results[0][f"out_{n}"].reshape(s) for n, s in zip(_SHAPES, _RETURNED))
```

```python
from contextlib import ExitStack

import numpy as np

import concourse.bass as bass
from concourse import mybir

F32 = mybir.dt.float32
I32 = mybir.dt.int32
ACT = mybir.ActivationFunctionType
ALU = mybir.AluOpType
AX = mybir.AxisListType

P = 128
D = 1024
KT = D // P
HD = 64
HALF = HD // 2
NH = 8
NPAIR = NH // 2
N_META, SEQ, DEC, PAST, CHUNK = 16, 512, 32, 512, 64
N_PROMPT = N_META + SEQ
N_ROWS = N_PROMPT + DEC
OFF = [0, 80, 208, 336, 464]
ROWS = [80, 128, 128, 128, 96]
NT = len(OFF)
KEYS = [80, 208, 336, 464, PAST + DEC]
KEY_ROWS = [80, 128, 128, 128, 64]
NCB = PAST // P
SEL_PROMPT = min(256, SEQ // 4)
SEL_SAMPLE = min(256, (PAST + DEC) // 4)
EPS = 1e-6
NG, EPG, NE, FE = 4, 8, 32, 256
CAP = 64
MAX_OVER = (2 * N_ROWS) // CAP
NBLK = NE + MAX_OVER
N_SLOTS = NBLK * CAP
BIG = 1.0e30
HIDDEN = float(np.float32(-3.0e38))
Z_CAP = 30.0
TAKEN = float(np.float32(-3.2e38))

C_SQ, C_SK, C_SV, C_DQ, C_DK, C_IQ, C_IK, C_GSB, C_GDSA = 0, 512, 1024, 1536, 2048, 2304, 2816, 2888, 3912
N_SMALL1, N_SMALL2 = 72, 256

K_ID, K_NTRI, K_NONE, K_STRI, K_COS, K_SIN, K_IOTA, K_THR, K_VALID, K_RID = (
    0, 128, 256, 384, 512, 832, 1152, 1216, 1224, 1229)
K_COLS = 1234


def constants():
    c = np.zeros((P, K_COLS), np.float32)
    i = np.arange(P)
    c[:, K_ID:K_ID + P] = np.eye(P)
    c[:, K_NTRI:K_NTRI + P] = -(i[:, None] >= i[None, :]).astype(np.float32)
    c[:, K_NONE:K_NONE + P] = -1.0
    c[:, K_STRI:K_STRI + P] = (i[:, None] < i[None, :])
    freqs = (10000.0 ** (-np.arange(HALF) / HALF)).astype(np.float32)
    for t in range(NT):
        pos = OFF[t] + i
        if t == NT - 1:
            pos = np.where(i < 64, pos, PAST + i - 64)
        ang = (pos.astype(np.float32)[:, None] * freqs[None, :].astype(np.float32)).astype(np.float64)
        c[:, K_COS + t * HD:K_COS + (t + 1) * HD] = np.concatenate([np.cos(ang), np.cos(ang)], 1)
        c[:, K_SIN + t * HD:K_SIN + (t + 1) * HD] = np.concatenate([-np.sin(ang), np.sin(ang)], 1)
        c[:ROWS[t], K_VALID + t] = 1.0
        c[:ROWS[t], K_RID + t] = OFF[t] + i[:ROWS[t]]
    c[:, K_IOTA:K_IOTA + CAP] = np.arange(CAP)
    c[:, K_THR:K_THR + 8] = CAP * (1 + np.arange(8))
    return c


def row_pieces(t):
    if t == 0:
        return [(0, N_META, "meta", 0), (N_META, ROWS[0], "prompt", 0)]
    if t == NT - 1:
        return [(0, 64, "prompt", OFF[t] - N_META), (64, 96, "sample", 0)]
    return [(0, P, "prompt", OFF[t] - N_META)]


GROUPS = [(208, N_PROMPT, [4, 3, 2, 1, 0]), (0, 208, [1, 0])]


def sb_steps():
    steps = []
    for pair in range(NPAIR):
        for g, (lo, hi, blocks) in enumerate(GROUPS):
            for n, j in enumerate(blocks):
                for half in range(2):
                    q0 = max(OFF[j], lo)
                    steps.append(dict(kind="prompt", pair=pair, g=g, half=half, j=j, lo=lo, hi=hi, q0=q0,
                                      n=hi - q0, nk=KEY_ROWS[j], diag=OFF[j] >= lo, first=n == 0,
                                      last=n == len(blocks) - 1, stream=2 * (g % 2) + half,
                                      cover0=max(OFF[blocks[n - 1]], lo) if n else hi,
                                      acc=2 * pair + g))
    for n, j in enumerate([NCB] + list(range(NCB - 1, -1, -1))):
        for half in range(2):
            steps.append(dict(kind="sample", half=half, j=j, n=NPAIR * DEC, nk=DEC if j == NCB else P,
                              diag=j == NCB, first=n == 0, last=j == 0, stream=half, acc=2 * NPAIR))
    return steps


STEPS = sb_steps()
NSTEP = len(STEPS)
ZR, SPR, WR = 6, 6, 3
TRI_LAG, PV_LAG = 3, 5


def build(nc, a, out):
    ctx = ExitStack()
    with ctx:
        def sem(name):
            return ctx.enter_context(nc.semaphore(name))

        def sems(name, n):
            return [sem(f"{name}{i}") for i in range(n)]

        def sb(name, cols, dt=F32, rows=P):
            return ctx.enter_context(nc.sbuf_tensor(name, [rows, cols], dt))

        SLOT = 3 * 2048
        arena = sb("arena", 4 * SLOT + KT * N_ROWS)
        xnT = sb("xnT", KT * N_ROWS)
        ring_w = sb("ring_w", 2 * 4096)
        hreg = sb("hreg", NT * D)
        cst = sb("cst", K_COLS)
        g1 = sb("g1", KT)
        gqk = sb("gqk", 4 * HD)
        tabs = sb("tabs", 4 * NT * HD)
        small = sb("small", 1400)

        at = [0]

        def carve(cols):
            s = arena[:, at[0]:at[0] + cols]
            at[0] += cols
            assert at[0] <= 4 * SLOT + KT * N_ROWS, at[0]
            return s

        sqT = carve(NPAIR * N_ROWS).rearrange("p (b r) -> p b r", b=NPAIR)
        skT = carve(NPAIR * N_ROWS).rearrange("p (b r) -> p b r", b=NPAIR)
        ksT = carve(NPAIR * PAST).rearrange("p (b r) -> p b r", b=NPAIR)
        svP = carve(NT * 512).rearrange("p (t c) -> p t c", t=NT)
        svC = carve(NCB * 512).rearrange("p (t c) -> p t c", t=NCB)
        svN = carve(512)
        dqT = carve(NPAIR * N_ROWS).rearrange("p (b r) -> p b r", b=NPAIR)
        dkiT = carve(3 * N_ROWS).rearrange("p (b r) -> p b r", b=3)
        dkiC = carve(3 * PAST).rearrange("p (b r) -> p b r", b=3)
        dvP = carve(NT * 128).rearrange("p (t c) -> p t c", t=NT)
        dvC = carve(NCB * 128).rearrange("p (t c) -> p t c", t=NCB)
        dvN = carve(128)
        sc0 = at[0]
        SC = [carve(k) for k in KEYS]
        natD = arena[:, sc0:sc0 + NCB * 384].rearrange("p (t b u c) -> p t b u c", t=NCB, b=3, u=2)
        rb = carve(2 * 512).rearrange("p (i c) -> p i c", i=2)
        mark = at[0]
        ropeA = carve(2 * 512).rearrange("p (i c) -> p i c", i=2)
        ropeB = carve(2 * 512).rearrange("p (i c) -> p i c", i=2)
        ropeQ = carve(2 * 512).rearrange("p (i c) -> p i c", i=2)
        kd = carve(NT * 384).rearrange("p (t b u c) -> p t b u c", t=NT, b=3, u=2)
        natS = carve(NCB * 512).rearrange("p (t c) -> p t c", t=NCB)
        skR = natS
        skR4 = carve(512)
        at[0] = mark
        spb = carve(SPR * 320).rearrange("p (i c) -> p i c", i=SPR)
        wtb = carve(WR * 320).rearrange("p (i c) -> p i c", i=WR)
        sufb = carve(4 * 320).rearrange("p (i c) -> p i c", i=4)
        at[0] = mark
        Lb = carve(2 * 544).rearrange("p (i c) -> p i c", i=2)
        pb = carve(3 * 544).rearrange("p (i c) -> p i c", i=3)
        pTb = carve(8 * 512).rearrange("p (i c) -> p i c", i=8)
        merged = arena[:, 4 * SLOT:].rearrange("p (k r) -> p k r", k=KT)
        xT = xnT[:, :].rearrange("p (k r) -> p k r", k=KT)
        X = hreg[:, :].rearrange("p (t d) -> p t d", t=NT)
        osbT = hreg[:, 0:NPAIR * N_ROWS].rearrange("p (b r) -> p b r", b=NPAIR)
        odsaT = hreg[:, NPAIR * N_ROWS:2 * NPAIR * N_ROWS].rearrange("p (b r) -> p b r", b=NPAIR)
        zeros = hreg[:, 2 * NPAIR * N_ROWS:2 * NPAIR * N_ROWS + 512]
        iqT = odsaT
        wslot = [ring_w[:, s * 4096:(s + 1) * 4096] for s in range(2)]
        moe_w = [arena[:, s * SLOT:(s + 1) * SLOT] for s in range(4)]
        Xg = ring_w[0:CAP, 0:2 * D].rearrange("p (i d) -> p i d", i=2)
        Yb = ring_w[:, 2 * D:3 * D].rearrange("p (i d) -> p i d", i=2)
        xgT = ring_w[:, 3 * D:4 * D].rearrange("p (i k s) -> p i k s", i=2, k=KT)
        hid = ring_w[:, 4 * D:4 * D + 256].rearrange("p (i c) -> p i c", i=2)
        sil = ring_w[:, 4 * D + 256:4 * D + 512].rearrange("p (i c) -> p i c", i=2)
        hidT = ring_w[:, 4 * D + 512:4 * D + 768].rearrange("p (i c) -> p i c", i=2)
        lgT = tabs[:, 640:1200]
        x2row = ring_w[:, 4 * D:6 * D].rearrange("p (i d) -> p i d", i=2)
        g2b = ring_w[:, 6 * D:7 * D]
        scrap = ring_w[:, 7 * D:8 * D]

        so = [0]

        def sm(cols):
            s = small[:, so[0]:so[0] + cols]
            so[0] += cols
            assert so[0] <= 1400
            return s

        ss = sm(NT)
        rstd = sm(NT)
        ssq = sm(2 * NH).rearrange("p (i h) -> p i h", i=2)
        rq = sm(2 * NH).rearrange("p (i h) -> p i h", i=2)
        iws = sm(NT * NH).rearrange("p (t h) -> p t h", t=NT)
        top8 = sm(8)
        mhalf = sm(NH)
        mx = sm(2)
        nbias = sm(2)
        rsum = sm(3)
        wr = sm(KT * 36).rearrange("p (k c) -> p k c", k=KT)
        rl = sm(NT * 36).rearrange("p (t c) -> p t c", t=NT)
        oh = [sm(NT * NE).rearrange("p (t e) -> p t e", t=NT) for _ in range(2)]
        gx = sm(64)
        ew = [sm(NT) for _ in range(2)]
        elg = sm(NT * 8).rearrange("p (t e) -> p t e", t=NT)
        v_max, v_rest, v_base, v_gp, v_p, v_o = (sm(NT) for _ in range(6))
        v_top = [sm(NT) for _ in range(2)]
        v_e = [sm(NT) for _ in range(2)]
        g_eq = sm(NT * NG).rearrange("p (t g) -> p t g", t=NT)
        elm = sm(NT * EPG).rearrange("p (t e) -> p t e", t=NT)
        elx = sm(NT * EPG).rearrange("p (t e) -> p t e", t=NT)
        at_slot = [ring_w[:, c * 640:c * 640 + NT * CAP].rearrange("p (t s) -> p t s", t=NT) for c in range(2)]
        at_block = [ring_w[:, 1280 + c * 640:1280 + c * 640 + NT * NBLK].rearrange("p (t b) -> p t b", t=NT)
                    for c in range(2)]
        rt = sb("rt", NT * NE * 3 + 5 * NE + (NT + 1) * NE)
        earlier = rt[:, NT * NE * 3 + 5 * NE:]
        slot_part = [sb(f"slot_part{c}", NT, I32) for c in range(2)]
        slot_i = [sb(f"slot_i{c}", NT, I32) for c in range(2)]
        idxs = sb("idxs", NBLK, I32, CAP)
        idx_now = sb("idx_now", 2, I32, CAP)
        over_i = sb("over_i", MAX_OVER + 1, I32, 1)

        ident = cst[:, K_ID:K_ID + P]
        ntri = cst[:, K_NTRI:K_NTRI + P]
        nones = cst[:, K_NONE:K_NONE + P]
        stri = cst[:, K_STRI:K_STRI + P]
        cos = cst[:, K_COS:K_COS + NT * HD].rearrange("p (t c) -> p t c", t=NT)
        sin = cst[:, K_SIN:K_SIN + NT * HD].rearrange("p (t c) -> p t c", t=NT)
        iota = cst[:, K_IOTA:K_IOTA + CAP]
        thr = cst[:, K_THR:K_THR + 8]
        valid = cst[:, K_VALID:K_VALID + NT]
        rid = cst[:, K_RID:K_RID + NT]
        tab = tabs[:, :].rearrange("p (w t c) -> p w t c", w=4, t=NT)

        pair01 = ctx.enter_context(nc.psum_tensor("pair01", [P, 1024], F32))
        pair23 = ctx.enter_context(nc.psum_tensor("pair23", [P, 1024], F32))
        pair45 = ctx.enter_context(nc.psum_tensor("pair45", [P, 1024], F32))
        pair67 = ctx.enter_context(nc.psum_tensor("pair67", [P, 1024], F32))
        pairs = [pair01, pair23, pair45, pair67]
        bank = [p[:, s * 512:(s + 1) * 512] for p in pairs for s in range(2)]

        xn2_d = nc.dram_tensor("xn2_d", [N_ROWS, D], F32).ap()
        y_d = nc.dram_tensor("y_d", [N_SLOTS, D], F32).ap()

        const_in = sem("const_in")
        gains_in = sem("gains_in")
        x_in = sems("x_in", NT)
        cache_k_in = sem("cache_k_in")
        cache_v_in = sem("cache_v_in")
        chunk_in = sems("chunk_in", 14)
        ss_ready = sem("ss_ready")
        rstd_ready = sem("rstd_ready")
        rstd2_ready = sem("rstd2_ready")
        xs_ready = sem("xs_ready")
        tr_ready = sem("tr_ready")
        tr_free_act = sem("tr_free_act")
        tr_free_dve = sem("tr_free_dve")
        pj_ready = sem("pj_ready")
        pj_free_act = sem("pj_free_act")
        pj_free_dve = sem("pj_free_dve")
        tables_ready = sem("tables_ready")
        rope_parts = sem("rope_parts")
        squares = sem("squares")
        rows_ready = sem("rows_ready")
        ix_ready = sem("ix_ready")
        relu_ready = sem("relu_ready")
        relu_used = sem("relu_used")
        topk_done = sem("topk_done")
        vnew_in = sem("vnew_in")
        keys_out = sem("keys_out")
        sk_rows = sem("sk_rows")
        sv_rows = sem("sv_rows")
        small_rows = sem("small_rows")
        z_ready = sem("z_ready")
        cap_ready = sem("cap_ready")
        ln_ready = sem("ln_ready")
        sp_ready = sem("sp_ready")
        sp_masked = sem("sp_masked")
        suf_ready = sem("suf_ready")
        logw_ready = sem("logw_ready")
        w_ready = sem("w_ready")
        w_masked = sem("w_masked")
        pv_done = sem("pv_done")
        acc_ready = sem("acc_ready")
        acc_free = sem("acc_free")
        lg_ready = sem("lg_ready")
        lb_ready = sem("lb_ready")
        p_ready = sem("p_ready")
        pT_ready = sem("pT_ready")
        pT_copied = sem("pT_copied")
        pn_ready = sem("pn_ready")
        oT_copied = sem("oT_copied")
        pvd_done = sem("pvd_done")
        gate_ready = sem("gate_ready")
        half_merged = sem("half_merged")
        merged_ready = sem("merged_ready")
        xres_in = sem("xres_in")
        wr_in = sem("wr_in")
        g2_in = sem("g2_in")
        h_ready = sem("h_ready")
        ss2_ready = sem("ss2_ready")
        x2_ready = sem("x2_ready")
        x2_stored = sems("x2_stored", NT)
        logits_ready = sem("logits_ready")
        rexp_ready = sem("rexp_ready")
        rvals_ready = sem("rvals_ready")
        gvals_ready = sem("gvals_ready")
        onehot_ready = sem("onehot_ready")
        pos_ready = sem("pos_ready")
        slots_ready = sem("slots_ready")
        idx_ready = sem("idx_ready")
        idx_in = sem("idx_in")
        mw_in = sems("mw_in", 4)
        idx_now_ready = sem("idx_now_ready")
        gath = sems("gath", 2)
        xgp_ready = sems("xgp_ready", 2)
        xgT_ready = sems("xgT_ready", 2)
        gu_ready = sem("gu_ready")
        silu_ready = sem("silu_ready")
        hid_ready = sem("hid_ready")
        hT_ready = sem("hT_ready")
        hidT_ready = sem("hidT_ready")
        y_done = sems("y_done", 4)
        y_copied = sems("y_copied", 2)
        y_out = sems("y_out", 2)
        o_w = sem("o_w")
        o_idx = sem("o_idx")
        o_g = sem("o_g")
        o_step = sem("o_step")
        comb_in = sems("comb_in", 2 * NT)
        results_out = sem("results_out")
        final_ready = sem("final_ready")
        y_final_out = sem("y_final_out")
        pe_turns = sem("pe_turns")
        pool_turns = sem("pool_turns")
        zero_ready = sem("zero_ready")
        y_zeroed = sem("y_zeroed")
        act_chain = sem("act_chain")
        dve_chain = sem("dve_chain")
        pool_chain = sem("pool_chain")

        slots = [0, 1, 0, 1, 0, 1, 0, 1, 0, 2, 1, 0, 3, 4]
        chunk_at = [moe_w[5 - s][:, 0:4096] if s >= 2 else wslot[s] for s in slots]

        used_at = [5, 10, 15, 20, 28, 36, 44, 52, 68, 100, 84, 100, 110, 110]

        def free_before(n):
            return max([used_at[m] for m in range(n) if slots[m] == slots[n]], default=0)

        win = a["w_in"].rearrange("(p k) c -> p k c", k=KT)

        def load_chunk(eng, n):
            if free_before(n):
                eng.wait_ge(pj_ready, free_before(n))
            v = chunk_at[n]
            if n == 1:
                v = v[:, 0:KT * 328].rearrange("p (k c) -> p k c", k=KT)
                eng.dma_start(v[:, :, 0:N_SMALL1], win[:, :, C_IK:C_IK + N_SMALL1]).then_inc(chunk_in[n], 16)
                eng.dma_start(v[:, :, N_SMALL1:328], win[:, :, C_DK:C_DK + N_SMALL2]).then_inc(chunk_in[n], 16)
                return
            v8 = v.rearrange("p (k c) -> p k c", k=KT)
            col = {0: C_IQ, 2: C_DQ, 3: C_SV, 4: C_SK, 5: C_SQ, 6: C_GSB, 7: C_GSB + 512,
                   10: C_GDSA, 11: C_GDSA + 512}
            if n in col:
                src, v = win[:, :, col[n]:col[n] + 512], v8
            elif n == 8:
                src = a["w_sb_branch"].rearrange("(k p) c -> p k c", p=P)
                v = v.rearrange("p (k c) -> p k c", k=4)
            elif n == 9:
                v = v.rearrange("p (k c) -> p k c", k=4)
                for kv in range(2):
                    src = a["w_dsa_branch"][256 * kv:256 * (kv + 1), :].rearrange("(k p) c -> p k c", p=64)
                    eng.dma_start(v[64 * kv:64 * (kv + 1)], src).then_inc(chunk_in[n], 16)
                return
            else:
                src = a["w_out"].rearrange("(k p) c -> p k c", p=P)[:, :, (n - 12) * 512:(n - 11) * 512]
                v = v8
            eng.dma_start(v, src).then_inc(chunk_in[n], 16)

        def chunk_arrived(eng, n):
            eng.wait_ge(chunk_in[n], 32 if n in (1, 9) else 16)

        PJ = (["dve"] * 15 + ["act"] * (NT + 16) + ["act"] * 16 + ["dve"] * 16 + ["act", "dve"] * 16
              + ["dve"] * 10 + ["act"] * 2)
        J_IQ, J_SM, J_DQ, J_SV, J_SK, J_SQ = 0, 5, 10, 15, 20, 28
        J_GSB, J_A, J_GB, J_WO, J_RT = 36, 52, 68, 100, 110
        TR = ["dve"] * 10 + ["act"] * 8 + ["act"] * 20 + ["act"] * 11
        T_X, T_C, T_IQ, T_SM, T_DQ, T_SK, T_X2 = 0, 10, 18, 23, 28, 33, 38

        def emptied(order, who, n):
            return sum(w == who for w in order[:n + 1])

        def pj_wait_free(eng, n):
            if n >= 4:
                who = PJ[n - 4]
                eng.wait_ge(pj_free_act if who == "act" else pj_free_dve, emptied(PJ, who, n - 4))

        def tr_wait_free(eng, n):
            if n >= 2:
                who = TR[n - 2]
                eng.wait_ge(tr_free_act if who == "act" else tr_free_dve, emptied(TR, who, n - 2))

        FG = [(0, 280), (280, 560)]
        IX = []
        for t in range(1, NT):
            for h in range(NH):
                IX += [(t, h, 0, 272), (t, h, 272, 544)] if t == NT - 1 else [(t, h, 0, KEYS[t])]

        block = ctx.enter_context(nc.Block())

        @block.sync
        def _(sp):
            sp.dma_start(X[0:N_META, 0, :], a["meta_tokens"]).then_inc(x_in[0], 16)
            sp.dma_start(X[N_META:ROWS[0], 0, :], a["x_prompt"][0:ROWS[0] - N_META, :]).then_inc(x_in[0], 16)
            sp.dma_start(cst[:, :], a["consts"]).then_inc(const_in, 16)
            sp.dma_start(g1[:, :], a["norm1_g"].rearrange("(p k) -> p k", k=KT)).then_inc(gains_in, 16)
            for t in range(1, NT):
                for p0, p1, which, r0 in row_pieces(t):
                    sp.dma_start(X[p0:p1, t, :], a["x_" + which][r0:r0 + p1 - p0, :]).then_inc(x_in[t], 16)
            load_chunk(sp, 0)
            for w, name in enumerate(("dsa_q_norm_g", "dsa_k_norm_g")):
                g = a[name].rearrange("(o c) -> o c", o=1)
                q = gqk[:, 2 * w * HD:2 * (w + 1) * HD]
                sp.dma_start(q[:, 0:HD], g.broadcast_to([P, HD])).then_inc(gains_in, 16)
                sp.dma_start(q[:, HD:HD + HALF], g[:, HALF:HD].broadcast_to([P, HALF])).then_inc(gains_in, 16)
                sp.dma_start(q[:, HD + HALF:2 * HD], g[:, 0:HALF].broadcast_to([P, HALF])).then_inc(gains_in, 16)
            sp.dma_start(natS, a["cache_sb_k"].rearrange("(t p) c -> p t c", p=P)).then_inc(cache_k_in, 16)
            for u in range(2):
                for b in range(2):
                    sp.dma_start(natD[:, :, b, u, :],
                                 a["cache_dsa_k"][:, b, :].rearrange("(t p) c -> p t c", p=P)).then_inc(cache_k_in, 16)
                sp.dma_start(natD[:, :, 2, u, :],
                             a["cache_idx_k"].rearrange("(t p) c -> p t c", p=P)).then_inc(cache_k_in, 16)
            load_chunk(sp, 1)
            sp.dma_start(svC, a["cache_sb_v"].rearrange("(t p) c -> p t c", p=P)).then_inc(cache_v_in, 16)
            sp.dma_start(dvC, a["cache_dsa_v"].rearrange("(t p) c -> p t c", p=P)).then_inc(cache_v_in, 16)
            load_chunk(sp, 2)

            def store_rows(src, dst_prompt, dst_sample, t):
                n = KEY_ROWS[t]
                sp.dma_start(dst_prompt[OFF[t]:OFF[t] + n, :], src[0:n]).then_inc(keys_out, 16)
                if t == NT - 1:
                    sp.dma_start(dst_sample[:, :], src[64:96]).then_inc(keys_out, 16)

            load_chunk(sp, 3)
            for t in range(NT):
                sp.wait_ge(small_rows, t + 1)
                for b in range(2):
                    store_rows(kd[:, t, b, 0, :], out["dk_p"][:, b, :], out["dk_s"][:, b, :], t)
                store_rows(kd[:, t, 2, 0, :], out["ik_p"], out["ik_s"], t)
                store_rows(dvP[:, t, :], out["dv_p"], out["dv_s"], t)
            sp.dma_start(dvN[0:DEC, :], dvP[64:96, NT - 1, :]).then_inc(vnew_in, 16)
            load_chunk(sp, 4)
            load_chunk(sp, 5)
            for t in range(NT):
                sp.wait_ge(sv_rows, t + 1)
                store_rows(svP[:, t, :], out["sv_p"], out["sv_s"], t)
            sp.dma_start(svN[0:DEC, :], svP[64:96, NT - 1, :]).then_inc(vnew_in, 16)
            load_chunk(sp, 6)
            load_chunk(sp, 7)
            for t in range(NT):
                sp.wait_ge(sk_rows, t + 1)
                store_rows(skR4 if t == NT - 1 else skR[:, t, :], out["sk_p"], out["sk_s"], t)
            wg = a["w_gate"].rearrange("e (p k) f -> (e p) (k f)", k=KT)
            wu = a["w_up"].rearrange("e (p k) f -> (e p) (k f)", k=KT)
            wd = a["w_down"].rearrange("e (j p) c -> p (e j) c", j=2)

            def load_expert(slot, e, arrived):
                for n, w in enumerate((wg, wu)):
                    sp.dma_start(moe_w[slot][:, n * 2048:(n + 1) * 2048], w[bass.ds(e * P, P), :])\
                        .then_inc(arrived, 16)
                sp.dma_start(moe_w[slot][:, 4096:6144].rearrange("p (j c) -> p j c", j=2),
                             wd[:, bass.ds(e * 2, 2), :]).then_inc(arrived, 16)

            sp.wait_ge(oT_copied, NT)
            sp.wait_ge(acc_free, 2 * NPAIR + 1)
            sp.wait_ge(vnew_in, 32)
            with sp.Fori(0, NE // 4) as i:
                for s in range(4):
                    if s:
                        sp.wait_ge(pj_ready, used_at[{3: 9, 2: 12, 1: 13}[s]])
                    sp.wait_ge(y_done[s], i)
                    load_expert(s, i * 4 + s, mw_in[s])
            over = sp.value_load(over_i[0:1, MAX_OVER:MAX_OVER + 1], min_val=0, max_val=MAX_OVER)
            with sp.If(over > 0):
                sp.wait_ge(y_done[0], NE // 4)
                with sp.Fori(0, MAX_OVER) as b:
                    sp.wait_ge(o_step, b * 10)
                    e = sp.value_load(over_i[0:1, bass.ds(b, 1)], min_val=0, max_val=NE - 1)
                    load_expert(0, e, o_w)
            for t in range(NT):
                sp.wait_ge(final_ready, t + 1)
                for p0, p1, which, r0 in row_pieces(t):
                    if which != "meta":
                        sp.dma_start(out["y_" + which][r0:r0 + p1 - p0, :], X[p0:p1, t, :]).then_inc(y_final_out, 16)
            sp.wait_ge(y_final_out, 16 * (NT + 1))
            sp.wait_ge(keys_out, 16 * 6 * (NT + 1))

        @block.tensor
        def _(pe):
            tr = [0]
            pj = [0]

            def tr_job(items, n):
                tr_wait_free(pe, tr[0])
                b = bank[4 + tr[0] % 2]
                for i, (src, idn) in enumerate(items):
                    cols = src.shape[1]
                    last = nc.tensor.transpose(b[0:cols, i * n:i * n + src.shape[0]], src, idn)
                last.then_inc(tr_ready, 1)
                tr[0] += 1

            def pj_job(mms, view):
                pj_wait_free(pe, pj[0])
                o = view(bank[pj[0] % 4])
                for i, (l, r) in enumerate(mms):
                    last = nc.tensor.matmul(o, l, r, start=i == 0, stop=i == len(mms) - 1)
                last.then_inc(pj_ready, 1)
                pj[0] += 1

            pe.wait_ge(const_in, 16)
            for t in range(NT):
                pe.wait_ge(xs_ready, t + 1)
                xk = X[0:ROWS[t], t, :].rearrange("p (c k) -> p k c", k=KT)
                for q in range(2):
                    tr_job([(xk[:, 4 * q + i, :], ident[0:ROWS[t], 0:ROWS[t]]) for i in range(4)], ROWS[t])
            pe.wait_ge(cache_k_in, 16 * 7)
            for c in range(NCB):
                tr_job([(natS[:, c, P * i:P * (i + 1)], ident) for i in range(4)], P)
                tr_job([(natD[:, c, i].rearrange("p u c -> p (u c)"), ident) for i in range(3)], P)

            def by_rows(n, t, cols):
                v = chunk_at[n][:, 0:KT * cols].rearrange("p (k c) -> p k c", k=KT)
                pj_job([(xT[:, k, OFF[t]:OFF[t] + ROWS[t]], v[:, k, :]) for k in range(KT)],
                       lambda b: b[0:ROWS[t], 0:cols])

            def roped_chunk(n, cols, rows_before, tile):
                chunk_arrived(pe, n)
                for t in range(NT + 1):
                    if t < NT:
                        by_rows(n, t, cols)
                    if t:
                        pe.wait_ge(rows_ready, rows_before + t)
                        tr_job(tile(t - 1), ROWS[t - 1])

            pe.wait_ge(tr_free_dve, 10)
            tile4 = lambda t: [(ropeA[0:ROWS[t], t % 2, P * i:P * (i + 1)], ident[0:ROWS[t], 0:ROWS[t]])
                               for i in range(4)]
            roped_chunk(0, 512, 0, tile4)
            roped_chunk(1, 328, NT, lambda t: [(kd[0:ROWS[t], t, i].rearrange("p u c -> p (u c)"),
                                                ident[0:ROWS[t], 0:ROWS[t]]) for i in range(3)])

            pe.wait_ge(tr_free_act, emptied(TR, "act", T_DQ - 1))
            for i, (t, h, k0, k1) in enumerate(IX):
                if i >= 2:
                    pe.wait_ge(relu_ready, i - 1)
                b = bank[6 + i % 2]
                hp = slice(64 * (h % 2), 64 * (h % 2) + 64)
                n = KEY_ROWS[t]
                last = nc.tensor.matmul(b[0:n, 0:k1 - k0], iqT[hp, h // 2, OFF[t]:OFF[t] + n], dkiT[hp, 2, k0:k1],
                                        start=True, stop=True)
                if t == NT - 1:
                    q = iqT[hp, h // 2, N_PROMPT:N_ROWS]
                    last = nc.tensor.matmul(b[64:96, 0:min(k1, PAST) - k0], q, dkiC[hp, 2, k0:min(k1, PAST)],
                                            start=True, stop=True)
                    if k1 > PAST:
                        last = nc.tensor.matmul(b[64:96, PAST - k0:k1 - k0], q, dkiT[hp, 2, N_PROMPT:N_ROWS],
                                                start=True, stop=True)
                last.then_inc(ix_ready, 1)

            roped_chunk(2, 512, 2 * NT, tile4)
            chunk_arrived(pe, 3)
            for t in range(NT):
                by_rows(3, t, 512)

            def by_width(v, rhs, cb, g):
                lo, hi = FG[g]
                kt = v.shape[1]
                pj_job([(v[:, k, P * cb:P * (cb + 1)], rhs[:, k, lo:hi]) for k in range(kt)],
                       lambda b: b[:, 0:hi - lo])

            def chunk8(n):
                return chunk_at[n].rearrange("p (k c) -> p k c", k=KT)

            for n in (4, 5):
                chunk_arrived(pe, n)
                for cb in range(4):
                    for g in range(2):
                        by_width(chunk8(n), xT, cb, g)
            for t in range(NT):
                tr_job([(skT[:, i, OFF[t]:OFF[t] + ROWS[t]], ident) for i in range(4)], P)

            pe.wait_ge(pj_free_act, emptied(PJ, "act", J_GSB - 1))
            pe.wait_ge(pj_free_dve, emptied(PJ, "dve", J_GSB - 1))
            pe.wait_ge(tr_free_act, emptied(TR, "act", T_X2 - 1))
            pe.wait_ge(relu_ready, len(IX))
            pe.wait_ge(cache_v_in, 32)
            pe.wait_ge(vnew_in, 32)
            for i in range(NSTEP + PV_LAG):
                if i < NSTEP:
                    s = STEPS[i]
                    if i >= ZR:
                        pe.wait_ge(w_ready, i - ZR + 1)
                    z = bank[2 + i % ZR]
                    if s["kind"] == "prompt":
                        hp = slice(64 * s["half"], 64 * s["half"] + 64)
                        last = nc.tensor.matmul(z[0:s["nk"], 0:s["n"]],
                                                skT[hp, s["pair"], OFF[s["j"]]:OFF[s["j"]] + s["nk"]],
                                                sqT[hp, s["pair"], s["q0"]:s["hi"]], start=True, stop=True,
                                                skip_group_check=True)
                    else:
                        hp = slice(64 * s["half"], 64 * s["half"] + 64)
                        for b in range(NPAIR):
                            k = (skT[hp, b, N_PROMPT:N_ROWS] if s["diag"]
                                 else ksT[hp, b, P * s["j"]:P * (s["j"] + 1)])
                            last = nc.tensor.matmul(z[0:s["nk"], b * DEC:(b + 1) * DEC], k,
                                                    sqT[hp, b, N_PROMPT:N_ROWS], start=b == 0, stop=True,
                                                    skip_group_check=True)
                    last.then_inc(z_ready, 1)
                m = i - TRI_LAG
                if 0 <= m < NSTEP:
                    s = STEPS[m]
                    z = bank[2 + m % ZR]
                    pe.wait_ge(sp_masked, m + 1)
                    last = nc.tensor.matmul(z[0:s["nk"], 0:s["n"]], ntri[0:s["nk"], 0:s["nk"]],
                                            spb[0:s["nk"], m % SPR, 0:s["n"]], start=False, stop=True,
                                            skip_group_check=True)
                    if not s["first"]:
                        pe.wait_ge(suf_ready, m - 1)
                        c0 = s["cover0"] - s["q0"] if s["kind"] == "prompt" else 0
                        o0 = s["cover0"] - s["lo"] if s["kind"] == "prompt" else 0
                        last = nc.tensor.matmul(z[0:s["nk"], c0:s["n"]], nones[:, 0:s["nk"]],
                                                sufb[:, s["stream"], o0:o0 + s["n"] - c0], start=False, stop=True,
                                                skip_group_check=True)
                    last.then_inc(logw_ready, 1)
                m = i - PV_LAG
                if 0 <= m < NSTEP:
                    s = STEPS[m]
                    pe.wait_ge(w_masked, m + 1)
                    acc = bank[s["acc"] % 2]
                    if s["first"] and s["acc"] >= 2:
                        pe.wait_ge(acc_free, s["acc"] - 1)
                    if s["kind"] == "prompt":
                        h = 2 * s["pair"] + s["half"]
                        o = acc[64 * s["half"]:64 * s["half"] + 64, s["q0"] - s["lo"]:s["hi"] - s["lo"]]
                        last = nc.tensor.matmul(o, svP[0:s["nk"], s["j"], 64 * h:64 * h + 64],
                                                wtb[0:s["nk"], m % WR, 0:s["n"]], start=s["first"], stop=s["last"],
                                                skip_group_check=True)
                    else:
                        for b in range(NPAIR):
                            h = 2 * b + s["half"]
                            v = svN[0:DEC, 64 * h:64 * h + 64] if s["diag"] else svC[:, s["j"], 64 * h:64 * h + 64]
                            o = acc[64 * s["half"]:64 * s["half"] + 64, DEC * b:DEC * (b + 1)]
                            last = nc.tensor.matmul(o, v, wtb[0:s["nk"], m % WR, b * DEC:(b + 1) * DEC],
                                                    start=s["first"] and b == 0, stop=True, skip_group_check=True)
                    last.then_inc(pv_done, 1)

            pe.wait_ge(acc_free, 2 * NPAIR + 1)
            jobs = [(t, h) for t in range(NT) for h in range(NH)]

            for i in range(len(jobs) + 2):
                if i < len(jobs):
                    t, h = jobs[i]
                    if i >= 2:
                        pe.wait_ge(lb_ready, i - 1)
                    pr = pairs[i % 2]
                    hp = slice(64 * (h % 2), 64 * (h % 2) + 64)
                    kv = h // 4
                    n = KEY_ROWS[t]
                    q = dqT[hp, h // 2, OFF[t]:OFF[t] + n]
                    if t < NT - 1:
                        last = nc.tensor.matmul(pr[0:n, 0:KEYS[t]], q, dkiT[hp, kv, 0:KEYS[t]], start=True, stop=True)
                    else:
                        qs = dqT[hp, h // 2, N_PROMPT:N_ROWS]
                        for b in range(2):
                            k0, k1 = 272 * b, 272 * (b + 1)
                            o = pr[:, 512 * b:512 * b + 272]
                            nc.tensor.matmul(o[0:64, :], q, dkiT[hp, kv, k0:k1], start=True, stop=True)
                            last = nc.tensor.matmul(o[64:96, 0:min(k1, PAST) - k0], qs, dkiC[hp, kv, k0:min(k1, PAST)],
                                                    start=True, stop=True)
                        last = nc.tensor.matmul(o[64:96, PAST - k0:272], qs, dkiT[hp, kv, N_PROMPT:N_ROWS],
                                                start=True, stop=True)
                    last.then_inc(lg_ready, 1)
                m = i - 2
                if m < 0:
                    continue
                t, h = jobs[m]
                pe.wait_ge(pn_ready, m + 1)
                if m >= 2:
                    pe.wait_ge(pT_copied, m - 1)
                b = bank[4 + m % 2]
                r = ROWS[t]
                for kb in range(t + 1):
                    nk = KEY_ROWS[kb]
                    n = KEY_ROWS[t]
                    last = nc.tensor.transpose(b[0:nk, kb * r:kb * r + n], pb[0:n, m % 3, OFF[kb]:OFF[kb] + nk],
                                               ident[0:n, 0:n])
                if t == NT - 1:
                    for kb in range(NCB + 1):
                        nk = P if kb < NCB else DEC
                        last = nc.tensor.transpose(b[0:nk, kb * r + 64:kb * r + 96],
                                                   pb[64:96, m % 3, P * kb:P * kb + nk], ident[64:96, 64:96])
                last.then_inc(pT_ready, 1)
                if h == NH - 1:
                    pe.wait_ge(pT_copied, m + 1)
                    if t >= 2:
                        pe.wait_ge(oT_copied, t - 1)
                    o = bank[6 + t % 2][:, 0:4 * r].rearrange("p (g q) -> p g q", g=4)
                    n = KEY_ROWS[t]
                    for kb in range(t + 1):
                        nk = KEY_ROWS[kb]
                        for kv in range(2):
                            last = nc.tensor.matmul(o[64 * kv:64 * (kv + 1), :, 0:n],
                                                    dvP[0:nk, kb, 64 * kv:64 * kv + 64],
                                                    pTb[0:nk, 4 * kv:4 * kv + 4, kb * r:kb * r + n],
                                                    start=kb == 0, stop=True, skip_group_check=True)
                    if t == NT - 1:
                        for kb in range(NCB + 1):
                            nk = P if kb < NCB else DEC
                            v = dvC[:, kb] if kb < NCB else dvN[0:DEC]
                            for kv in range(2):
                                last = nc.tensor.matmul(o[64 * kv:64 * (kv + 1), :, 64:96],
                                                        v[:, 64 * kv:64 * kv + 64],
                                                        pTb[0:nk, 4 * kv:4 * kv + 4, kb * r + 64:kb * r + 96],
                                                        start=False, stop=True, skip_group_check=True)
                    last.then_inc(pvd_done, 1)

            pe.wait_ge(oT_copied, NT)
            for n in (6, 7):
                chunk_arrived(pe, n)
                for cb in range(4):
                    for g in range(2):
                        by_width(chunk8(n), xT, cb, g)
            chunk_arrived(pe, 8)
            for cb in range(8):
                for g in range(2):
                    by_width(chunk_at[8].rearrange("p (k c) -> p k c", k=4), osbT, cb, g)
            chunk_arrived(pe, 9)
            for cb in range(8):
                chunk_arrived(pe, 10 + cb // 4)
                for g in range(2):
                    by_width(chunk8(10 + cb // 4), xT, cb % 4, g)
                    by_width(chunk_at[9].rearrange("p (k c) -> p k c", k=4), odsaT, cb, g)
            pe.wait_ge(merged_ready, 16)
            chunk_arrived(pe, 12)
            chunk_arrived(pe, 13)
            for t in range(NT + 2):
                if t < NT:
                    for c in range(2):
                        pj_job([(merged[:, k, OFF[t]:OFF[t] + ROWS[t]], chunk8(12 + c)[:, k, :]) for k in range(KT)],
                               lambda b: b[0:ROWS[t], :])
                u = t - 2
                if u >= 0:
                    pe.wait_ge(x2_ready, u + 1)
                    xk = x2row[0:ROWS[u], u % 2, :].rearrange("p (c k) -> p k c", k=KT)
                    for q in range(2):
                        tr_job([(xk[:, 4 * q + i, :], ident[0:ROWS[u], 0:ROWS[u]]) for i in range(4)], ROWS[u])
            pe.wait_ge(wr_in, 32)
            pe.wait_ge(tr_free_act, emptied(TR, "act", T_X2 + 2 * NT - 1))
            for lo, hi in FG:
                pj_job([(wr[:, k, :], xT[:, k, lo:hi]) for k in range(KT)], lambda b: b[0:36, 0:hi - lo])
            pe.wait_ge(pj_free_act, emptied(PJ, "act", len(PJ) - 1))
            tr_wait_free(pe, tr[0])
            for t in range(NT):
                last = nc.tensor.transpose(bank[4 + tr[0] % 2][0:ROWS[t], 36 * t:36 * (t + 1)],
                                           lgT[0:36, OFF[t]:OFF[t] + ROWS[t]], ident[0:36, 0:36])
            last.then_inc(tr_ready, 1)
            pe.wait_ge(onehot_ready, 1)
            b = bank[0]
            pe.wait_ge(pj_free_act, emptied(PJ, "act", len(PJ) - 1))
            nc.tensor.matmul(b[:, 0:NT * NE], stri, rt[:, 0:NT * NE], start=True, stop=True, skip_group_check=True)
            nc.tensor.matmul(b[:, 0:(NT + 1) * NE], nones, earlier, start=False, stop=True, skip_group_check=True)\
                .then_inc(pos_ready, 1)
            pe.wait_ge(slots_ready, 1)
            for c in range(2):
                for t in range(NT):
                    last = nc.tensor.matmul(bank[1][0:CAP, 0:NBLK], at_slot[c][:, t, :], at_block[c][:, t, :],
                                            start=c + t == 0, stop=c == 1 and t == NT - 1)
            last.then_inc(idx_ready, 1)

            def x_to_width(q, done):
                x = Xg[:, q, :].rearrange("p (c k) -> p k c", k=KT)
                for k in range(KT):
                    last = nc.tensor.transpose(bank[4 * q][:, k * CAP:(k + 1) * CAP], x[:, k, :], ident[0:CAP, 0:CAP])
                last.then_inc(done, 1)

            def gate_up(q, w, done):
                wv = w[:, 0:4096].rearrange("p (g k c) -> p g k c", g=2, k=KT)
                for k in range(KT):
                    for f in range(2):
                        last = nc.tensor.matmul(
                            bank[4 * q + 1][64 * f:64 * f + 64, 0:256].rearrange("p (g c) -> p g c", g=2),
                            xgT[:, q, k, :], wv[:, :, k, P * f:P * (f + 1)], start=k == 0, stop=k == KT - 1)
                last.then_inc(done, 1)

            def hidden_to_width(q, done):
                nc.tensor.transpose(bank[4 * q + 2][:, 0:P], hid[:, q, :], ident).then_inc(done, 1)

            def down(q, w, done):
                wv = w[:, 4096:6144].rearrange("p (j c) -> p j c", j=2)
                for f in range(2):
                    for c in range(2):
                        last = nc.tensor.matmul(bank[4 * q + 3][64 * c:64 * c + 64, :],
                                                hidT[:, q, 64 * f:64 * f + 64], wv[:, f, 512 * c:512 * (c + 1)],
                                                start=f == 0, stop=f == 1)
                last.then_inc(done, 1)

            def down_in_turn(i, s):
                pe.wait_ge(hidT_ready, i * 4 + s + 1)
                pe.wait_ge(y_copied[s % 2], i * 2 + s // 2)
                down(s % 2, moe_w[s], y_done[s])

            pe.wait_ge(gath[0], 16)
            x_to_width(0, xgp_ready[0])
            with pe.Fori(0, NE // 4) as i:
                for s in range(4):
                    q = s % 2
                    pe.wait_ge(xgT_ready[q], i * 2 + s // 2 + 1)
                    pe.wait_ge(mw_in[s], i * 48 + 48)
                    gate_up(q, moe_w[s], gu_ready)
                    pe.wait_ge(gath[1 - q], (i * 2 + (s + 1) // 2 + 1) * 16)
                    nc.tensor.sem_inc(pe_turns, 1)
                    x_to_width(1 - q, xgp_ready[1 - q])
                    if s:
                        down_in_turn(i, s - 1)
                    pe.wait_ge(hid_ready, i * 4 + s + 1)
                    hidden_to_width(q, hT_ready)
                down_in_turn(i, 3)
            over = pe.value_load(over_i[0:1, MAX_OVER:MAX_OVER + 1], min_val=0, max_val=MAX_OVER)
            with pe.If(over > 0):
                pe.wait_ge(xgT_ready[0], NE // 2 + 1)
                pe.wait_ge(y_copied[0], NE // 2)
                with pe.Fori(0, MAX_OVER) as b:
                    pe.wait_ge(o_g, b * 16 + 16)
                    nc.tensor.sem_inc(pe_turns, 1)
                    x_to_width(0, o_step)
                    pe.wait_ge(o_w, b * 48 + 48)
                    pe.wait_ge(o_step, b * 10 + 2)
                    gate_up(0, moe_w[0], o_step)
                    pe.wait_ge(o_step, b * 10 + 5)
                    hidden_to_width(0, o_step)
                    pe.wait_ge(o_step, b * 10 + 7)
                    down(0, moe_w[0], o_step)

        @block.scalar
        def _(act):
            tr = [0]
            chain = [0]

            def link(ins):
                chain[0] += 1
                ins.then_inc(act_chain, 1)
                act.wait_ge(act_chain, chain[0])

            nc.scalar.preload_act_table_set("natural_log_exp_and_others")
            for t in range(NT):
                r = ROWS[t]
                act.wait_ge(x_in[t], 16 * len(row_pieces(t)))
                link(nc.scalar.activation(arena[0:r, 0:D], X[0:r, t, :], ACT.Square, scale=1.0 / 32.0,
                                          accum_out=ss[0:r, t:t + 1]))
                nc.scalar.sem_inc(ss_ready, 1)
            tr[0] = 10

            def tr_copy(dst, n, cols, rows=P):
                act.wait_ge(tr_ready, tr[0] + 1)
                b = bank[4 + tr[0] % 2]
                nc.scalar.activation(dst, b[0:rows, 0:n * cols].rearrange("p (i c) -> p i c", i=n), ACT.Copy)\
                    .then_inc(tr_free_act, 1)
                tr[0] += 1

            for c in range(NCB):
                tr_copy(ksT[:, :, P * c:P * (c + 1)], 4, P)
                tr_copy(dkiC[:, :, P * c:P * (c + 1)], 3, P)
            act.wait_ge(xs_ready, NT)
            act.wait_ge(tr_ready, 10)
            for t in range(NT):
                tr_copy(iqT[:, :, OFF[t]:OFF[t] + ROWS[t]], 4, ROWS[t])

            def pj_copy(n, dst, src, func=ACT.Copy, scale=1.0, also=None):
                act.wait_ge(pj_ready, n + 1)
                ins = nc.scalar.activation(dst, src(bank[n % 4]), func, scale=scale)
                ins.then_inc(pj_free_act, 1)

            def squares_of(n, t, i, c0, cols):
                act.wait_ge(pj_ready, n + t + 1)
                if i >= 2:
                    act.wait_ge(rope_parts, i - 1 + NT)
                r = ROWS[t]
                nc.scalar.activation(ropeQ[0:r, i % 2, 0:cols], bank[(n + t) % 4][0:r, c0:c0 + cols],
                                     ACT.Square, scale=1.0 / 8.0).then_inc(squares, 1)

            for t in range(NT + 1):
                if t < NT:
                    squares_of(J_SM, t, t, N_SMALL1, 128)
                if t:
                    tr_copy(dkiT[:, :, OFF[t - 1]:OFF[t - 1] + ROWS[t - 1]], 3, ROWS[t - 1])
            for i, (t, h, k0, k1) in enumerate(IX):
                r = ROWS[t]
                act.wait_ge(ix_ready, i + 1)
                if i >= 2:
                    act.wait_ge(relu_used, i - 1)
                nc.scalar.activation(rb[0:r, i % 2, 0:k1 - k0], bank[6 + i % 2][0:r, 0:k1 - k0], ACT.Relu)\
                    .then_inc(relu_ready, 1)
            for t in range(NT + 1):
                if t < NT:
                    squares_of(J_DQ, t, NT + t, 0, 512)
                if t:
                    tr_copy(dqT[:, :, OFF[t - 1]:OFF[t - 1] + ROWS[t - 1]], 4, ROWS[t - 1])
            for t in range(NT):
                r = ROWS[t]
                act.wait_ge(pj_ready, J_SV + t + 1)
                link(nc.scalar.activation(svP[0:r, t, :], bank[(J_SV + t) % 4][0:r, :], ACT.Copy))
                nc.scalar.sem_inc(pj_free_act, 1)
                nc.scalar.sem_inc(sv_rows, 1)
            for n0, dst, scale in ((J_SK, skT, 1.0), (J_SQ, sqT, HD ** -0.5)):
                for cb in range(4):
                    for g in range(2):
                        lo, hi = FG[g]
                        pj_copy(n0 + 2 * cb + g, dst[:, cb, lo:hi], lambda b: b[:, 0:hi - lo], scale=scale)
            for t in range(NT):
                r = ROWS[t]
                act.wait_ge(tr_ready, tr[0] + 1)
                dst = skR4 if t == NT - 1 else skR[:, t, :]
                link(nc.scalar.activation(dst[0:r, :], bank[4 + tr[0] % 2][0:r, :], ACT.Copy))
                nc.scalar.sem_inc(tr_free_act, 1)
                nc.scalar.sem_inc(sk_rows, 1)
                tr[0] += 1

            for i in range(NSTEP + TRI_LAG):
                if i < NSTEP:
                    s = STEPS[i]
                    act.wait_ge(cap_ready, i + 1)
                    v = spb[0:s["nk"], i % SPR, 0:s["n"]]
                    link(nc.scalar.activation(v, v, ACT.Exp))
                    nc.scalar.activation(v, v, ACT.Ln, bias=1.0).then_inc(ln_ready, 1)
                m = i - TRI_LAG
                if 0 <= m < NSTEP:
                    s = STEPS[m]
                    act.wait_ge(logw_ready, m + 1)
                    if m >= WR:
                        act.wait_ge(pv_done, m - WR + 1)
                    nc.scalar.activation(wtb[0:s["nk"], m % WR, 0:s["n"]], bank[2 + m % ZR][0:s["nk"], 0:s["n"]],
                                         ACT.Exp).then_inc(w_ready, 1)
                e = i - TRI_LAG - 2
                if 0 <= e < NSTEP and e + 1 < NSTEP and STEPS[e]["acc"] != STEPS[e + 1]["acc"]:
                    s = STEPS[e]
                    act.wait_ge(pv_done, e + 1)
                    nc.scalar.activation(osbT[:, s["pair"], s["lo"]:s["hi"]], bank[s["acc"] % 2][:, 0:s["hi"] - s["lo"]],
                                         ACT.Copy).then_inc(acc_free, 1)
            act.wait_ge(pv_done, NSTEP)
            nc.scalar.activation(osbT[:, :, N_PROMPT:N_ROWS],
                                 bank[0][:, 0:NPAIR * DEC].rearrange("p (b q) -> p b q", b=NPAIR),
                                 ACT.Copy).then_inc(acc_free, 1)

            jobs = [(t, h) for t in range(NT) for h in range(NH)]
            for i in range(len(jobs) + 2):
                if i < len(jobs):
                    t, h = jobs[i]
                    r, w = ROWS[t], KEYS[t]
                    act.wait_ge(lb_ready, i + 1)
                    if i >= 3:
                        act.wait_ge(pT_ready, i - 2)
                    nc.scalar.activation(pb[0:r, i % 3, 0:w], Lb[0:r, i % 2, 0:w], ACT.Exp, scale=HD ** -0.5,
                                         bias=nbias[0:r, i % 2:i % 2 + 1],
                                         accum_out=rsum[0:r, i % 3:i % 3 + 1]).then_inc(p_ready, 1)
                m = i - 2
                if m < 0:
                    continue
                t, h = jobs[m]
                act.wait_ge(pT_ready, m + 1)
                if h == 0 and t:
                    act.wait_ge(pvd_done, t)
                n = (t + 1) * ROWS[t]
                nc.scalar.activation(pTb[:, h, 0:n], bank[4 + m % 2][:, 0:n], ACT.Copy).then_inc(pT_copied, 1)
                if h == NH - 1:
                    act.wait_ge(pvd_done, t + 1)
                    nc.scalar.activation(odsaT[:, :, OFF[t]:OFF[t] + ROWS[t]],
                                         bank[6 + t % 2][:, 0:4 * ROWS[t]].rearrange("p (g q) -> p g q", g=4),
                                         ACT.Copy).then_inc(oT_copied, 1)

            for cb in range(8):
                for g in range(2):
                    lo, hi = FG[g]
                    n = J_GSB + 2 * cb + g
                    act.wait_ge(pj_ready, n + 1)
                    link(nc.scalar.activation(merged[:, cb, lo:hi], bank[n % 4][:, 0:hi - lo], ACT.Sigmoid))
                    nc.scalar.sem_inc(pj_free_act, 1)
                    nc.scalar.sem_inc(gate_ready, 1)
            for j in range(16):
                cb, g = j // 2, j % 2
                lo, hi = FG[g]
                n = J_GB + 2 * j
                act.wait_ge(pj_ready, n + 1)
                if j >= 2:
                    act.wait_ge(half_merged, j - 1)
                link(nc.scalar.activation(tabs[:, (j % 2) * 280:(j % 2) * 280 + hi - lo], bank[n % 4][:, 0:hi - lo],
                                          ACT.Sigmoid))
                nc.scalar.sem_inc(pj_free_act, 1)
                nc.scalar.sem_inc(gate_ready, 1)
            for t in range(NT + 2):
                if t < NT:
                    r = ROWS[t]
                    act.wait_ge(h_ready, t + 1)
                    link(nc.scalar.activation(scrap[0:r, :], X[0:r, t, :], ACT.Square, scale=1.0 / 32.0,
                                              accum_out=ss[0:r, t:t + 1]))
                    nc.scalar.sem_inc(ss2_ready, 1)
                u = t - 2
                if u >= 0:
                    for q in range(2):
                        tr_copy(xT[:, 4 * q:4 * q + 4, OFF[u]:OFF[u] + ROWS[u]], 4, ROWS[u])
            for g, (lo, hi) in enumerate(FG):
                n = J_RT + g
                act.wait_ge(pj_ready, n + 1)
                nc.scalar.activation(lgT[0:36, lo:hi], bank[n % 4][0:36, 0:hi - lo], ACT.Copy).then_inc(pj_free_act, 1)
            act.wait_ge(tr_ready, tr[0] + 1)
            nc.scalar.activation(rl, bank[4 + tr[0] % 2][:, 0:36 * NT].rearrange("p (t c) -> p t c", t=NT), ACT.Copy)\
                .then_inc(logits_ready, 1)
            act.wait_ge(rvals_ready, 1)
            link(nc.scalar.activation(gx[:, 0:4 * NT], gx[:, 0:4 * NT], ACT.Exp))
            nc.scalar.sem_inc(rexp_ready, 1)
            act.wait_ge(rvals_ready, 2)
            link(nc.scalar.activation(gx[:, 40:40 + NT], gx[:, 40:40 + NT], ACT.Exp))
            nc.scalar.sem_inc(rexp_ready, 1)

            def copy_x(q, done):
                nc.scalar.activation(xgT[:, q], bank[4 * q].rearrange("p (k s) -> p k s", k=KT), ACT.Copy)\
                    .then_inc(done, 1)

            def silu(q, done):
                nc.scalar.activation(sil[:, q, :], bank[4 * q + 1][:, 0:P], ACT.Silu).then_inc(done, 1)

            def store_y(q, first):
                for c in range(2):
                    act.dma_start(y_d[bass.ds(first, CAP), 512 * c:512 * (c + 1)], Yb[64 * c:64 * c + 64, q, :])\
                        .then_inc(y_out[q], 16)

            def y_in_turn(i, s):
                q = s % 2
                act.wait_ge(y_done[s], i + 1)
                act.wait_ge(y_out[q], (i * 2 + s // 2) * 32)
                nc.scalar.activation(Yb[:, q, :], bank[4 * q + 3], ACT.Copy).then_inc(y_copied[q], 1)
                act.wait_ge(y_copied[q], i * 2 + s // 2 + 1)
                store_y(q, (i * 4 + s) * CAP)

            act.wait_ge(xgp_ready[0], 1)
            copy_x(0, xgT_ready[0])
            with act.Fori(0, NE // 4) as i:
                for s in range(4):
                    q = s % 2
                    act.wait_ge(gu_ready, i * 4 + s + 1)
                    silu(q, silu_ready)
                    act.wait_ge(xgp_ready[1 - q], i * 2 + (s + 1) // 2 + 1)
                    copy_x(1 - q, xgT_ready[1 - q])
                    if s:
                        y_in_turn(i, s - 1)
                y_in_turn(i, 3)
            for q in range(2):
                act.wait_ge(y_out[q], NE // 2 * 32)
            over = act.value_load(over_i[0:1, MAX_OVER:MAX_OVER + 1], min_val=0, max_val=MAX_OVER)
            with act.If(over > 0):
                with act.Fori(0, MAX_OVER) as b:
                    act.wait_ge(o_step, b * 10 + 1)
                    copy_x(0, o_step)
                    act.wait_ge(o_step, b * 10 + 3)
                    silu(0, o_step)
                    act.wait_ge(o_step, b * 10 + 8)
                    nc.scalar.activation(Yb[:, 0, :], bank[3], ACT.Copy).then_inc(o_step, 1)
                    act.wait_ge(o_step, b * 10 + 9)
                    store_y(0, (b + NE) * CAP)
                    act.wait_ge(y_out[0], (b + NE // 2 + 1) * 32)
                    nc.scalar.sem_inc(o_step, 1)
            nc.scalar.sem_inc(results_out, 1)

        @block.gpsimd
        def _(pool):
            chain = [0]

            def link(ins):
                chain[0] += 1
                ins.then_inc(pool_chain, 1)
                pool.wait_ge(pool_chain, chain[0])

            def inverse_root(t, ready, done):
                r = ROWS[t]
                pool.wait_ge(ready, t + 1)
                link(nc.gpsimd.tensor_scalar(rstd[0:r, t:t + 1], ss[0:r, t:t + 1], EPS, None, ALU.add))
                nc.gpsimd.tensor_tensor(rstd[0:r, t:t + 1], rstd[0:r, t:t + 1], mhalf[0:r, 0:1], ALU.pow)\
                    .then_inc(done, 1)

            link(nc.gpsimd.memset(mhalf, -0.5))
            for t in range(NT):
                inverse_root(t, ss_ready, rstd_ready)
            pool.wait_ge(const_in, 16)
            pool.wait_ge(gains_in, 16 * 7)
            for w in range(2):
                for v, base in ((0, cos), (1, sin)):
                    g = gqk[:, (2 * w + v) * HD:(2 * w + v + 1) * HD].rearrange("p (o c) -> p o c", o=1)
                    link(nc.gpsimd.tensor_tensor(tab[:, 2 * w + v], base, g.broadcast_to([P, NT, HD]), ALU.mult))
            nc.gpsimd.sem_inc(tables_ready, 1)
            pool.wait_ge(zero_ready, 1)
            pool.dma_start(y_d[NE * CAP:, :].rearrange("(p a) (b c) -> p a b c", p=64, b=2)
                           .rearrange("p a b c -> p (a b) c"),
                           zeros[0:64, :].rearrange("p (o c) -> p o c", o=1).broadcast_to([64, 2 * MAX_OVER, 512]))\
                .then_inc(y_zeroed, 16)
            for n in range(3 * NT):
                t, kind = n % NT, n // NT
                r = ROWS[t]
                pool.wait_ge(rope_parts, n + 1)
                if kind:
                    hs = 2 if kind == 1 else NH
                    f = rq[0:r, n % 2, 0:hs]
                    link(nc.gpsimd.tensor_scalar(f, ssq[0:r, n % 2, 0:hs], EPS, None, ALU.add))
                    link(nc.gpsimd.tensor_tensor(f, f, mhalf[0:r, 0:hs], ALU.pow))
                if kind == 1:
                    d = kd[0:r, t, :, 0, :]
                    link(nc.gpsimd.tensor_tensor(d, d, ropeB[0:r, n % 2, 0:192].rearrange("p (b c) -> p b c", b=3),
                                                 ALU.add))
                    link(nc.gpsimd.tensor_tensor(d[:, 0:2], d[:, 0:2],
                                                 rq[0:r, n % 2, 0:2].rearrange("p (h o) -> p h o", o=1)
                                                 .broadcast_to([r, 2, HD]), ALU.mult))
                    link(nc.gpsimd.tensor_copy(kd[0:r, t, :, 1, :], d))
                    nc.gpsimd.sem_inc(small_rows, 1)
                else:
                    A = ropeA[0:r, t % 2, :]
                    link(nc.gpsimd.tensor_tensor(A, A, ropeB[0:r, n % 2, :], ALU.add))
                    if kind == 2:
                        A3 = A.rearrange("p (h c) -> p h c", h=NH)
                        link(nc.gpsimd.tensor_tensor(A3, A3, rq[0:r, n % 2, :].rearrange("p (h o) -> p h o", o=1)
                                                     .broadcast_to([r, NH, HD]), ALU.mult))
                nc.gpsimd.sem_inc(rows_ready, 1)

            pool.wait_ge(keys_out, 16 * 6 * (NT + 1))
            for i in range(NSTEP + PV_LAG):
                m = i - 1
                if 0 <= m < NSTEP:
                    s = STEPS[m]
                    if s["first"]:
                        prev = [k for k in range(m) if STEPS[k]["stream"] == s["stream"]]
                        if prev:
                            pool.wait_ge(logw_ready, prev[-1] + 1)
                        link(nc.gpsimd.memset(sufb[:, s["stream"], :], 0.0))
                    pool.wait_ge(sp_ready, m + 1)
                    v = spb[0:s["nk"], m % SPR, 0:s["n"]]
                    if s["diag"]:
                        if s["kind"] == "prompt":
                            w = min(s["nk"], s["n"])
                            v = v[:, 0:w]
                            link(nc.gpsimd.affine_select(out=v, in_=v, compare_op=ALU.is_gt, fill=0.0, base=0,
                                                         pattern=[[1, w]], channel_multiplier=-1))
                        else:
                            v3 = v.rearrange("p (b q) -> p b q", b=NPAIR)
                            link(nc.gpsimd.affine_select(out=v3, in_=v3, compare_op=ALU.is_gt, fill=0.0, base=0,
                                                         pattern=[[0, NPAIR], [1, DEC]], channel_multiplier=-1))
                    nc.gpsimd.sem_inc(sp_masked, 1)
                m = i - TRI_LAG
                if 0 <= m < NSTEP:
                    s = STEPS[m]
                    if not s["last"]:
                        pool.wait_ge(logw_ready, m + 1)
                        o0 = s["q0"] - s["lo"] if s["kind"] == "prompt" else 0
                        v = sufb[0:s["nk"], s["stream"], o0:o0 + s["n"]]
                        link(nc.gpsimd.tensor_tensor(v, v, spb[0:s["nk"], m % SPR, 0:s["n"]], ALU.add))
                    nc.gpsimd.sem_inc(suf_ready, 1)
                m = i - TRI_LAG - 1
                if 0 <= m < NSTEP:
                    s = STEPS[m]
                    pool.wait_ge(w_ready, m + 1)
                    if s["diag"]:
                        if s["kind"] == "prompt":
                            w = min(s["nk"], s["n"])
                            v = wtb[0:s["nk"], m % WR, 0:w]
                            link(nc.gpsimd.affine_select(out=v, in_=v, compare_op=ALU.is_gt, fill=0.0, base=0,
                                                         pattern=[[1, w]], channel_multiplier=-1))
                        else:
                            v3 = wtb[0:s["nk"], m % WR, 0:s["n"]].rearrange("p (b q) -> p b q", b=NPAIR)
                            link(nc.gpsimd.affine_select(out=v3, in_=v3, compare_op=ALU.is_gt, fill=0.0, base=0,
                                                         pattern=[[0, NPAIR], [1, DEC]], channel_multiplier=-1))
                    nc.gpsimd.sem_inc(w_masked, 1)

            pool.wait_ge(oT_copied, NT)
            load_chunk(pool, 8)
            load_chunk(pool, 9)
            load_chunk(pool, 10)
            load_chunk(pool, 11)
            pool.dma_start(wr[:, :, 0:4], a["w_group"].rearrange("(p k) c -> p k c", k=KT)).then_inc(wr_in, 16)
            pool.dma_start(wr[:, :, 4:36], a["w_router"].rearrange("(p k) c -> p k c", k=KT)).then_inc(wr_in, 16)
            load_chunk(pool, 12)
            load_chunk(pool, 13)
            pool.wait_ge(y_zeroed, 16)
            pool.wait_ge(pj_ready, used_at[11])
            for t in range(NT):
                for p0, p1, which, r0 in row_pieces(t):
                    src = a["meta_tokens"] if which == "meta" else a["x_" + which]
                    pool.dma_start(X[p0:p1, t, :], src[r0:r0 + p1 - p0, :]).then_inc(xres_in, 16)
            pool.wait_ge(pj_ready, used_at[10])
            pool.dma_start(g2b, a["norm2_g"].rearrange("(o c) -> o c", o=1).broadcast_to([P, D])).then_inc(g2_in, 16)
            for t in range(NT):
                inverse_root(t, ss2_ready, rstd2_ready)
                pool.wait_ge(x2_ready, t + 1)
                pool.dma_start(xn2_d[OFF[t]:OFF[t] + ROWS[t], :], x2row[0:ROWS[t], t % 2, :]).then_inc(x2_stored[t], 16)
            pool.wait_ge(idx_in, 1)
            for t in range(NT):
                pool.wait_ge(x2_stored[t], 16)
            def gather(q, block_no, copied):
                nc.gpsimd.tensor_copy(idx_now[:, q:q + 1], idxs[:, block_no]).then_inc(idx_now_ready, 1)
                pool.wait_ge(idx_now_ready, copied)
                nc.gpsimd.sem_inc(pool_turns, 1)
                pool.indirect_dma_start(Xg[:, q, :], None, xn2_d,
                                        bass.IndirectOffsetOnAxis(ap=idx_now[:, q:q + 1], axis=0)).then_inc(gath[q], 16)

            for q in range(2):
                gather(q, slice(q, q + 1), q + 1)
            with pool.Fori(0, NE // 4) as i:
                for s in range(4):
                    q = s % 2
                    pool.wait_ge(xgp_ready[q], i * 2 + s // 2 + 1)
                    gather(q, bass.ds(i * 4 + s + 2, 1), i * 4 + s + 3)
            pool.wait_ge(gath[0], (NE // 2 + 1) * 16)
            pool.wait_ge(gath[1], (NE // 2 + 1) * 16)
            over = pool.value_load(over_i[0:1, MAX_OVER:MAX_OVER + 1], min_val=0, max_val=MAX_OVER)
            with pool.If(over > 0):
                pool.wait_ge(xgp_ready[0], NE // 2 + 1)
                with pool.Fori(0, MAX_OVER) as b:
                    pool.wait_ge(o_step, b * 10)
                    nc.gpsimd.tensor_copy(idx_now[:, 0:1], idxs[:, bass.ds(b + NE, 1)]).then_inc(o_idx, 1)
                    pool.wait_ge(o_idx, b + 1)
                    nc.gpsimd.sem_inc(pool_turns, 1)
                    pool.indirect_dma_start(Xg[:, 0, :], None, xn2_d,
                                            bass.IndirectOffsetOnAxis(ap=idx_now[:, 0:1], axis=0)).then_inc(o_g, 16)
            pool.wait_ge(results_out, 1)
            for t in range(NT):
                for c in range(2):
                    n = 2 * t + c
                    pool.indirect_dma_start(arena[0:ROWS[t], n * D:(n + 1) * D], None, y_d,
                                            bass.IndirectOffsetOnAxis(ap=slot_i[c][0:ROWS[t], t:t + 1], axis=0))\
                        .then_inc(comb_in[n], 16)

        @block.vector
        def _(dve):
            chain = [0]

            def link(ins):
                chain[0] += 1
                ins.then_inc(dve_chain, 1)
                dve.wait_ge(dve_chain, chain[0])
                return ins

            for p in pairs:
                link(nc.vector.memset(p[:, :], 0.0))

            def norm_rows(t, ready, out_ap):
                r = ROWS[t]
                dve.wait_ge(ready, t + 1)
                link(nc.vector.tensor_scalar(out_ap, X[0:r, t, :], rstd[0:r, t:t + 1], None, ALU.mult))

            for t in range(NT):
                norm_rows(t, rstd_ready, X[0:ROWS[t], t, :])
                nc.vector.sem_inc(xs_ready, 1)
            dve.wait_ge(gains_in, 16 * 7)
            for n in range(2 * NT):
                t, q = n // 2, n % 2
                r = ROWS[t]
                dve.wait_ge(tr_ready, n + 1)
                nc.vector.tensor_tensor(xT[:, 4 * q:4 * q + 4, OFF[t]:OFF[t] + r],
                                        bank[4 + n % 2][:, 0:4 * r].rearrange("p (i c) -> p i c", i=4),
                                        g1[:, 4 * q:4 * q + 4].rearrange("p (k o) -> p k o", o=1)
                                        .broadcast_to([P, 4, r]), ALU.mult).then_inc(tr_free_dve, 1)

            def rope(src, A, B, ct, st, r, heads):
                def bc(v, w):
                    return v.rearrange("p (o c) -> p o c", o=1).broadcast_to([r, heads, w])
                nc.vector.tensor_tensor(A, src, bc(ct, HD), ALU.mult)
                nc.vector.tensor_tensor(B[:, :, 0:HALF], src[:, :, HALF:HD], bc(st[:, 0:HALF], HALF), ALU.mult)
                return nc.vector.tensor_tensor(B[:, :, HALF:HD], src[:, :, 0:HALF], bc(st[:, HALF:HD], HALF), ALU.mult)

            def wait_rope_buffers(n):
                if n >= 2:
                    dve.wait_ge(rows_ready, n - 1)

            nc.vector.memset(zeros, 0.0).then_inc(zero_ready, 1)
            dve.wait_ge(tables_ready, 1)
            for t in range(NT):
                r = ROWS[t]
                n = J_IQ + t
                dve.wait_ge(pj_ready, n + 1)
                wait_rope_buffers(t)
                if t >= 2:
                    dve.wait_ge(tr_ready, T_IQ + t - 1)
                src = bank[n % 4][0:r, :].rearrange("p (h c) -> p h c", h=NH)
                link(rope(src, ropeA[0:r, t % 2, :].rearrange("p (h c) -> p h c", h=NH),
                          ropeB[0:r, t % 2, :].rearrange("p (h c) -> p h c", h=NH), cos[0:r, t], sin[0:r, t], r, NH))
                nc.vector.sem_inc(pj_free_dve, 1)
                nc.vector.sem_inc(rope_parts, 1)
            for t in range(NT):
                r = ROWS[t]
                n = J_SM + t
                m = NT + t
                b = bank[n % 4][0:r, :]
                dve.wait_ge(squares, t + 1)
                wait_rope_buffers(m)
                nc.vector.tensor_scalar(iws[0:r, t, :], b[:, HD:HD + NH], HD ** -0.5 * NH ** -0.5, None, ALU.mult)
                nc.vector.tensor_copy(dvP[0:r, t, :], b[:, N_SMALL1 + 128:328])
                B = ropeB[0:r, m % 2, 0:192].rearrange("p (b c) -> p b c", b=3)
                rope(b[:, 0:HD].rearrange("p (h c) -> p h c", h=1), kd[0:r, t, 2:3, 0, :], B[:, 2:3], cos[0:r, t],
                     sin[0:r, t], r, 1)
                rope(b[:, N_SMALL1:N_SMALL1 + 128].rearrange("p (h c) -> p h c", h=2), kd[0:r, t, 0:2, 0, :],
                     B[:, 0:2], tab[0:r, 2, t], tab[0:r, 3, t], r, 2)
                link(nc.vector.tensor_reduce(ssq[0:r, m % 2, 0:2],
                                             ropeQ[0:r, t % 2, 0:128].rearrange("p (h c) -> p h c", h=2), AX.X, ALU.add))
                nc.vector.sem_inc(pj_free_dve, 1)
                nc.vector.sem_inc(rope_parts, 1)
            for i, (t, h, k0, k1) in enumerate(IX):
                r = ROWS[t]
                dve.wait_ge(relu_ready, i + 1)
                s = SC[t][0:r, k0:k1]
                if h == 0:
                    link(nc.vector.tensor_scalar(s, rb[0:r, i % 2, 0:k1 - k0], iws[0:r, t, 0:1], None, ALU.mult))
                else:
                    link(nc.vector.scalar_tensor_tensor(s, rb[0:r, i % 2, 0:k1 - k0], iws[0:r, t, h:h + 1], s,
                                                        ALU.mult, ALU.add))
                nc.vector.sem_inc(relu_used, 1)
            for t in range(NT):
                r = ROWS[t]
                n = J_DQ + t
                m = 2 * NT + t
                dve.wait_ge(squares, NT + t + 1)
                wait_rope_buffers(m)
                if t >= 2:
                    dve.wait_ge(tr_ready, T_DQ + t - 1)
                src = bank[n % 4][0:r, :].rearrange("p (h c) -> p h c", h=NH)
                rope(src, ropeA[0:r, t % 2, :].rearrange("p (h c) -> p h c", h=NH),
                     ropeB[0:r, m % 2, :].rearrange("p (h c) -> p h c", h=NH), tab[0:r, 0, t], tab[0:r, 1, t], r, NH)
                link(nc.vector.tensor_reduce(ssq[0:r, m % 2, :],
                                             ropeQ[0:r, (NT + t) % 2, :].rearrange("p (h c) -> p h c", h=NH),
                                             AX.X, ALU.add))
                nc.vector.sem_inc(pj_free_dve, 1)
                nc.vector.sem_inc(rope_parts, 1)
            link(nc.vector.memset(SC[0][0:ROWS[0], :], 0.0))
            link(nc.vector.memset(SC[0][0:N_META, N_META:KEYS[0]], -BIG))
            for t in range(1, NT):
                r = ROWS[t]
                w = KEYS[t]
                hide = w - CHUNK if t < NT - 1 else N_PROMPT
                link(nc.vector.memset(SC[t][0:64, hide:w], HIDDEN))
                for n in range(SEL_PROMPT // 8):
                    link(nc.vector.max(top8[0:r, :], SC[t][0:r, :]))
                    link(nc.vector.match_replace(SC[t][0:r, :], top8[0:r, :], SC[t][0:r, :], TAKEN))
                if t == NT - 1:
                    for n in range((SEL_SAMPLE - SEL_PROMPT) // 8):
                        link(nc.vector.max(top8[64:96, :], SC[t][64:96, :]))
                        link(nc.vector.match_replace(SC[t][64:96, :], top8[64:96, :], SC[t][64:96, :], TAKEN))
                link(nc.vector.tensor_scalar(SC[t][0:r, :], SC[t][0:r, :], TAKEN, -BIG, ALU.not_equal, ALU.mult))

            dve.wait_ge(keys_out, 16 * 6 * (NT + 1))
            for i in range(NSTEP + 1):
                if i < NSTEP:
                    s = STEPS[i]
                    dve.wait_ge(z_ready, i + 1)
                    if i >= SPR:
                        dve.wait_ge(logw_ready, i - SPR + 1)
                        dve.wait_ge(suf_ready, i - SPR + 1)
                    nc.vector.tensor_scalar(spb[0:s["nk"], i % SPR, 0:s["n"]], bank[2 + i % ZR][0:s["nk"], 0:s["n"]],
                                            Z_CAP, None, ALU.min).then_inc(cap_ready, 1)
                m = i - 1
                if m >= 0:
                    s = STEPS[m]
                    dve.wait_ge(ln_ready, m + 1)
                    v = spb[0:s["nk"], m % SPR, 0:s["n"]]
                    nc.vector.tensor_tensor(v, bank[2 + m % ZR][0:s["nk"], 0:s["n"]], v, ALU.max)\
                        .then_inc(sp_ready, 1)

            jobs = [(t, h) for t in range(NT) for h in range(NH)]

            def normalize(m):
                r, w = ROWS[jobs[m][0]], KEYS[jobs[m][0]]
                dve.wait_ge(p_ready, m + 1)
                link(nc.vector.reciprocal(rsum[0:r, m % 3:m % 3 + 1], rsum[0:r, m % 3:m % 3 + 1]))
                nc.vector.tensor_scalar(pb[0:r, m % 3, 0:w], pb[0:r, m % 3, 0:w], rsum[0:r, m % 3:m % 3 + 1], None,
                                        ALU.mult).then_inc(pn_ready, 1)

            for i, (t, h) in enumerate(jobs):
                r, w = ROWS[t], KEYS[t]
                dve.wait_ge(lg_ready, i + 1)
                if i >= 2:
                    dve.wait_ge(p_ready, i - 1)
                pr = pairs[i % 2]
                if t < NT - 1:
                    src, bias, dst = pr[0:r, 0:w], SC[t][0:r, :], Lb[0:r, i % 2, 0:w]
                else:
                    src = pr[0:r, :].rearrange("p (b c) -> p b c", b=2)[:, :, 0:272]
                    bias = SC[t][0:r, :].rearrange("p (b c) -> p b c", b=2)
                    dst = Lb[0:r, i % 2, 0:w].rearrange("p (b c) -> p b c", b=2)
                link(nc.vector.tensor_tensor_reduce(out=dst, in0=src, in1=bias, scale=1.0, scalar=HIDDEN,
                                                    op0=ALU.add, op1=ALU.max, accum_out=mx[0:r, i % 2:i % 2 + 1]))
                link(nc.vector.tensor_scalar(nbias[0:r, i % 2:i % 2 + 1], mx[0:r, i % 2:i % 2 + 1], -HD ** -0.5, None,
                                             ALU.mult))
                nc.vector.sem_inc(lb_ready, 1)
                if i >= 1:
                    normalize(i - 1)
            normalize(len(jobs) - 1)

            for j in range(16):
                cb, g = j // 2, j % 2
                lo, hi = FG[g]
                n = J_A + j
                dve.wait_ge(pj_ready, n + 1)
                dve.wait_ge(gate_ready, j + 1)
                link(nc.vector.tensor_tensor(merged[:, cb, lo:hi], bank[n % 4][:, 0:hi - lo], merged[:, cb, lo:hi],
                                             ALU.mult))
                nc.vector.sem_inc(pj_free_dve, 1)
            for j in range(16):
                cb, g = j // 2, j % 2
                lo, hi = FG[g]
                n = J_GB + 2 * j + 1
                dve.wait_ge(pj_ready, n + 1)
                dve.wait_ge(gate_ready, 17 + j)
                gt = tabs[:, (j % 2) * 280:(j % 2) * 280 + hi - lo]
                link(nc.vector.tensor_tensor(gt, bank[n % 4][:, 0:hi - lo], gt, ALU.mult))
                nc.vector.sem_inc(pj_free_dve, 1)
                link(nc.vector.tensor_tensor(merged[:, cb, lo:hi], merged[:, cb, lo:hi], gt, ALU.add))
                nc.vector.sem_inc(half_merged, 1)
                nc.vector.sem_inc(merged_ready, 1)
            def second_norm(t):
                r = ROWS[t]
                if t >= 2:
                    dve.wait_ge(x2_stored[t - 2], 16)
                    dve.wait_ge(tr_ready, T_X2 + 2 * (t - 2) + 2)
                dve.wait_ge(rstd2_ready, t + 1)
                nc.vector.scalar_tensor_tensor(x2row[0:r, t % 2, :], X[0:r, t, :], rstd[0:r, t:t + 1], g2b[0:r, :],
                                               ALU.mult, ALU.mult).then_inc(x2_ready, 1)

            dve.wait_ge(xres_in, 16 * (NT + 2))
            dve.wait_ge(g2_in, 16)
            for t in range(NT + 1):
                if t < NT:
                    r = ROWS[t]
                    for c in range(2):
                        n = J_WO + 2 * t + c
                        dve.wait_ge(pj_ready, n + 1)
                        v = X[0:r, t, 512 * c:512 * (c + 1)]
                        link(nc.vector.tensor_tensor(v, bank[n % 4][0:r, :], v, ALU.add))
                        nc.vector.sem_inc(pj_free_dve, 1)
                    nc.vector.sem_inc(h_ready, 1)
                if t:
                    second_norm(t - 1)

            dve.wait_ge(logits_ready, 1)
            def per_row(v, n):
                return v.rearrange("p (t o) -> p t o", o=1).broadcast_to([P, NT, n])

            def tt(o, x, y, op):
                link(nc.vector.tensor_tensor(o, x, y, op))

            def ts(o, x, c1, c2, op0, op1=None):
                if op1 is None:
                    link(nc.vector.tensor_scalar(o, x, c1, None, op0))
                else:
                    link(nc.vector.tensor_scalar(o, x, c1, c2, op0, op1))

            def red(o, x, op):
                link(nc.vector.tensor_reduce(o, x, AX.X, op))

            g = rl[:, :, 0:NG]
            d = gx[:, 0:NG * NT].rearrange("p (t g) -> p t g", t=NT)
            red(v_max, g, ALU.max)
            tt(d, g, per_row(v_max, NG), ALU.subtract)
            nc.vector.sem_inc(rvals_ready, 1)
            tt(g_eq, g, per_row(v_max, NG), ALU.is_equal)
            ts(v_rest, v_max, 0.0, 1.0, ALU.mult, ALU.add)
            for k in range(NG):
                if k:
                    tt(v_rest, v_rest, g_eq[:, :, k - 1], ALU.subtract)
                tt(g_eq[:, :, k], g_eq[:, :, k], v_rest, ALU.mult)
            for k in range(NG):
                el = rl[:, :, NG + EPG * k:NG + EPG * (k + 1)]
                tt(elm if k else elg, el, g_eq[:, :, k:k + 1].broadcast_to([P, NT, EPG]), ALU.mult)
                if k:
                    tt(elg, elg, elm, ALU.add)
            ts(v_base, g_eq[:, :, 1], float(EPG), None, ALU.mult)
            for k in range(2, NG):
                link(nc.vector.scalar_tensor_tensor(v_base, g_eq[:, :, k], float(EPG * k), v_base, ALU.mult, ALU.add))
            dve.wait_ge(rexp_ready, 1)
            red(v_gp, d, ALU.add)
            link(nc.vector.reciprocal(v_gp, v_gp))
            iota8 = iota[:, 0:EPG].rearrange("p (o e) -> p o e", o=1).broadcast_to([P, NT, EPG])
            for c in range(2):
                red(v_top[c], elg, ALU.max)
                tt(elm, elg, per_row(v_top[c], EPG), ALU.is_equal)
                ts(elx, iota8, -100.0, None, ALU.add)
                tt(elx, elx, elm, ALU.mult)
                red(v_e[c], elx, ALU.min)
                ts(v_e[c], v_e[c], 100.0, None, ALU.add)
                if c == 0:
                    tt(elm, iota8, per_row(v_e[c], EPG), ALU.is_equal)
                    link(nc.vector.scalar_tensor_tensor(elg, elm, -BIG, elg, ALU.mult, ALU.add))
                tt(v_e[c], v_e[c], v_base, ALU.add)
            ex = gx[:, 40:40 + NT]
            tt(ex, v_top[1], v_top[0], ALU.subtract)
            nc.vector.sem_inc(rvals_ready, 1)
            iota32 = iota[:, 0:NE].rearrange("p (o e) -> p o e", o=1).broadcast_to([P, NT, NE])
            for c in range(2):
                tt(oh[c], iota32, per_row(v_e[c], NE), ALU.is_equal)
                tt(oh[c], oh[c], per_row(valid, NE), ALU.mult)
            W = NT * NE
            M = rt[:, 0:W].rearrange("p (t e) -> p t e", t=NT)
            tt(M, oh[0], oh[1], ALU.add)
            link(nc.vector.memset(earlier[:, 0:NE], 0.0))
            for t in range(NT):
                tt(earlier[:, NE * (t + 1):NE * (t + 2)], earlier[:, NE * t:NE * (t + 1)], rt[:, NE * t:NE * (t + 1)],
                   ALU.subtract)
            nc.vector.sem_inc(onehot_ready, 1)
            dve.wait_ge(rexp_ready, 2)
            ts(ew[0], ex, 1.0, None, ALU.add)
            link(nc.vector.reciprocal(ew[0], ew[0]))
            tt(ew[0], ew[0], v_gp, ALU.mult)
            tt(ew[1], ew[0], ex, ALU.mult)
            pos = rt[:, 2 * W:3 * W].rearrange("p (t e) -> p t e", t=NT)
            cnt = rt[:, 3 * W:3 * W + NE]
            blocks = rt[:, 3 * W + NE:3 * W + 2 * NE]
            upto = rt[:, 3 * W + 2 * NE:3 * W + 3 * NE]
            before = rt[:, 3 * W + 3 * NE:3 * W + 4 * NE]
            ones = rt[:, 3 * W + 4 * NE:3 * W + 5 * NE]
            cmp = tabs[:, 0:8 * NE].rearrange("p (e k) -> p e k", k=8)
            dve.wait_ge(pos_ready, 1)
            link(nc.vector.tensor_copy(rt[:, 2 * W:3 * W + NE], bank[0][:, 0:W + NE]))
            tt(cmp, cnt.rearrange("p (e o) -> p e o", o=1).broadcast_to([P, NE, 8]),
               thr.rearrange("p (o k) -> p o k", o=1).broadcast_to([P, NE, 8]), ALU.is_gt)
            red(blocks, cmp, ALU.add)
            link(nc.vector.memset(ones, 1.0))
            link(nc.vector.tensor_tensor_scan(upto, ones, blocks, 0.0, ALU.mult, ALU.add))
            tt(before, upto, blocks, ALU.subtract)
            for c in range(2):
                tmp = tabs[:, 0:W].rearrange("p (t e) -> p t e", t=NT)
                tt(tmp, oh[c], pos, ALU.mult)
                red(v_p, tmp, ALU.add)
                tt(tmp, oh[c], before.rearrange("p (o e) -> p o e", o=1).broadcast_to([P, NT, NE]), ALU.mult)
                red(v_o, tmp, ALU.add)
                tt(v_o, v_o, v_e[c], ALU.subtract)
                ts(v_o, v_o, float(CAP), float(NE * CAP - CAP), ALU.mult, ALU.add)
                ts(v_rest, v_p, float(CAP), None, ALU.is_ge)
                tt(v_o, v_o, v_rest, ALU.mult)
                tt(v_o, v_o, v_p, ALU.add)
                link(nc.vector.scalar_tensor_tensor(v_o, v_e[c], float(CAP), v_o, ALU.mult, ALU.add))
                link(nc.vector.tensor_copy(slot_i[c][:, :], v_o))
                for op, arg, dst, n in ((ALU.bitwise_and, CAP - 1, at_slot[c], CAP),
                                        (ALU.logical_shift_right, CAP.bit_length() - 1, at_block[c], NBLK)):
                    link(nc.vector.tensor_scalar(slot_part[0][:, :], slot_i[c][:, :], arg, None, op))
                    link(nc.vector.tensor_copy(v_rest, slot_part[0][:, :]))
                    tt(dst, iota[:, 0:n].rearrange("p (o e) -> p o e", o=1).broadcast_to([P, NT, n]),
                       per_row(v_rest, n), ALU.is_equal)
                tt(at_slot[c], at_slot[c], per_row(rid, CAP), ALU.mult)
            m17 = tabs[0:1, 0:MAX_OVER * NE].rearrange("p (b e) -> p b e", b=MAX_OVER)
            tt(m17, upto[0:1].rearrange("p (o e) -> p o e", o=1).broadcast_to([1, MAX_OVER, NE]),
               iota[0:1, 0:MAX_OVER].rearrange("p (b o) -> p b o", o=1).broadcast_to([1, MAX_OVER, NE]), ALU.is_le)
            o17 = tabs[0:1, 600:600 + MAX_OVER]
            red(o17, m17, ALU.add)
            ts(o17, o17, float(NE - 1), None, ALU.min)
            link(nc.vector.tensor_copy(over_i[0:1, 0:MAX_OVER], o17))
            link(nc.vector.tensor_copy(over_i[0:1, MAX_OVER:MAX_OVER + 1], upto[0:1, NE - 1:NE]))
            nc.vector.sem_inc(slots_ready, 1)
            dve.wait_ge(idx_ready, 1)
            nc.vector.tensor_copy(idxs[:, :], bank[1][0:CAP, 0:NBLK]).then_inc(idx_in, 1)

            def hidden(q, done):
                nc.vector.tensor_tensor(hid[:, q, :], sil[:, q, :], bank[4 * q + 1][:, P:2 * P], ALU.mult)\
                    .then_inc(done, 1)

            def copy_hidden(q, done):
                nc.vector.tensor_copy(hidT[:, q, :], bank[4 * q + 2][:, 0:P]).then_inc(done, 1)

            with dve.Fori(0, NE // 4) as i:
                for s in range(4):
                    q = s % 2
                    dve.wait_ge(silu_ready, i * 4 + s + 1)
                    hidden(q, hid_ready)
                    dve.wait_ge(hT_ready, i * 4 + s + 1)
                    copy_hidden(q, hidT_ready)
            over = dve.value_load(over_i[0:1, MAX_OVER:MAX_OVER + 1], min_val=0, max_val=MAX_OVER)
            with dve.If(over > 0):
                with dve.Fori(0, MAX_OVER) as b:
                    dve.wait_ge(o_step, b * 10 + 4)
                    hidden(0, o_step)
                    dve.wait_ge(o_step, b * 10 + 6)
                    copy_hidden(0, o_step)
            for t in range(NT):
                r = ROWS[t]
                for c in range(2):
                    n = 2 * t + c
                    dve.wait_ge(comb_in[n], 16)
                    link(nc.vector.scalar_tensor_tensor(X[0:r, t, :], arena[0:r, n * D:(n + 1) * D],
                                                        ew[c][0:r, t:t + 1], X[0:r, t, :], ALU.mult, ALU.add))
                nc.vector.sem_inc(final_ready, 1)


_SHAPES = {
    "y_prompt": [SEQ, D], "y_sample": [DEC, D],
    "sk_p": [N_PROMPT, 512], "sv_p": [N_PROMPT, 512], "dk_p": [N_PROMPT, 2, HD], "dv_p": [N_PROMPT, 128],
    "ik_p": [N_PROMPT, HD],
    "sk_s": [DEC, 512], "sv_s": [DEC, 512], "dk_s": [DEC, 2, HD], "dv_s": [DEC, 128], "ik_s": [DEC, HD],
}
_RETURNED = [
    (1, SEQ, D), (1, DEC, D),
    (1, 1, N_PROMPT, NH, HD), (1, 1, N_PROMPT, NH, HD), (1, 1, N_PROMPT, 2, HD), (1, 1, N_PROMPT, 2, HD),
    (1, 1, N_PROMPT, HD),
    (1, 1, DEC, NH, HD), (1, 1, DEC, NH, HD), (1, 1, DEC, 2, HD), (1, 1, DEC, 2, HD), (1, 1, DEC, HD),
]


def kernel(**inputs):
    import numpy as _np
    import concourse.bacc as _bacc
    from concourse import mybir as _mybir
    from concourse.bass_utils import run_bass_kernel_spmd as _run

    shapes = {
        "x_prompt": (SEQ, D), "x_sample": (DEC, D), "cache_sb_k": (PAST, 512), "cache_sb_v": (PAST, 512),
        "cache_dsa_k": (PAST, 2, HD), "cache_dsa_v": (PAST, 128), "cache_idx_k": (PAST, HD),
        "meta_tokens": (N_META, D), "norm1_g": (D,), "w_in": (D, 4936), "dsa_q_norm_g": (HD,),
        "dsa_k_norm_g": (HD,), "w_sb_branch": (512, D), "w_dsa_branch": (512, D), "w_out": (D, D),
        "norm2_g": (D,), "w_group": (D, NG), "w_router": (D, NE), "w_gate": (NE, D, FE), "w_up": (NE, D, FE),
        "w_down": (NE, FE, D),
    }
    nc = _bacc.Bacc("TRN2", target_bir_lowering=False, num_devices=1)
    arrays = {n: _np.ascontiguousarray(inputs[n]).reshape(s) for n, s in shapes.items()}
    arrays["consts"] = constants()
    arrays = {f"in_{n}": v for n, v in arrays.items()}
    args = {n[3:]: nc.dram_tensor(n, v.shape, _mybir.dt.from_np(v.dtype), kind="ExternalInput").ap()
            for n, v in arrays.items()}
    outs = {n: nc.dram_tensor(f"out_{n}", s, _mybir.dt.float32, kind="ExternalOutput").ap()
            for n, s in _SHAPES.items()}
    build(nc, args, outs)
    r = _run(nc, [arrays], core_ids=[0])
    return tuple(r.results[0][f"out_{n}"].reshape(s) for n, s in zip(_SHAPES, _RETURNED))
```

```python
from contextlib import ExitStack

import numpy as np

import concourse.bass as bass
from concourse import mybir

F32 = mybir.dt.float32
I32 = mybir.dt.int32
ACT = mybir.ActivationFunctionType
ALU = mybir.AluOpType
AX = mybir.AxisListType

P = 128
D = 1024
KT = D // P
HD = 64
HALF = HD // 2
NH = 8
NPAIR = NH // 2
N_META, SEQ, DEC, PAST, CHUNK = 16, 512, 32, 512, 64
N_PROMPT = N_META + SEQ
N_ROWS = N_PROMPT + DEC
OFF = [0, 80, 208, 336, 464]
ROWS = [80, 128, 128, 128, 96]
NT = len(OFF)
KEYS = [80, 208, 336, 464, PAST + DEC]
KEY_ROWS = [80, 128, 128, 128, 64]
NCB = PAST // P
SEL_PROMPT = min(256, SEQ // 4)
SEL_SAMPLE = min(256, (PAST + DEC) // 4)
EPS = 1e-6
NG, EPG, NE, FE = 4, 8, 32, 256
CAP = 64
MS = 6
ROUNDS = -(-NE // MS)
MAX_OVER = (2 * N_ROWS) // CAP
NBLK = NE + MAX_OVER
N_SLOTS = NBLK * CAP
BIG = 1.0e30
HIDDEN = float(np.float32(-3.0e38))
Z_CAP = 30.0
TAKEN = float(np.float32(-3.2e38))

C_SQ, C_SK, C_SV, C_DQ, C_DK, C_IQ, C_IK, C_GSB, C_GDSA = 0, 512, 1024, 1536, 2048, 2304, 2816, 2888, 3912
N_SMALL1, N_SMALL2 = 72, 256

K_ID, K_NTRI, K_NONE, K_STRI, K_COS, K_SIN, K_IOTA, K_THR, K_VALID, K_RID = (
    0, 128, 256, 384, 512, 832, 1152, 1216, 1224, 1229)
K_COLS = 1234


def constants():
    c = np.zeros((P, K_COLS), np.float32)
    i = np.arange(P)
    c[:, K_ID:K_ID + P] = np.eye(P)
    c[:, K_NTRI:K_NTRI + P] = -(i[:, None] >= i[None, :]).astype(np.float32)
    c[:, K_NONE:K_NONE + P] = -1.0
    c[:, K_STRI:K_STRI + P] = (i[:, None] < i[None, :])
    freqs = (10000.0 ** (-np.arange(HALF) / HALF)).astype(np.float32)
    for t in range(NT):
        pos = OFF[t] + i
        if t == NT - 1:
            pos = np.where(i < 64, pos, PAST + i - 64)
        ang = (pos.astype(np.float32)[:, None] * freqs[None, :].astype(np.float32)).astype(np.float64)
        c[:, K_COS + t * HD:K_COS + (t + 1) * HD] = np.concatenate([np.cos(ang), np.cos(ang)], 1)
        c[:, K_SIN + t * HD:K_SIN + (t + 1) * HD] = np.concatenate([-np.sin(ang), np.sin(ang)], 1)
        c[:ROWS[t], K_VALID + t] = 1.0
        c[:ROWS[t], K_RID + t] = OFF[t] + i[:ROWS[t]]
    c[:, K_IOTA:K_IOTA + CAP] = np.arange(CAP)
    c[:, K_THR:K_THR + 8] = CAP * (1 + np.arange(8))
    return c


def row_pieces(t):
    if t == 0:
        return [(0, N_META, "meta", 0), (N_META, ROWS[0], "prompt", 0)]
    if t == NT - 1:
        return [(0, 64, "prompt", OFF[t] - N_META), (64, 96, "sample", 0)]
    return [(0, P, "prompt", OFF[t] - N_META)]


GROUPS = [(208, N_PROMPT, [4, 3, 2, 1, 0]), (0, 208, [1, 0])]


def sb_steps():
    steps = []
    sample = [dict(kind="sample", half=half, j=j, n=NPAIR * DEC, nk=DEC if j == NCB else P, diag=j == NCB,
                   first=j == NCB, last=j == 0, stream=4 + half, acc=2 * NPAIR + 2, bank=7)
              for j in range(NCB, -1, -1) for half in range(2)]
    for pair in range(NPAIR):
        by_group = [[], []]
        for g, (lo, hi, blocks) in enumerate(GROUPS):
            for n, j in enumerate(blocks):
                for half in range(2):
                    q0 = max(OFF[j], lo)
                    by_group[g].append(dict(kind="prompt", pair=pair, g=g, half=half, j=j, lo=lo, hi=hi, q0=q0,
                                            n=hi - q0, nk=KEY_ROWS[j], diag=OFF[j] >= lo, first=n == 0,
                                            last=n == len(blocks) - 1, stream=2 * (g % 2) + half,
                                            cover0=max(OFF[blocks[n - 1]], lo) if n else hi,
                                            acc=2 * pair + g, bank=g))
        many, few = by_group
        steps += sample[2 * pair:2 * pair + 2] if pair else []
        steps += many[:6] + few[:2] + many[6:8] + few[2:] + (sample[:2] if not pair else []) + many[8:]
        steps += sample[8:] if pair == NPAIR - 2 else []
    for i, s in enumerate(steps):
        s["prev"] = max([k for k in range(i) if steps[k]["stream"] == s["stream"]], default=None)
        s["closes"] = all(t["acc"] != s["acc"] for t in steps[i + 1:])
    for i, s in enumerate(steps):
        s["bank_free"] = max([sum(t["closes"] for t in steps[:k + 1]) for k in range(i)
                              if steps[k]["closes"] and steps[k]["acc"] == s["acc"] - 2], default=0)
    return steps


STEPS = sb_steps()
NSTEP = len(STEPS)
ZR, SPR, WR = 5, 6, 5
TRI_LAG, PV_LAG = 3, 7
LR, PR, TURN_LAG = 3, 4, 3


def build(nc, a, out):
    ctx = ExitStack()
    with ctx:
        def sem(name):
            return ctx.enter_context(nc.semaphore(name))

        def sems(name, n):
            return [sem(f"{name}{i}") for i in range(n)]

        def sb(name, cols, dt=F32, rows=P):
            return ctx.enter_context(nc.sbuf_tensor(name, [rows, cols], dt))

        SLOT = 3 * 2048
        arena = sb("arena", 4 * SLOT + KT * N_ROWS)
        xnT = sb("xnT", KT * N_ROWS)
        ring_w = sb("ring_w", 2 * 4096)
        hreg = sb("hreg", NT * D)
        cst = sb("cst", K_COLS)
        g1 = sb("g1", KT)
        gqk = sb("gqk", 4 * HD)
        tabs = sb("tabs", 4 * NT * HD)
        small = sb("small", 1400)

        at = [0]

        def carve(cols):
            s = arena[:, at[0]:at[0] + cols]
            at[0] += cols
            assert at[0] <= 4 * SLOT + KT * N_ROWS, at[0]
            return s

        sqT = carve(NPAIR * N_ROWS).rearrange("p (b r) -> p b r", b=NPAIR)
        skT = carve(NPAIR * N_ROWS).rearrange("p (b r) -> p b r", b=NPAIR)
        ksT = carve(NPAIR * PAST).rearrange("p (b r) -> p b r", b=NPAIR)
        svP = carve(NT * 512).rearrange("p (t c) -> p t c", t=NT)
        svC = carve(NCB * 512).rearrange("p (t c) -> p t c", t=NCB)
        svN = carve(512)
        dqT = carve(NPAIR * N_ROWS).rearrange("p (b r) -> p b r", b=NPAIR)
        dkiT = carve(3 * N_ROWS).rearrange("p (b r) -> p b r", b=3)
        dkiC = carve(3 * PAST).rearrange("p (b r) -> p b r", b=3)
        dvP = carve(NT * 128).rearrange("p (t c) -> p t c", t=NT)
        dvC = carve(NCB * 128).rearrange("p (t c) -> p t c", t=NCB)
        dvN = carve(128)
        sc0 = at[0]
        SC = [carve(k) for k in KEYS]
        natD = arena[:, sc0:sc0 + NCB * 384].rearrange("p (t b u c) -> p t b u c", t=NCB, b=3, u=2)
        rb = carve(2 * 512).rearrange("p (i c) -> p i c", i=2)
        mark = at[0]
        ropeA = carve(2 * 512).rearrange("p (i c) -> p i c", i=2)
        ropeB = carve(2 * 512).rearrange("p (i c) -> p i c", i=2)
        ropeQ = carve(2 * 512).rearrange("p (i c) -> p i c", i=2)
        kd = carve(NT * 384).rearrange("p (t b u c) -> p t b u c", t=NT, b=3, u=2)
        natS = carve(NCB * 512).rearrange("p (t c) -> p t c", t=NCB)
        skR = natS
        skR4 = carve(512)
        at[0] = mark
        spb = carve(SPR * 320).rearrange("p (i c) -> p i c", i=SPR)
        wtb = carve(WR * 320).rearrange("p (i c) -> p i c", i=WR)
        sufb = carve(6 * 320).rearrange("p (i c) -> p i c", i=6)
        at[0] = mark
        Lb = carve(LR * 544).rearrange("p (i c) -> p i c", i=LR)
        pb = carve(PR * 544).rearrange("p (i c) -> p i c", i=PR)
        pTb = carve(8 * 512).rearrange("p (i c) -> p i c", i=8)
        merged = arena[:, 4 * SLOT:].rearrange("p (k r) -> p k r", k=KT)
        xT = xnT[:, :].rearrange("p (k r) -> p k r", k=KT)
        X = hreg[:, :].rearrange("p (t d) -> p t d", t=NT)
        osbT = hreg[:, 0:NPAIR * N_ROWS].rearrange("p (b r) -> p b r", b=NPAIR)
        odsaT = hreg[:, NPAIR * N_ROWS:2 * NPAIR * N_ROWS].rearrange("p (b r) -> p b r", b=NPAIR)
        zeros = hreg[:, 2 * NPAIR * N_ROWS:2 * NPAIR * N_ROWS + 512]
        iqT = odsaT
        wslot = [ring_w[:, s * 4096:(s + 1) * 4096] for s in range(2)]
        moe_w = [arena[:, s * SLOT:(s + 1) * SLOT] for s in (0, 2, 3, 1)]
        Xg = ring_w[0:CAP, 0:2 * D].rearrange("p (i d) -> p i d", i=2)
        Yb = ring_w[:, 2 * D:3 * D].rearrange("p (i d) -> p i d", i=2)
        xgT = ring_w[:, 3 * D:4 * D].rearrange("p (i k s) -> p i k s", i=2, k=KT)
        moe_gu = [w[:, 0:4096] for w in moe_w] + [arena[:, 4 * SLOT:4 * SLOT + 4096], xnT[:, 0:4096]]
        moe_dn = [[w[:, 4096 + D * j:4096 + D * (j + 1)] for j in range(2)] for w in moe_w]
        moe_dn += [[ring_w[:, (6 + j) * D:(7 + j) * D] for j in range(2)], [ring_w[:, 5 * D:6 * D], tabs[:, 0:D]]]
        hid = ring_w[:, 4 * D:4 * D + 256].rearrange("p (i c) -> p i c", i=2)
        sil = ring_w[:, 4 * D + 256:4 * D + 512].rearrange("p (i c) -> p i c", i=2)
        hidT = ring_w[:, 4 * D + 512:4 * D + 768].rearrange("p (i c) -> p i c", i=2)
        lgT = tabs[:, 640:1200]
        x2row = ring_w[:, 0:2 * D].rearrange("p (i d) -> p i d", i=2)
        g2b = ring_w[:, 2 * D:3 * D]
        scrap = ring_w[:, 3 * D:4 * D]

        so = [0]

        def sm(cols):
            s = small[:, so[0]:so[0] + cols]
            so[0] += cols
            assert so[0] <= 1400
            return s

        ss = sm(NT)
        rstd = sm(NT)
        ssq = sm(2 * NH).rearrange("p (i h) -> p i h", i=2)
        rq = sm(2 * NH).rearrange("p (i h) -> p i h", i=2)
        iws = sm(NT * NH).rearrange("p (t h) -> p t h", t=NT)
        top8 = sm(8)
        mhalf = sm(NH)
        mx = sm(LR)
        nbias = sm(LR)
        rsum = sm(PR)
        wr = sm(KT * 36).rearrange("p (k c) -> p k c", k=KT)
        rl = sm(NT * 36).rearrange("p (t c) -> p t c", t=NT)
        oh = sm(2 * NT * NE).rearrange("p (c t e) -> p c t e", c=2, t=NT)
        gx = sm(64)
        ew = [sm(NT) for _ in range(2)]
        v_max, v_first, v_gp = (sm(NT) for _ in range(3))
        v_top = [sm(NT) for _ in range(2)]
        v_slot = sm(2 * NT)
        g_eq = sm(NT * NG).rearrange("p (t g) -> p t g", t=NT)
        at_slot = ring_w[:, 0:2 * NT * CAP].rearrange("p (c s) -> p c s", s=CAP)
        at_block = ring_w[:, 640:640 + 2 * NT * NBLK].rearrange("p (c b) -> p c b", b=NBLK)
        rt = sb("rt", 3 * (NT + 1) * NE + 5 * NE)
        marks, earlier, go_on = (rt[:, i * (NT + 1) * NE:(i + 1) * (NT + 1) * NE].rearrange("p (e t) -> p e t", e=NE)
                                 for i in range(3))
        blocks, upto, over_base, by_cap, ones = (
            rt[:, 3 * (NT + 1) * NE + i * NE:3 * (NT + 1) * NE + (i + 1) * NE] for i in range(5))
        slot_part = [sb(f"slot_part{c}", 2 * NT, I32) for c in range(2)]
        slot_i = sb("slot_i", 2 * NT, I32)
        idxs = sb("idxs", NBLK, I32, CAP)
        idx_now = sb("idx_now", 2, I32, CAP)
        over_i = sb("over_i", MAX_OVER + 1, I32, 1)

        ident = cst[:, K_ID:K_ID + P]
        ntri = cst[:, K_NTRI:K_NTRI + P]
        nones = cst[:, K_NONE:K_NONE + P]
        stri = cst[:, K_STRI:K_STRI + P]
        cos = cst[:, K_COS:K_COS + NT * HD].rearrange("p (t c) -> p t c", t=NT)
        sin = cst[:, K_SIN:K_SIN + NT * HD].rearrange("p (t c) -> p t c", t=NT)
        iota = cst[:, K_IOTA:K_IOTA + CAP]
        thr = cst[:, K_THR:K_THR + 8]
        valid = cst[:, K_VALID:K_VALID + NT]
        rid = cst[:, K_RID:K_RID + NT]
        tab = tabs[:, :].rearrange("p (w t c) -> p w t c", w=4, t=NT)

        pair01 = ctx.enter_context(nc.psum_tensor("pair01", [P, 1024], F32))
        pair23 = ctx.enter_context(nc.psum_tensor("pair23", [P, 1024], F32))
        pair45 = ctx.enter_context(nc.psum_tensor("pair45", [P, 1024], F32))
        pair67 = ctx.enter_context(nc.psum_tensor("pair67", [P, 1024], F32))
        pairs = [pair01, pair23, pair45, pair67]
        bank = [p[:, s * 512:(s + 1) * 512] for p in pairs for s in range(2)]

        xn2_d = nc.dram_tensor("xn2_d", [N_ROWS, D], F32).ap()
        y_d = nc.dram_tensor("y_d", [N_SLOTS, D], F32).ap()

        ident_in = sem("ident_in")
        const_in = sem("const_in")
        g1_in = sem("g1_in")
        gains_in = sem("gains_in")
        x_in = sems("x_in", NT)
        cache_k_in = sem("cache_k_in")
        cache_v_in = sem("cache_v_in")
        chunk_in = sems("chunk_in", 14)
        ss_ready = sem("ss_ready")
        rstd_ready = sem("rstd_ready")
        rstd2_ready = sem("rstd2_ready")
        xs_ready = sem("xs_ready")
        tr_ready = sem("tr_ready")
        tr_free_act = sem("tr_free_act")
        tr_free_dve = sem("tr_free_dve")
        pj_ready = sem("pj_ready")
        pj_free_act = sem("pj_free_act")
        pj_free_dve = sem("pj_free_dve")
        tables_ready = sem("tables_ready")
        rope_parts = sem("rope_parts")
        squares = sem("squares")
        rows_ready = sem("rows_ready")
        ix_ready = sem("ix_ready")
        relu_ready = sem("relu_ready")
        relu_used = sem("relu_used")
        vnew_in = sem("vnew_in")
        keys_out = sem("keys_out")
        sk_rows = sem("sk_rows")
        sv_rows = sem("sv_rows")
        small_rows = sem("small_rows")
        z_ready = sem("z_ready")
        cap_ready = sem("cap_ready")
        ln_ready = sem("ln_ready")
        sp_ready = sem("sp_ready")
        sp_masked = sem("sp_masked")
        suf_ready = sem("suf_ready")
        logw_ready = sem("logw_ready")
        w_ready = sem("w_ready")
        w_masked = sem("w_masked")
        pv_done = sem("pv_done")
        acc_free = sem("acc_free")
        lg_ready = sem("lg_ready")
        lb_ready = sem("lb_ready")
        p_ready = sem("p_ready")
        pT_ready = sem("pT_ready")
        pT_copied = sem("pT_copied")
        pn_ready = sem("pn_ready")
        oT_copied = sem("oT_copied")
        pvd_done = sem("pvd_done")
        gate_ready = sem("gate_ready")
        half_merged = sem("half_merged")
        merged_ready = sem("merged_ready")
        xres_in = sem("xres_in")
        wr_in = sem("wr_in")
        g2_in = sem("g2_in")
        h_ready = sem("h_ready")
        ss2_ready = sem("ss2_ready")
        x2_ready = sem("x2_ready")
        x2_stored = sems("x2_stored", NT)
        logits_ready = sem("logits_ready")
        rexp_ready = sem("rexp_ready")
        rvals_ready = sem("rvals_ready")
        onehot_ready = sem("onehot_ready")
        pos_ready = sem("pos_ready")
        slots_ready = sem("slots_ready")
        idx_ready = sem("idx_ready")
        idx_in = sem("idx_in")
        mw_in = sems("mw_in", MS)
        idx_now_ready = sem("idx_now_ready")
        gath = sems("gath", 2)
        xgp_ready = sems("xgp_ready", 2)
        xgT_ready = sems("xgT_ready", 2)
        gu_ready = sem("gu_ready")
        silu_ready = sem("silu_ready")
        hid_ready = sem("hid_ready")
        hT_ready = sem("hT_ready")
        hidT_ready = sem("hidT_ready")
        y_done = sems("y_done", MS)
        y_copied = sems("y_copied", 2)
        y_out = sems("y_out", 2)
        o_w = sem("o_w")
        o_idx = sem("o_idx")
        o_g = sem("o_g")
        o_step = sem("o_step")
        comb_in = sems("comb_in", 2 * NT)
        results_out = sem("results_out")
        final_ready = sem("final_ready")
        y_final_out = sem("y_final_out")
        pe_turns = sem("pe_turns")
        pool_turns = sem("pool_turns")
        zero_ready = sem("zero_ready")
        y_zeroed = sem("y_zeroed")
        act_chain = sem("act_chain")
        dve_chain = sem("dve_chain")
        pool_chain = sem("pool_chain")

        slots = [0, 1, 0, 1, 0, 1, 0, 1, 0, 2, 1, 0, 1, 3]
        chunk_at = [moe_w[s][:, 0:4096] if s >= 2 else wslot[s] for s in slots]

        used_at = [5, 10, 15, 20, 28, 36, 44, 52, 68, 100, 84, 100, 110, 110]

        def free_before(n):
            return max([used_at[m] for m in range(n) if slots[m] == slots[n]], default=0)

        win = a["w_in"].rearrange("(p k) c -> p k c", k=KT)

        def load_chunk(eng, n):
            if free_before(n):
                eng.wait_ge(pj_ready, free_before(n))
            v = chunk_at[n]
            if n == 1:
                v = v[:, 0:KT * 328].rearrange("p (k c) -> p k c", k=KT)
                eng.dma_start(v[:, :, 0:N_SMALL1], win[:, :, C_IK:C_IK + N_SMALL1]).then_inc(chunk_in[n], 16)
                eng.dma_start(v[:, :, N_SMALL1:328], win[:, :, C_DK:C_DK + N_SMALL2]).then_inc(chunk_in[n], 16)
                return
            v8 = v.rearrange("p (k c) -> p k c", k=KT)
            col = {0: C_IQ, 2: C_DQ, 3: C_SV, 4: C_SK, 5: C_SQ, 6: C_GSB, 7: C_GSB + 512,
                   10: C_GDSA, 11: C_GDSA + 512}
            if n in col:
                src, v = win[:, :, col[n]:col[n] + 512], v8
            elif n == 8:
                src = a["w_sb_branch"].rearrange("(k p) c -> p k c", p=P)
                v = v.rearrange("p (k c) -> p k c", k=4)
            elif n == 9:
                v = v.rearrange("p (k c) -> p k c", k=4)
                for kv in range(2):
                    src = a["w_dsa_branch"][256 * kv:256 * (kv + 1), :].rearrange("(k p) c -> p k c", p=64)
                    eng.dma_start(v[64 * kv:64 * (kv + 1)], src).then_inc(chunk_in[n], 16)
                return
            else:
                src = a["w_out"].rearrange("(k p) c -> p k c", p=P)[:, :, (n - 12) * 512:(n - 11) * 512]
                v = v8
            eng.dma_start(v, src).then_inc(chunk_in[n], 16)

        def chunk_arrived(eng, n):
            eng.wait_ge(chunk_in[n], 32 if n in (1, 9) else 16)

        PJ = (["dve"] * 15 + ["act"] * (NT + 16) + ["act"] * 16 + ["dve"] * 16 + ["act", "dve"] * 16
              + ["dve"] * 10 + ["act"] * 2)
        J_IQ, J_SM, J_DQ, J_SV, J_SK, J_SQ = 0, 5, 10, 15, 20, 28
        J_GSB, J_A, J_GB, J_WO, J_RT = 36, 52, 68, 100, 110
        TR = ["dve"] * 10 + ["act"] * 8 + ["act"] * 20 + ["act"] * 11
        T_X, T_IQ, T_C, T_SM, T_DQ, T_SK, T_X2 = 0, 10, 14, 23, 28, 33, 38

        def emptied(order, who, n):
            return sum(w == who for w in order[:n + 1])

        def pj_wait_free(eng, n):
            if n >= 4:
                who = PJ[n - 4]
                eng.wait_ge(pj_free_act if who == "act" else pj_free_dve, emptied(PJ, who, n - 4))

        def tr_wait_free(eng, n):
            if n >= 2:
                who = TR[n - 2]
                eng.wait_ge(tr_free_act if who == "act" else tr_free_dve, emptied(TR, who, n - 2))

        FG = [(0, 280), (280, 560)]
        RG = [(0, OFF[NT - 1]), (OFF[NT - 1], N_ROWS)]
        IX = []
        for t in range(1, NT):
            for h in range(NH):
                IX += [(t, h, 0, 272), (t, h, 272, 544)] if t == NT - 1 else [(t, h, 0, KEYS[t])]

        block = ctx.enter_context(nc.Block())

        @block.sync
        def _(sp):
            sp.dma_start(X[0:N_META, 0, :], a["meta_tokens"]).then_inc(x_in[0], 16)
            sp.dma_start(X[N_META:ROWS[0], 0, :], a["x_prompt"][0:ROWS[0] - N_META, :]).then_inc(x_in[0], 16)
            sp.dma_start(ident, a["consts"][:, 0:P]).then_inc(ident_in, 16)
            sp.dma_start(g1[:, :], a["norm1_g"].rearrange("(p k) -> p k", k=KT)).then_inc(g1_in, 16)
            for t in range(1, NT):
                for p0, p1, which, r0 in row_pieces(t):
                    sp.dma_start(X[p0:p1, t, :], a["x_" + which][r0:r0 + p1 - p0, :]).then_inc(x_in[t], 16)
            load_chunk(sp, 0)
            sp.dma_start(cst[:, P:], a["consts"][:, P:]).then_inc(const_in, 16)
            for w, name in enumerate(("dsa_q_norm_g", "dsa_k_norm_g")):
                g = a[name].rearrange("(o c) -> o c", o=1)
                q = gqk[:, 2 * w * HD:2 * (w + 1) * HD]
                sp.dma_start(q[:, 0:HD], g.broadcast_to([P, HD])).then_inc(gains_in, 16)
                sp.dma_start(q[:, HD:HD + HALF], g[:, HALF:HD].broadcast_to([P, HALF])).then_inc(gains_in, 16)
                sp.dma_start(q[:, HD + HALF:2 * HD], g[:, 0:HALF].broadcast_to([P, HALF])).then_inc(gains_in, 16)
            sp.dma_start(natS, a["cache_sb_k"].rearrange("(t p) c -> p t c", p=P)).then_inc(cache_k_in, 16)
            for u in range(2):
                for b in range(2):
                    sp.dma_start(natD[:, :, b, u, :],
                                 a["cache_dsa_k"][:, b, :].rearrange("(t p) c -> p t c", p=P)).then_inc(cache_k_in, 16)
                sp.dma_start(natD[:, :, 2, u, :],
                             a["cache_idx_k"].rearrange("(t p) c -> p t c", p=P)).then_inc(cache_k_in, 16)
            load_chunk(sp, 1)
            sp.dma_start(svC, a["cache_sb_v"].rearrange("(t p) c -> p t c", p=P)).then_inc(cache_v_in, 16)
            sp.dma_start(dvC, a["cache_dsa_v"].rearrange("(t p) c -> p t c", p=P)).then_inc(cache_v_in, 16)
            load_chunk(sp, 2)

            def store_rows(src, dst_prompt, dst_sample, t):
                n = KEY_ROWS[t]
                sp.dma_start(dst_prompt[OFF[t]:OFF[t] + n, :], src[0:n]).then_inc(keys_out, 16)
                if t == NT - 1:
                    sp.dma_start(dst_sample[:, :], src[64:96]).then_inc(keys_out, 16)

            load_chunk(sp, 3)
            for t in range(NT):
                sp.wait_ge(small_rows, t + 1)
                for b in range(2):
                    store_rows(kd[:, t, b, 0, :], out["dk_p"][:, b, :], out["dk_s"][:, b, :], t)
                store_rows(kd[:, t, 2, 0, :], out["ik_p"], out["ik_s"], t)
                store_rows(dvP[:, t, :], out["dv_p"], out["dv_s"], t)
            sp.dma_start(dvN[0:DEC, :], dvP[64:96, NT - 1, :]).then_inc(vnew_in, 16)
            load_chunk(sp, 4)
            load_chunk(sp, 5)
            for t in range(NT):
                sp.wait_ge(sv_rows, t + 1)
                store_rows(svP[:, t, :], out["sv_p"], out["sv_s"], t)
            sp.dma_start(svN[0:DEC, :], svP[64:96, NT - 1, :]).then_inc(vnew_in, 16)
            load_chunk(sp, 6)
            for t in range(NT):
                sp.wait_ge(sk_rows, t + 1)
                store_rows(skR4 if t == NT - 1 else skR[:, t, :], out["sk_p"], out["sk_s"], t)
            load_chunk(sp, 7)
            wg = a["w_gate"].rearrange("e (p k) f -> (e p) (k f)", k=KT)
            wu = a["w_up"].rearrange("e (p k) f -> (e p) (k f)", k=KT)
            wd = a["w_down"].rearrange("e (j p) c -> p (e j) c", j=2)

            def load_expert(slot, e, arrived):
                for n, w in enumerate((wg, wu)):
                    sp.dma_start(moe_gu[slot][:, n * 2048:(n + 1) * 2048], w[bass.ds(e * P, P), :])\
                        .then_inc(arrived, 16)
                for j in range(2):
                    if slot == 5 and j:
                        sp.wait_ge(slots_ready, 1)
                    sp.dma_start(moe_dn[slot][j], wd[:, bass.ds(e * 2 + j, 1), :].rearrange("p o c -> p (o c)"))\
                        .then_inc(arrived, 16)

            def load_turn(i, s):
                if s in (2, 3):
                    sp.wait_ge(pj_ready, used_at[{2: 9, 3: 13}[s]])
                if s == 4:
                    sp.wait_ge(pj_ready, used_at[13])
                if s == 5:
                    sp.wait_ge(logits_ready, 1)
                sp.wait_ge(y_done[s], i)
                load_expert(s, i * MS + s, mw_in[s])

            sp.wait_ge(oT_copied, NT)
            sp.wait_ge(acc_free, 2 * NPAIR + 1)
            sp.wait_ge(vnew_in, 32)
            with sp.Fori(0, NE // MS) as i:
                for s in range(MS):
                    load_turn(i, s)
            for s in range(NE % MS):
                load_turn(NE // MS, s)
            over = sp.value_load(over_i[0:1, MAX_OVER:MAX_OVER + 1], min_val=0, max_val=MAX_OVER)
            with sp.If(over > 0):
                sp.wait_ge(y_done[0], ROUNDS)
                with sp.Fori(0, MAX_OVER) as b:
                    sp.wait_ge(o_step, b * 10)
                    e = sp.value_load(over_i[0:1, bass.ds(b, 1)], min_val=0, max_val=NE - 1)
                    load_expert(0, e, o_w)
            for t in range(NT):
                sp.wait_ge(final_ready, t + 1)
                for p0, p1, which, r0 in row_pieces(t):
                    if which != "meta":
                        sp.dma_start(out["y_" + which][r0:r0 + p1 - p0, :], X[p0:p1, t, :]).then_inc(y_final_out, 16)
            sp.wait_ge(y_final_out, 16 * (NT + 1))
            sp.wait_ge(keys_out, 16 * 6 * (NT + 1))

        @block.tensor
        def _(pe):
            tr = [0]
            pj = [0]

            def tr_job(items, n):
                tr_wait_free(pe, tr[0])
                b = bank[4 + tr[0] % 2]
                for i, (src, idn) in enumerate(items):
                    cols = src.shape[1]
                    last = nc.tensor.transpose(b[0:cols, i * n:i * n + src.shape[0]], src, idn)
                last.then_inc(tr_ready, 1)
                tr[0] += 1

            def pj_job(mms, view):
                pj_wait_free(pe, pj[0])
                o = view(bank[pj[0] % 4])
                for i, (l, r) in enumerate(mms):
                    last = nc.tensor.matmul(o, l, r, start=i == 0, stop=i == len(mms) - 1)
                last.then_inc(pj_ready, 1)
                pj[0] += 1

            pe.wait_ge(ident_in, 16)
            for t in range(NT):
                pe.wait_ge(xs_ready, t + 1)
                xk = X[0:ROWS[t], t, :].rearrange("p (c k) -> p k c", k=KT)
                for q in range(2):
                    tr_job([(xk[:, 4 * q + i, :], ident[0:ROWS[t], 0:ROWS[t]]) for i in range(4)], ROWS[t])
            def by_rows(n, t, cols):
                v = chunk_at[n][:, 0:KT * cols].rearrange("p (k c) -> p k c", k=KT)
                pj_job([(xT[:, k, OFF[t]:OFF[t] + ROWS[t]], v[:, k, :]) for k in range(KT)],
                       lambda b: b[0:ROWS[t], 0:cols])

            def turned(kind, t):
                pe.wait_ge(rows_ready, kind * NT + t + 1)
                idn = ident[0:ROWS[t], 0:ROWS[t]]
                if kind == 1:
                    tr_job([(kd[0:ROWS[t], t, i].rearrange("p u c -> p (u c)"), idn) for i in range(3)], ROWS[t])
                else:
                    tr_job([(ropeA[0:ROWS[t], t % 2, P * i:P * (i + 1)], idn) for i in range(4)], ROWS[t])

            pe.wait_ge(tr_free_dve, 10)
            chunk_arrived(pe, 0)
            for t in range(NT):
                by_rows(0, t, 512)
                if t:
                    turned(0, t - 1)
            pe.wait_ge(cache_k_in, 16 * 7)
            for c in range(NCB):
                tr_job([(natS[:, c, P * i:P * (i + 1)], ident) for i in range(4)], P)
                tr_job([(natD[:, c, i].rearrange("p u c -> p (u c)"), ident) for i in range(3)], P)
            turned(0, NT - 1)
            chunk_arrived(pe, 1)
            for t in range(NT):
                by_rows(1, t, 328)
                if t:
                    turned(1, t - 1)
            chunk_arrived(pe, 2)
            by_rows(2, 0, 512)
            by_rows(2, 1, 512)
            turned(1, NT - 1)

            pe.wait_ge(tr_free_act, emptied(TR, "act", T_DQ - 1))
            for i, (t, h, k0, k1) in enumerate(IX):
                if i >= 2:
                    pe.wait_ge(relu_ready, i - 1)
                b = bank[6 + i % 2]
                hp = slice(64 * (h % 2), 64 * (h % 2) + 64)
                n = KEY_ROWS[t]
                last = nc.tensor.matmul(b[0:n, 0:k1 - k0], iqT[hp, h // 2, OFF[t]:OFF[t] + n], dkiT[hp, 2, k0:k1],
                                        start=True, stop=True)
                if t == NT - 1:
                    q = iqT[hp, h // 2, N_PROMPT:N_ROWS]
                    last = nc.tensor.matmul(b[64:96, 0:min(k1, PAST) - k0], q, dkiC[hp, 2, k0:min(k1, PAST)],
                                            start=True, stop=True)
                    if k1 > PAST:
                        last = nc.tensor.matmul(b[64:96, PAST - k0:k1 - k0], q, dkiT[hp, 2, N_PROMPT:N_ROWS],
                                                start=True, stop=True)
                last.then_inc(ix_ready, 1)

            for t in range(2, NT):
                by_rows(2, t, 512)
                turned(2, t - 2)
            chunk_arrived(pe, 3)
            for t in range(NT):
                by_rows(3, t, 512)
                if t < 2:
                    turned(2, NT - 2 + t)

            def by_width(v, rhs, cb, g):
                lo, hi = FG[g]
                kt = v.shape[1]
                pj_job([(v[:, k, P * cb:P * (cb + 1)], rhs[:, k, lo:hi]) for k in range(kt)],
                       lambda b: b[:, 0:hi - lo])

            def chunk8(n):
                return chunk_at[n].rearrange("p (k c) -> p k c", k=KT)

            for n in (4, 5):
                chunk_arrived(pe, n)
                for j in range(8):
                    by_width(chunk8(n), xT, j // 2, j % 2)
                    t = j - 1
                    if n == 5 and 0 <= t < NT:
                        pe.wait_ge(pj_free_act, emptied(PJ, "act", J_SQ - 1))
                        tr_job([(skT[:, i, OFF[t]:OFF[t] + ROWS[t]], ident) for i in range(4)], P)

            pe.wait_ge(pj_free_act, emptied(PJ, "act", J_GSB - 1))
            pe.wait_ge(pj_free_dve, emptied(PJ, "dve", J_GSB - 1))
            pe.wait_ge(tr_free_act, emptied(TR, "act", T_X2 - 1))
            pe.wait_ge(relu_ready, len(IX))
            pe.wait_ge(cache_v_in, 32)
            pe.wait_ge(vnew_in, 32)
            for i in range(NSTEP + PV_LAG):
                if i < NSTEP:
                    s = STEPS[i]
                    if i >= ZR:
                        pe.wait_ge(w_ready, i - ZR + 1)
                    z = bank[2 + i % ZR]
                    if s["kind"] == "prompt":
                        hp = slice(64 * s["half"], 64 * s["half"] + 64)
                        last = nc.tensor.matmul(z[0:s["nk"], 0:s["n"]],
                                                skT[hp, s["pair"], OFF[s["j"]]:OFF[s["j"]] + s["nk"]],
                                                sqT[hp, s["pair"], s["q0"]:s["hi"]], start=True, stop=True,
                                                skip_group_check=True)
                    else:
                        hp = slice(64 * s["half"], 64 * s["half"] + 64)
                        for b in range(NPAIR):
                            k = (skT[hp, b, N_PROMPT:N_ROWS] if s["diag"]
                                 else ksT[hp, b, P * s["j"]:P * (s["j"] + 1)])
                            last = nc.tensor.matmul(z[0:s["nk"], b * DEC:(b + 1) * DEC], k,
                                                    sqT[hp, b, N_PROMPT:N_ROWS], start=b == 0, stop=True,
                                                    skip_group_check=True)
                    last.then_inc(z_ready, 1)
                m = i - TRI_LAG
                if 0 <= m < NSTEP:
                    s = STEPS[m]
                    z = bank[2 + m % ZR]
                    pe.wait_ge(sp_masked, m + 1)
                    last = nc.tensor.matmul(z[0:s["nk"], 0:s["n"]], ntri[0:s["nk"], 0:s["nk"]],
                                            spb[0:s["nk"], m % SPR, 0:s["n"]], start=False, stop=True,
                                            skip_group_check=True)
                    if not s["first"]:
                        pe.wait_ge(suf_ready, s["prev"] + 1)
                        c0 = s["cover0"] - s["q0"] if s["kind"] == "prompt" else 0
                        o0 = s["cover0"] - s["lo"] if s["kind"] == "prompt" else 0
                        last = nc.tensor.matmul(z[0:s["nk"], c0:s["n"]], nones[:, 0:s["nk"]],
                                                sufb[:, s["stream"], o0:o0 + s["n"] - c0], start=False, stop=True,
                                                skip_group_check=True)
                    last.then_inc(logw_ready, 1)
                m = i - PV_LAG
                if 0 <= m < NSTEP:
                    s = STEPS[m]
                    pe.wait_ge(w_masked, m + 1)
                    acc = bank[s["bank"]]
                    if s["first"] and s["bank_free"]:
                        pe.wait_ge(acc_free, s["bank_free"])
                    if s["kind"] == "prompt":
                        h = 2 * s["pair"] + s["half"]
                        o = acc[64 * s["half"]:64 * s["half"] + 64, s["q0"] - s["lo"]:s["hi"] - s["lo"]]
                        last = nc.tensor.matmul(o, svP[0:s["nk"], s["j"], 64 * h:64 * h + 64],
                                                wtb[0:s["nk"], m % WR, 0:s["n"]], start=s["first"], stop=s["last"],
                                                skip_group_check=True)
                    else:
                        for b in range(NPAIR):
                            h = 2 * b + s["half"]
                            v = svN[0:DEC, 64 * h:64 * h + 64] if s["diag"] else svC[:, s["j"], 64 * h:64 * h + 64]
                            o = acc[64 * s["half"]:64 * s["half"] + 64, DEC * b:DEC * (b + 1)]
                            last = nc.tensor.matmul(o, v, wtb[0:s["nk"], m % WR, b * DEC:(b + 1) * DEC],
                                                    start=s["first"] and b == 0, stop=True, skip_group_check=True)
                    last.then_inc(pv_done, 1)

            pe.wait_ge(acc_free, 2 * NPAIR + 1)
            def weigh_values(t):
                r = ROWS[t]
                pe.wait_ge(pT_copied, NH * (t + 1))
                if t >= 2:
                    pe.wait_ge(oT_copied, t - 1)
                o = bank[6 + t % 2][:, 0:4 * r].rearrange("p (g q) -> p g q", g=4)
                n = KEY_ROWS[t]
                for kb in range(t + 1):
                    nk = KEY_ROWS[kb]
                    for kv in range(2):
                        last = nc.tensor.matmul(o[64 * kv:64 * (kv + 1), :, 0:n],
                                                dvP[0:nk, kb, 64 * kv:64 * kv + 64],
                                                pTb[0:nk, 4 * kv:4 * kv + 4, kb * r:kb * r + n],
                                                start=kb == 0, stop=True, skip_group_check=True)
                if t == NT - 1:
                    for kb in range(NCB + 1):
                        nk = P if kb < NCB else DEC
                        v = dvC[:, kb] if kb < NCB else dvN[0:DEC]
                        for kv in range(2):
                            last = nc.tensor.matmul(o[64 * kv:64 * (kv + 1), :, 64:96],
                                                    v[:, 64 * kv:64 * kv + 64],
                                                    pTb[0:nk, 4 * kv:4 * kv + 4, kb * r + 64:kb * r + 96],
                                                    start=False, stop=True, skip_group_check=True)
                last.then_inc(pvd_done, 1)

            jobs = [(t, h) for t in range(NT) for h in range(NH)]

            for i in range(len(jobs) + TURN_LAG):
                if i < len(jobs):
                    t, h = jobs[i]
                    if i >= 2:
                        pe.wait_ge(lb_ready, i - 1)
                    pr = pairs[i % 2]
                    hp = slice(64 * (h % 2), 64 * (h % 2) + 64)
                    kv = h // 4
                    n = KEY_ROWS[t]
                    q = dqT[hp, h // 2, OFF[t]:OFF[t] + n]
                    if t < NT - 1:
                        last = nc.tensor.matmul(pr[0:n, 0:KEYS[t]], q, dkiT[hp, kv, 0:KEYS[t]], start=True, stop=True)
                    else:
                        qs = dqT[hp, h // 2, N_PROMPT:N_ROWS]
                        for b in range(2):
                            k0, k1 = 272 * b, 272 * (b + 1)
                            o = pr[:, 512 * b:512 * b + 272]
                            nc.tensor.matmul(o[0:64, :], q, dkiT[hp, kv, k0:k1], start=True, stop=True)
                            last = nc.tensor.matmul(o[64:96, 0:min(k1, PAST) - k0], qs, dkiC[hp, kv, k0:min(k1, PAST)],
                                                    start=True, stop=True)
                        last = nc.tensor.matmul(o[64:96, PAST - k0:272], qs, dkiT[hp, kv, N_PROMPT:N_ROWS],
                                                start=True, stop=True)
                    last.then_inc(lg_ready, 1)
                m = i - TURN_LAG
                if m < 0:
                    continue
                t, h = jobs[m]
                if h == 0 and t:
                    weigh_values(t - 1)
                pe.wait_ge(pn_ready, m + 1)
                if m >= 2:
                    pe.wait_ge(pT_copied, m - 1)
                b = bank[4 + m % 2]
                r = ROWS[t]
                for kb in range(t + 1):
                    nk = KEY_ROWS[kb]
                    n = KEY_ROWS[t]
                    last = nc.tensor.transpose(b[0:nk, kb * r:kb * r + n], pb[0:n, m % PR, OFF[kb]:OFF[kb] + nk],
                                               ident[0:n, 0:n])
                if t == NT - 1:
                    for kb in range(NCB + 1):
                        nk = P if kb < NCB else DEC
                        last = nc.tensor.transpose(b[0:nk, kb * r + 64:kb * r + 96],
                                                   pb[64:96, m % PR, P * kb:P * kb + nk], ident[64:96, 64:96])
                last.then_inc(pT_ready, 1)
            weigh_values(NT - 1)

            pe.wait_ge(oT_copied, NT)
            for n in (6, 7):
                chunk_arrived(pe, n)
                for cb in range(4):
                    for g in range(2):
                        by_width(chunk8(n), xT, cb, g)
            chunk_arrived(pe, 8)
            for cb in range(8):
                for g in range(2):
                    by_width(chunk_at[8].rearrange("p (k c) -> p k c", k=4), osbT, cb, g)
            chunk_arrived(pe, 9)
            for cb in range(8):
                chunk_arrived(pe, 10 + cb // 4)
                for g in range(2):
                    by_width(chunk8(10 + cb // 4), xT, cb % 4, g)
                    by_width(chunk_at[9].rearrange("p (k c) -> p k c", k=4), odsaT, cb, g)
            pe.wait_ge(merged_ready, 16)
            chunk_arrived(pe, 12)
            chunk_arrived(pe, 13)
            for t in range(NT + 2):
                if t < NT:
                    for c in range(2):
                        pj_job([(merged[:, k, OFF[t]:OFF[t] + ROWS[t]], chunk8(12 + c)[:, k, :]) for k in range(KT)],
                               lambda b: b[0:ROWS[t], :])
                u = t - 2
                if u >= 0:
                    pe.wait_ge(x2_ready, u + 1)
                    xk = x2row[0:ROWS[u], u % 2, :].rearrange("p (c k) -> p k c", k=KT)
                    for q in range(2):
                        tr_job([(xk[:, 4 * q + i, :], ident[0:ROWS[u], 0:ROWS[u]]) for i in range(4)], ROWS[u])
                    if u >= NT - 2:
                        pe.wait_ge(wr_in, 32)
                        pe.wait_ge(tr_free_act, emptied(TR, "act", T_X2 + 2 * u + 1))
                        lo, hi = RG[u - (NT - 2)]
                        pj_job([(wr[:, k, :], xT[:, k, lo:hi]) for k in range(KT)], lambda b: b[0:36, 0:hi - lo])
            pe.wait_ge(pj_free_act, emptied(PJ, "act", len(PJ) - 1))
            tr_wait_free(pe, tr[0])
            for t in range(NT):
                last = nc.tensor.transpose(bank[4 + tr[0] % 2][0:ROWS[t], 36 * t:36 * (t + 1)],
                                           lgT[0:36, OFF[t]:OFF[t] + ROWS[t]], ident[0:36, 0:36])
            last.then_inc(tr_ready, 1)
            pe.wait_ge(onehot_ready, 1)
            b = bank[0]
            pe.wait_ge(pj_free_act, emptied(PJ, "act", len(PJ) - 1))
            nc.tensor.matmul(b[:, 0:(NT + 1) * NE].rearrange("p (t e) -> p t e", e=NE), nones,
                             earlier.rearrange("p e t -> p t e"), start=True, stop=True, skip_group_check=True)
            nc.tensor.matmul(b[:, 0:NT * NE].rearrange("p (t e) -> p t e", e=NE), stri,
                             marks[:, :, 1:].rearrange("p e t -> p t e"), start=False, stop=True,
                             skip_group_check=True).then_inc(pos_ready, 1)
            pe.wait_ge(slots_ready, 1)
            for n in range(2 * NT):
                last = nc.tensor.matmul(bank[1][0:CAP, 0:NBLK], at_slot[:, n, :], at_block[:, n, :],
                                        start=n == 0, stop=n == 2 * NT - 1)
            last.then_inc(idx_ready, 1)

            def x_to_width(q, done):
                x = Xg[:, q, :].rearrange("p (c k) -> p k c", k=KT)
                for k in range(KT):
                    last = nc.tensor.transpose(bank[4 * q][:, k * CAP:(k + 1) * CAP], x[:, k, :], ident[0:CAP, 0:CAP])
                last.then_inc(done, 1)

            def gate_up(q, slot, done):
                wv = moe_gu[slot].rearrange("p (g k c) -> p g k c", g=2, k=KT)
                for k in range(KT):
                    for f in range(2):
                        last = nc.tensor.matmul(
                            bank[4 * q + 1][64 * f:64 * f + 64, 0:256].rearrange("p (g c) -> p g c", g=2),
                            xgT[:, q, k, :], wv[:, :, k, P * f:P * (f + 1)], start=k == 0, stop=k == KT - 1)
                last.then_inc(done, 1)

            def hidden_to_width(q, done):
                nc.tensor.transpose(bank[4 * q + 2][:, 0:P], hid[:, q, :], ident).then_inc(done, 1)

            def down(q, slot, done):
                for f in range(2):
                    for c in range(2):
                        last = nc.tensor.matmul(bank[4 * q + 3][64 * c:64 * c + 64, :],
                                                hidT[:, q, 64 * f:64 * f + 64],
                                                moe_dn[slot][f][:, 512 * c:512 * (c + 1)],
                                                start=f == 0, stop=f == 1)
                last.then_inc(done, 1)

            def down_in_turn(i, s):
                pe.wait_ge(hidT_ready, i * MS + s + 1)
                pe.wait_ge(y_copied[s % 2], i * (MS // 2) + s // 2)
                down(s % 2, s, y_done[s])

            def expert(i, s):
                q = s % 2
                pe.wait_ge(xgT_ready[q], i * (MS // 2) + s // 2 + 1)
                pe.wait_ge(mw_in[s], i * 64 + 64)
                gate_up(q, s, gu_ready)
                pe.wait_ge(gath[1 - q], (i * (MS // 2) + (s + 1) // 2 + 1) * 16)
                nc.tensor.sem_inc(pe_turns, 1)
                x_to_width(1 - q, xgp_ready[1 - q])
                if s:
                    down_in_turn(i, s - 1)
                pe.wait_ge(hid_ready, i * MS + s + 1)
                hidden_to_width(q, hT_ready)

            pe.wait_ge(gath[0], 16)
            x_to_width(0, xgp_ready[0])
            with pe.Fori(0, NE // MS) as i:
                for s in range(MS):
                    expert(i, s)
                down_in_turn(i, MS - 1)
            for s in range(NE % MS):
                expert(NE // MS, s)
            down_in_turn(NE // MS, NE % MS - 1)
            over = pe.value_load(over_i[0:1, MAX_OVER:MAX_OVER + 1], min_val=0, max_val=MAX_OVER)
            with pe.If(over > 0):
                pe.wait_ge(xgT_ready[0], NE // 2 + 1)
                pe.wait_ge(y_copied[0], NE // 2)
                with pe.Fori(0, MAX_OVER) as b:
                    pe.wait_ge(o_g, b * 16 + 16)
                    nc.tensor.sem_inc(pe_turns, 1)
                    x_to_width(0, o_step)
                    pe.wait_ge(o_w, b * 64 + 64)
                    pe.wait_ge(o_step, b * 10 + 2)
                    gate_up(0, 0, o_step)
                    pe.wait_ge(o_step, b * 10 + 5)
                    hidden_to_width(0, o_step)
                    pe.wait_ge(o_step, b * 10 + 7)
                    down(0, 0, o_step)

        @block.scalar
        def _(act):
            tr = [0]
            chain = [0]

            def link(ins):
                chain[0] += 1
                ins.then_inc(act_chain, 1)
                act.wait_ge(act_chain, chain[0])

            nc.scalar.preload_act_table_set("natural_log_exp_and_others")
            for t in range(NT):
                r = ROWS[t]
                act.wait_ge(x_in[t], 16 * len(row_pieces(t)))
                link(nc.scalar.activation(arena[0:r, 0:D], X[0:r, t, :], ACT.Square, scale=1.0 / 32.0,
                                          accum_out=ss[0:r, t:t + 1]))
                nc.scalar.sem_inc(ss_ready, 1)
            tr[0] = 10

            def tr_copy(dst, n, cols, rows=P):
                act.wait_ge(tr_ready, tr[0] + 1)
                b = bank[4 + tr[0] % 2]
                nc.scalar.activation(dst, b[0:rows, 0:n * cols].rearrange("p (i c) -> p i c", i=n), ACT.Copy)\
                    .then_inc(tr_free_act, 1)
                tr[0] += 1

            act.wait_ge(xs_ready, NT)
            act.wait_ge(tr_ready, 10)
            for t in range(NT):
                if t == NT - 1:
                    for c in range(NCB):
                        tr_copy(ksT[:, :, P * c:P * (c + 1)], 4, P)
                        tr_copy(dkiC[:, :, P * c:P * (c + 1)], 3, P)
                tr_copy(iqT[:, :, OFF[t]:OFF[t] + ROWS[t]], 4, ROWS[t])

            def pj_copy(n, dst, src, func=ACT.Copy, scale=1.0):
                act.wait_ge(pj_ready, n + 1)
                ins = nc.scalar.activation(dst, src(bank[n % 4]), func, scale=scale)
                ins.then_inc(pj_free_act, 1)

            def squares_of(n, t, i, c0, cols):
                act.wait_ge(pj_ready, n + t + 1)
                if i >= 2:
                    act.wait_ge(rope_parts, i - 1 + NT)
                r = ROWS[t]
                nc.scalar.activation(ropeQ[0:r, i % 2, 0:cols], bank[(n + t) % 4][0:r, c0:c0 + cols],
                                     ACT.Square, scale=1.0 / 8.0).then_inc(squares, 1)

            for t in range(NT + 1):
                if t < NT:
                    squares_of(J_SM, t, t, N_SMALL1, 128)
                if t:
                    tr_copy(dkiT[:, :, OFF[t - 1]:OFF[t - 1] + ROWS[t - 1]], 3, ROWS[t - 1])
            for i, (t, h, k0, k1) in enumerate(IX):
                r = ROWS[t]
                act.wait_ge(ix_ready, i + 1)
                if i >= 2:
                    act.wait_ge(relu_used, i - 1)
                nc.scalar.activation(rb[0:r, i % 2, 0:k1 - k0], bank[6 + i % 2][0:r, 0:k1 - k0], ACT.Relu)\
                    .then_inc(relu_ready, 1)
            for t in range(NT + 1):
                if t < NT:
                    squares_of(J_DQ, t, NT + t, 0, 512)
                if t:
                    tr_copy(dqT[:, :, OFF[t - 1]:OFF[t - 1] + ROWS[t - 1]], 4, ROWS[t - 1])
            for t in range(NT):
                r = ROWS[t]
                act.wait_ge(pj_ready, J_SV + t + 1)
                link(nc.scalar.activation(svP[0:r, t, :], bank[(J_SV + t) % 4][0:r, :], ACT.Copy))
                nc.scalar.sem_inc(pj_free_act, 1)
                nc.scalar.sem_inc(sv_rows, 1)
            for n0, dst, scale in ((J_SK, skT, 1.0), (J_SQ, sqT, HD ** -0.5)):
                for j in range(8):
                    lo, hi = FG[j % 2]
                    pj_copy(n0 + j, dst[:, j // 2, lo:hi], lambda b: b[:, 0:hi - lo], scale=scale)
                    t = j - 1
                    if n0 == J_SQ and 0 <= t < NT:
                        r = ROWS[t]
                        act.wait_ge(tr_ready, tr[0] + 1)
                        back = skR4 if t == NT - 1 else skR[:, t, :]
                        link(nc.scalar.activation(back[0:r, :], bank[4 + tr[0] % 2][0:r, :], ACT.Copy))
                        nc.scalar.sem_inc(tr_free_act, 1)
                        nc.scalar.sem_inc(sk_rows, 1)
                        tr[0] += 1

            for i in range(NSTEP + PV_LAG):
                if i < NSTEP:
                    s = STEPS[i]
                    act.wait_ge(cap_ready, i + 1)
                    v = spb[0:s["nk"], i % SPR, 0:s["n"]]
                    link(nc.scalar.activation(v, v, ACT.Exp))
                    nc.scalar.activation(v, v, ACT.Ln, bias=1.0).then_inc(ln_ready, 1)
                m = i - TRI_LAG
                if 0 <= m < NSTEP:
                    s = STEPS[m]
                    act.wait_ge(logw_ready, m + 1)
                    if m >= WR:
                        act.wait_ge(pv_done, m - WR + 1)
                    nc.scalar.activation(wtb[0:s["nk"], m % WR, 0:s["n"]], bank[2 + m % ZR][0:s["nk"], 0:s["n"]],
                                         ACT.Exp).then_inc(w_ready, 1)
                e = i - PV_LAG
                if 0 <= e < NSTEP and STEPS[e]["closes"]:
                    s = STEPS[e]
                    act.wait_ge(pv_done, e + 1)
                    if s["kind"] == "prompt":
                        dst, src = osbT[:, s["pair"], s["lo"]:s["hi"]], bank[s["bank"]][:, 0:s["hi"] - s["lo"]]
                    else:
                        dst = osbT[:, :, N_PROMPT:N_ROWS]
                        src = bank[s["bank"]][:, 0:NPAIR * DEC].rearrange("p (b q) -> p b q", b=NPAIR)
                    nc.scalar.activation(dst, src, ACT.Copy).then_inc(acc_free, 1)

            def outputs(t):
                act.wait_ge(pvd_done, t + 1)
                nc.scalar.activation(odsaT[:, :, OFF[t]:OFF[t] + ROWS[t]],
                                     bank[6 + t % 2][:, 0:4 * ROWS[t]].rearrange("p (g q) -> p g q", g=4),
                                     ACT.Copy).then_inc(oT_copied, 1)

            jobs = [(t, h) for t in range(NT) for h in range(NH)]
            for i in range(len(jobs) + TURN_LAG):
                if i < len(jobs):
                    t, h = jobs[i]
                    r, w = ROWS[t], KEYS[t]
                    act.wait_ge(lb_ready, i + 1)
                    if i >= PR:
                        act.wait_ge(pT_ready, i - PR + 1)
                    nc.scalar.activation(pb[0:r, i % PR, 0:w], Lb[0:r, i % LR, 0:w], ACT.Exp, scale=HD ** -0.5,
                                         bias=nbias[0:r, i % LR:i % LR + 1],
                                         accum_out=rsum[0:r, i % PR:i % PR + 1]).then_inc(p_ready, 1)
                m = i - TURN_LAG
                if m < 0:
                    continue
                t, h = jobs[m]
                act.wait_ge(pT_ready, m + 1)
                if h == 0 and t:
                    outputs(t - 1)
                n = (t + 1) * ROWS[t]
                nc.scalar.activation(pTb[:, h, 0:n], bank[4 + m % 2][:, 0:n], ACT.Copy).then_inc(pT_copied, 1)
            outputs(NT - 1)

            for cb in range(8):
                for g in range(2):
                    lo, hi = FG[g]
                    n = J_GSB + 2 * cb + g
                    act.wait_ge(pj_ready, n + 1)
                    link(nc.scalar.activation(merged[:, cb, lo:hi], bank[n % 4][:, 0:hi - lo], ACT.Sigmoid))
                    nc.scalar.sem_inc(pj_free_act, 1)
                    nc.scalar.sem_inc(gate_ready, 1)
            for j in range(16):
                cb, g = j // 2, j % 2
                lo, hi = FG[g]
                n = J_GB + 2 * j
                act.wait_ge(pj_ready, n + 1)
                if j >= 2:
                    act.wait_ge(half_merged, j - 1)
                link(nc.scalar.activation(tabs[:, (j % 2) * 280:(j % 2) * 280 + hi - lo], bank[n % 4][:, 0:hi - lo],
                                          ACT.Sigmoid))
                nc.scalar.sem_inc(pj_free_act, 1)
                nc.scalar.sem_inc(gate_ready, 1)
            for t in range(NT + 2):
                if t < NT:
                    r = ROWS[t]
                    act.wait_ge(h_ready, t + 1)
                    link(nc.scalar.activation(scrap[0:r, :], X[0:r, t, :], ACT.Square, scale=1.0 / 32.0,
                                              accum_out=ss[0:r, t:t + 1]))
                    nc.scalar.sem_inc(ss2_ready, 1)
                u = t - 2
                if u >= 0:
                    for q in range(2):
                        tr_copy(xT[:, 4 * q:4 * q + 4, OFF[u]:OFF[u] + ROWS[u]], 4, ROWS[u])
            for g, (lo, hi) in enumerate(RG):
                n = J_RT + g
                act.wait_ge(pj_ready, n + 1)
                nc.scalar.activation(lgT[0:36, lo:hi], bank[n % 4][0:36, 0:hi - lo], ACT.Copy).then_inc(pj_free_act, 1)
            act.wait_ge(tr_ready, tr[0] + 1)
            nc.scalar.activation(rl, bank[4 + tr[0] % 2][:, 0:36 * NT].rearrange("p (t c) -> p t c", t=NT), ACT.Copy)\
                .then_inc(logits_ready, 1)
            act.wait_ge(rvals_ready, 1)
            link(nc.scalar.activation(gx[:, 0:4 * NT], gx[:, 0:4 * NT], ACT.Exp))
            nc.scalar.sem_inc(rexp_ready, 1)
            act.wait_ge(rvals_ready, 2)
            link(nc.scalar.activation(gx[:, 40:40 + NT], gx[:, 40:40 + NT], ACT.Exp))
            nc.scalar.sem_inc(rexp_ready, 1)
            nc.scalar.activation(gx[:, 56:57], gx[:, 40:41], ACT.Silu)

            def copy_x(q, done):
                nc.scalar.activation(xgT[:, q], bank[4 * q].rearrange("p (k s) -> p k s", k=KT), ACT.Copy)\
                    .then_inc(done, 1)

            def silu(q, done):
                nc.scalar.activation(sil[:, q, :], bank[4 * q + 1][:, 0:P], ACT.Silu).then_inc(done, 1)

            def store_y(q, first):
                for c in range(2):
                    act.dma_start(y_d[bass.ds(first, CAP), 512 * c:512 * (c + 1)], Yb[64 * c:64 * c + 64, q, :])\
                        .then_inc(y_out[q], 16)

            def y_in_turn(i, s):
                q = s % 2
                act.wait_ge(y_done[s], i + 1)
                act.wait_ge(y_out[q], (i * (MS // 2) + s // 2) * 32)
                nc.scalar.activation(Yb[:, q, :], bank[4 * q + 3], ACT.Copy).then_inc(y_copied[q], 1)
                act.wait_ge(y_copied[q], i * (MS // 2) + s // 2 + 1)
                store_y(q, (i * MS + s) * CAP)

            def expert(i, s):
                q = s % 2
                act.wait_ge(gu_ready, i * MS + s + 1)
                silu(q, silu_ready)
                act.wait_ge(xgp_ready[1 - q], i * (MS // 2) + (s + 1) // 2 + 1)
                copy_x(1 - q, xgT_ready[1 - q])
                if s:
                    y_in_turn(i, s - 1)

            act.wait_ge(xgp_ready[0], 1)
            copy_x(0, xgT_ready[0])
            with act.Fori(0, NE // MS) as i:
                for s in range(MS):
                    expert(i, s)
                y_in_turn(i, MS - 1)
            for s in range(NE % MS):
                expert(NE // MS, s)
            y_in_turn(NE // MS, NE % MS - 1)
            for q in range(2):
                act.wait_ge(y_out[q], NE // 2 * 32)
            over = act.value_load(over_i[0:1, MAX_OVER:MAX_OVER + 1], min_val=0, max_val=MAX_OVER)
            with act.If(over > 0):
                with act.Fori(0, MAX_OVER) as b:
                    act.wait_ge(o_step, b * 10 + 1)
                    copy_x(0, o_step)
                    act.wait_ge(o_step, b * 10 + 3)
                    silu(0, o_step)
                    act.wait_ge(o_step, b * 10 + 8)
                    nc.scalar.activation(Yb[:, 0, :], bank[3], ACT.Copy).then_inc(o_step, 1)
                    act.wait_ge(o_step, b * 10 + 9)
                    store_y(0, (b + NE) * CAP)
                    act.wait_ge(y_out[0], (b + NE // 2 + 1) * 32)
                    nc.scalar.sem_inc(o_step, 1)
            nc.scalar.sem_inc(results_out, 1)

        @block.gpsimd
        def _(pool):
            chain = [0]

            def link(ins):
                chain[0] += 1
                ins.then_inc(pool_chain, 1)
                pool.wait_ge(pool_chain, chain[0])

            def inverse_root(t, ready, done):
                r = ROWS[t]
                pool.wait_ge(ready, t + 1)
                link(nc.gpsimd.tensor_scalar(rstd[0:r, t:t + 1], ss[0:r, t:t + 1], EPS, None, ALU.add))
                nc.gpsimd.tensor_tensor(rstd[0:r, t:t + 1], rstd[0:r, t:t + 1], mhalf[0:r, 0:1], ALU.pow)\
                    .then_inc(done, 1)

            link(nc.gpsimd.memset(mhalf, -0.5))
            for t in range(NT):
                inverse_root(t, ss_ready, rstd_ready)
            pool.wait_ge(const_in, 16)
            pool.wait_ge(gains_in, 16 * 6)
            for w in range(2):
                for v, base in ((0, cos), (1, sin)):
                    g = gqk[:, (2 * w + v) * HD:(2 * w + v + 1) * HD].rearrange("p (o c) -> p o c", o=1)
                    link(nc.gpsimd.tensor_tensor(tab[:, 2 * w + v], base, g.broadcast_to([P, NT, HD]), ALU.mult))
            nc.gpsimd.sem_inc(tables_ready, 1)
            pool.wait_ge(zero_ready, 1)
            pool.dma_start(y_d[NE * CAP:, :].rearrange("(p a) (b c) -> p a b c", p=64, b=2)
                           .rearrange("p a b c -> p (a b) c"),
                           zeros[0:64, :].rearrange("p (o c) -> p o c", o=1).broadcast_to([64, 2 * MAX_OVER, 512]))\
                .then_inc(y_zeroed, 16)
            for n in range(3 * NT):
                t, kind = n % NT, n // NT
                r = ROWS[t]
                pool.wait_ge(rope_parts, n + 1)
                if kind:
                    hs = 2 if kind == 1 else NH
                    f = rq[0:r, n % 2, 0:hs]
                    link(nc.gpsimd.tensor_scalar(f, ssq[0:r, n % 2, 0:hs], EPS, None, ALU.add))
                    link(nc.gpsimd.tensor_tensor(f, f, mhalf[0:r, 0:hs], ALU.pow))
                if kind == 1:
                    d = kd[0:r, t, :, 0, :]
                    link(nc.gpsimd.tensor_tensor(d, d, ropeB[0:r, n % 2, 0:192].rearrange("p (b c) -> p b c", b=3),
                                                 ALU.add))
                    link(nc.gpsimd.tensor_tensor(d[:, 0:2], d[:, 0:2],
                                                 rq[0:r, n % 2, 0:2].rearrange("p (h o) -> p h o", o=1)
                                                 .broadcast_to([r, 2, HD]), ALU.mult))
                    link(nc.gpsimd.tensor_copy(kd[0:r, t, :, 1, :], d))
                    nc.gpsimd.sem_inc(small_rows, 1)
                else:
                    A = ropeA[0:r, t % 2, :]
                    link(nc.gpsimd.tensor_tensor(A, A, ropeB[0:r, n % 2, :], ALU.add))
                    if kind == 2:
                        A3 = A.rearrange("p (h c) -> p h c", h=NH)
                        link(nc.gpsimd.tensor_tensor(A3, A3, rq[0:r, n % 2, :].rearrange("p (h o) -> p h o", o=1)
                                                     .broadcast_to([r, NH, HD]), ALU.mult))
                nc.gpsimd.sem_inc(rows_ready, 1)

            pool.wait_ge(keys_out, 16 * 6 * (NT + 1))
            for i in range(NSTEP + PV_LAG):
                m = i - 1
                if 0 <= m < NSTEP:
                    s = STEPS[m]
                    pool.wait_ge(sp_ready, m + 1)
                    v = spb[0:s["nk"], m % SPR, 0:s["n"]]
                    if s["diag"]:
                        if s["kind"] == "prompt":
                            w = min(s["nk"], s["n"])
                            v = v[:, 0:w]
                            link(nc.gpsimd.affine_select(out=v, in_=v, compare_op=ALU.is_gt, fill=0.0, base=0,
                                                         pattern=[[1, w]], channel_multiplier=-1))
                        else:
                            v3 = v.rearrange("p (b q) -> p b q", b=NPAIR)
                            link(nc.gpsimd.affine_select(out=v3, in_=v3, compare_op=ALU.is_gt, fill=0.0, base=0,
                                                         pattern=[[0, NPAIR], [1, DEC]], channel_multiplier=-1))
                    nc.gpsimd.sem_inc(sp_masked, 1)
                    if s["first"]:
                        if s["prev"] is not None:
                            pool.wait_ge(logw_ready, s["prev"] + 1)
                        link(nc.gpsimd.memset(sufb[:, s["stream"], :], 0.0))
                m = i - TRI_LAG
                if 0 <= m < NSTEP:
                    s = STEPS[m]
                    if not s["last"]:
                        pool.wait_ge(logw_ready, m + 1)
                        o0 = s["q0"] - s["lo"] if s["kind"] == "prompt" else 0
                        v = sufb[0:s["nk"], s["stream"], o0:o0 + s["n"]]
                        link(nc.gpsimd.tensor_tensor(v, v, spb[0:s["nk"], m % SPR, 0:s["n"]], ALU.add))
                    nc.gpsimd.sem_inc(suf_ready, 1)
                m = i - TRI_LAG - 1
                if 0 <= m < NSTEP:
                    s = STEPS[m]
                    pool.wait_ge(w_ready, m + 1)
                    if s["diag"]:
                        if s["kind"] == "prompt":
                            w = min(s["nk"], s["n"])
                            v = wtb[0:s["nk"], m % WR, 0:w]
                            link(nc.gpsimd.affine_select(out=v, in_=v, compare_op=ALU.is_gt, fill=0.0, base=0,
                                                         pattern=[[1, w]], channel_multiplier=-1))
                        else:
                            v3 = wtb[0:s["nk"], m % WR, 0:s["n"]].rearrange("p (b q) -> p b q", b=NPAIR)
                            link(nc.gpsimd.affine_select(out=v3, in_=v3, compare_op=ALU.is_gt, fill=0.0, base=0,
                                                         pattern=[[0, NPAIR], [1, DEC]], channel_multiplier=-1))
                    nc.gpsimd.sem_inc(w_masked, 1)

            pool.wait_ge(oT_copied, NT)
            load_chunk(pool, 8)
            load_chunk(pool, 9)
            load_chunk(pool, 10)
            load_chunk(pool, 11)
            pool.dma_start(wr[:, :, 0:4], a["w_group"].rearrange("(p k) c -> p k c", k=KT)).then_inc(wr_in, 16)
            pool.dma_start(wr[:, :, 4:36], a["w_router"].rearrange("(p k) c -> p k c", k=KT)).then_inc(wr_in, 16)
            load_chunk(pool, 12)
            load_chunk(pool, 13)
            pool.wait_ge(y_zeroed, 16)
            pool.wait_ge(pj_ready, used_at[11])
            for t in range(NT):
                for p0, p1, which, r0 in row_pieces(t):
                    src = a["meta_tokens"] if which == "meta" else a["x_" + which]
                    pool.dma_start(X[p0:p1, t, :], src[r0:r0 + p1 - p0, :]).then_inc(xres_in, 16)
            pool.dma_start(g2b, a["norm2_g"].rearrange("(o c) -> o c", o=1).broadcast_to([P, D])).then_inc(g2_in, 16)
            for t in range(NT):
                inverse_root(t, ss2_ready, rstd2_ready)
                pool.wait_ge(x2_ready, t + 1)
                pool.dma_start(xn2_d[OFF[t]:OFF[t] + ROWS[t], :], x2row[0:ROWS[t], t % 2, :]).then_inc(x2_stored[t], 16)
            pool.wait_ge(idx_in, 1)
            for t in range(NT):
                pool.wait_ge(x2_stored[t], 16)
            def gather(q, block_no, copied):
                nc.gpsimd.tensor_copy(idx_now[:, q:q + 1], idxs[:, block_no]).then_inc(idx_now_ready, 1)
                pool.wait_ge(idx_now_ready, copied)
                nc.gpsimd.sem_inc(pool_turns, 1)
                pool.indirect_dma_start(Xg[:, q, :], None, xn2_d,
                                        bass.IndirectOffsetOnAxis(ap=idx_now[:, q:q + 1], axis=0)).then_inc(gath[q], 16)

            for q in range(2):
                gather(q, slice(q, q + 1), q + 1)
            with pool.Fori(0, NE // 2) as i:
                for q in range(2):
                    pool.wait_ge(xgp_ready[q], i + 1)
                    gather(q, bass.ds(i * 2 + q + 2, 1), i * 2 + q + 3)
            pool.wait_ge(gath[0], (NE // 2 + 1) * 16)
            pool.wait_ge(gath[1], (NE // 2 + 1) * 16)
            over = pool.value_load(over_i[0:1, MAX_OVER:MAX_OVER + 1], min_val=0, max_val=MAX_OVER)
            with pool.If(over > 0):
                pool.wait_ge(xgp_ready[0], NE // 2 + 1)
                with pool.Fori(0, MAX_OVER) as b:
                    pool.wait_ge(o_step, b * 10)
                    nc.gpsimd.tensor_copy(idx_now[:, 0:1], idxs[:, bass.ds(b + NE, 1)]).then_inc(o_idx, 1)
                    pool.wait_ge(o_idx, b + 1)
                    nc.gpsimd.sem_inc(pool_turns, 1)
                    pool.indirect_dma_start(Xg[:, 0, :], None, xn2_d,
                                            bass.IndirectOffsetOnAxis(ap=idx_now[:, 0:1], axis=0)).then_inc(o_g, 16)
            pool.wait_ge(results_out, 1)
            for t in range(NT):
                for c in range(2):
                    n = 2 * t + c
                    pool.indirect_dma_start(arena[0:ROWS[t], n * D:(n + 1) * D], None, y_d,
                                            bass.IndirectOffsetOnAxis(ap=slot_i[0:ROWS[t], c * NT + t:c * NT + t + 1], axis=0))\
                        .then_inc(comb_in[n], 16)

        @block.vector
        def _(dve):
            chain = [0]

            def link(ins):
                chain[0] += 1
                ins.then_inc(dve_chain, 1)
                dve.wait_ge(dve_chain, chain[0])
                return ins

            for p in pairs:
                link(nc.vector.memset(p[:, :], 0.0))

            def norm_rows(t, ready, out_ap):
                r = ROWS[t]
                dve.wait_ge(ready, t + 1)
                link(nc.vector.tensor_scalar(out_ap, X[0:r, t, :], rstd[0:r, t:t + 1], None, ALU.mult))

            for t in range(NT):
                norm_rows(t, rstd_ready, X[0:ROWS[t], t, :])
                nc.vector.sem_inc(xs_ready, 1)
            dve.wait_ge(g1_in, 16)
            for n in range(2 * NT):
                t, q = n // 2, n % 2
                r = ROWS[t]
                dve.wait_ge(tr_ready, n + 1)
                nc.vector.tensor_tensor(xT[:, 4 * q:4 * q + 4, OFF[t]:OFF[t] + r],
                                        bank[4 + n % 2][:, 0:4 * r].rearrange("p (i c) -> p i c", i=4),
                                        g1[:, 4 * q:4 * q + 4].rearrange("p (k o) -> p k o", o=1)
                                        .broadcast_to([P, 4, r]), ALU.mult).then_inc(tr_free_dve, 1)

            def rope(src, A, B, ct, st, r, heads):
                def bc(v, w):
                    return v.rearrange("p (o c) -> p o c", o=1).broadcast_to([r, heads, w])
                nc.vector.tensor_tensor(A, src, bc(ct, HD), ALU.mult)
                nc.vector.tensor_tensor(B[:, :, 0:HALF], src[:, :, HALF:HD], bc(st[:, 0:HALF], HALF), ALU.mult)
                return nc.vector.tensor_tensor(B[:, :, HALF:HD], src[:, :, 0:HALF], bc(st[:, HALF:HD], HALF), ALU.mult)

            def wait_rope_buffers(n):
                if n >= 2:
                    dve.wait_ge(rows_ready, n - 1)

            nc.vector.memset(zeros, 0.0).then_inc(zero_ready, 1)
            dve.wait_ge(tables_ready, 1)
            for t in range(NT):
                r = ROWS[t]
                n = J_IQ + t
                dve.wait_ge(pj_ready, n + 1)
                wait_rope_buffers(t)
                if t >= 2:
                    dve.wait_ge(tr_ready, T_IQ + t - 1)
                src = bank[n % 4][0:r, :].rearrange("p (h c) -> p h c", h=NH)
                link(rope(src, ropeA[0:r, t % 2, :].rearrange("p (h c) -> p h c", h=NH),
                          ropeB[0:r, t % 2, :].rearrange("p (h c) -> p h c", h=NH), cos[0:r, t], sin[0:r, t], r, NH))
                nc.vector.sem_inc(pj_free_dve, 1)
                nc.vector.sem_inc(rope_parts, 1)
            for t in range(NT):
                r = ROWS[t]
                n = J_SM + t
                m = NT + t
                b = bank[n % 4][0:r, :]
                dve.wait_ge(squares, t + 1)
                wait_rope_buffers(m)
                nc.vector.tensor_scalar(iws[0:r, t, :], b[:, HD:HD + NH], HD ** -0.5 * NH ** -0.5, None, ALU.mult)
                nc.vector.tensor_copy(dvP[0:r, t, :], b[:, N_SMALL1 + 128:328])
                B = ropeB[0:r, m % 2, 0:192].rearrange("p (b c) -> p b c", b=3)
                rope(b[:, 0:HD].rearrange("p (h c) -> p h c", h=1), kd[0:r, t, 2:3, 0, :], B[:, 2:3], cos[0:r, t],
                     sin[0:r, t], r, 1)
                rope(b[:, N_SMALL1:N_SMALL1 + 128].rearrange("p (h c) -> p h c", h=2), kd[0:r, t, 0:2, 0, :],
                     B[:, 0:2], tab[0:r, 2, t], tab[0:r, 3, t], r, 2)
                link(nc.vector.tensor_reduce(ssq[0:r, m % 2, 0:2],
                                             ropeQ[0:r, t % 2, 0:128].rearrange("p (h c) -> p h c", h=2), AX.X, ALU.add))
                nc.vector.sem_inc(pj_free_dve, 1)
                nc.vector.sem_inc(rope_parts, 1)
            for i, (t, h, k0, k1) in enumerate(IX):
                r = ROWS[t]
                dve.wait_ge(relu_ready, i + 1)
                s = SC[t][0:r, k0:k1]
                if h == 0:
                    link(nc.vector.tensor_scalar(s, rb[0:r, i % 2, 0:k1 - k0], iws[0:r, t, 0:1], None, ALU.mult))
                else:
                    link(nc.vector.scalar_tensor_tensor(s, rb[0:r, i % 2, 0:k1 - k0], iws[0:r, t, h:h + 1], s,
                                                        ALU.mult, ALU.add))
                nc.vector.sem_inc(relu_used, 1)
            for t in range(NT):
                r = ROWS[t]
                n = J_DQ + t
                m = 2 * NT + t
                dve.wait_ge(squares, NT + t + 1)
                wait_rope_buffers(m)
                if t >= 2:
                    dve.wait_ge(tr_ready, T_DQ + t - 1)
                src = bank[n % 4][0:r, :].rearrange("p (h c) -> p h c", h=NH)
                rope(src, ropeA[0:r, t % 2, :].rearrange("p (h c) -> p h c", h=NH),
                     ropeB[0:r, m % 2, :].rearrange("p (h c) -> p h c", h=NH), tab[0:r, 0, t], tab[0:r, 1, t], r, NH)
                link(nc.vector.tensor_reduce(ssq[0:r, m % 2, :],
                                             ropeQ[0:r, (NT + t) % 2, :].rearrange("p (h c) -> p h c", h=NH),
                                             AX.X, ALU.add))
                nc.vector.sem_inc(pj_free_dve, 1)
                nc.vector.sem_inc(rope_parts, 1)
            link(nc.vector.memset(SC[0][0:ROWS[0], :], 0.0))
            link(nc.vector.memset(SC[0][0:N_META, N_META:KEYS[0]], -BIG))
            for t in range(1, NT):
                r = ROWS[t]
                w = KEYS[t]
                hide = w - CHUNK if t < NT - 1 else N_PROMPT
                link(nc.vector.memset(SC[t][0:64, hide:w], HIDDEN))
                for n in range(SEL_PROMPT // 8):
                    link(nc.vector.max(top8[0:r, :], SC[t][0:r, :]))
                    link(nc.vector.match_replace(SC[t][0:r, :], top8[0:r, :], SC[t][0:r, :], TAKEN))
                if t == NT - 1:
                    for n in range((SEL_SAMPLE - SEL_PROMPT) // 8):
                        link(nc.vector.max(top8[64:96, :], SC[t][64:96, :]))
                        link(nc.vector.match_replace(SC[t][64:96, :], top8[64:96, :], SC[t][64:96, :], TAKEN))
                link(nc.vector.tensor_scalar(SC[t][0:r, :], SC[t][0:r, :], TAKEN, -BIG, ALU.not_equal, ALU.mult))

            dve.wait_ge(keys_out, 16 * 6 * (NT + 1))
            for i in range(NSTEP + 1):
                if i < NSTEP:
                    s = STEPS[i]
                    dve.wait_ge(z_ready, i + 1)
                    if i >= SPR:
                        dve.wait_ge(logw_ready, i - SPR + 1)
                        dve.wait_ge(suf_ready, i - SPR + 1)
                    nc.vector.tensor_scalar(spb[0:s["nk"], i % SPR, 0:s["n"]], bank[2 + i % ZR][0:s["nk"], 0:s["n"]],
                                            Z_CAP, None, ALU.min).then_inc(cap_ready, 1)
                m = i - 1
                if m >= 0:
                    s = STEPS[m]
                    dve.wait_ge(ln_ready, m + 1)
                    v = spb[0:s["nk"], m % SPR, 0:s["n"]]
                    nc.vector.tensor_tensor(v, bank[2 + m % ZR][0:s["nk"], 0:s["n"]], v, ALU.max)\
                        .then_inc(sp_ready, 1)

            jobs = [(t, h) for t in range(NT) for h in range(NH)]

            def normalize(m):
                r, w = ROWS[jobs[m][0]], KEYS[jobs[m][0]]
                dve.wait_ge(p_ready, m + 1)
                link(nc.vector.reciprocal(rsum[0:r, m % PR:m % PR + 1], rsum[0:r, m % PR:m % PR + 1]))
                nc.vector.tensor_scalar(pb[0:r, m % PR, 0:w], pb[0:r, m % PR, 0:w], rsum[0:r, m % PR:m % PR + 1], None,
                                        ALU.mult).then_inc(pn_ready, 1)

            for i, (t, h) in enumerate(jobs):
                r, w = ROWS[t], KEYS[t]
                dve.wait_ge(lg_ready, i + 1)
                if i >= LR:
                    dve.wait_ge(p_ready, i - LR + 1)
                pr = pairs[i % 2]
                if t < NT - 1:
                    src, bias, dst = pr[0:r, 0:w], SC[t][0:r, :], Lb[0:r, i % LR, 0:w]
                else:
                    src = pr[0:r, :].rearrange("p (b c) -> p b c", b=2)[:, :, 0:272]
                    bias = SC[t][0:r, :].rearrange("p (b c) -> p b c", b=2)
                    dst = Lb[0:r, i % LR, 0:w].rearrange("p (b c) -> p b c", b=2)
                link(nc.vector.tensor_tensor_reduce(out=dst, in0=src, in1=bias, scale=1.0, scalar=HIDDEN,
                                                    op0=ALU.add, op1=ALU.max, accum_out=mx[0:r, i % LR:i % LR + 1]))
                link(nc.vector.tensor_scalar(nbias[0:r, i % LR:i % LR + 1], mx[0:r, i % LR:i % LR + 1], -HD ** -0.5, None,
                                             ALU.mult))
                nc.vector.sem_inc(lb_ready, 1)
                if i >= LR - 1:
                    normalize(i - LR + 1)
            for m in range(len(jobs) - LR + 1, len(jobs)):
                normalize(m)

            for j in range(16):
                cb, g = j // 2, j % 2
                lo, hi = FG[g]
                n = J_A + j
                dve.wait_ge(pj_ready, n + 1)
                dve.wait_ge(gate_ready, j + 1)
                link(nc.vector.tensor_tensor(merged[:, cb, lo:hi], bank[n % 4][:, 0:hi - lo], merged[:, cb, lo:hi],
                                             ALU.mult))
                nc.vector.sem_inc(pj_free_dve, 1)
            for j in range(16):
                cb, g = j // 2, j % 2
                lo, hi = FG[g]
                n = J_GB + 2 * j + 1
                dve.wait_ge(pj_ready, n + 1)
                dve.wait_ge(gate_ready, 17 + j)
                gt = tabs[:, (j % 2) * 280:(j % 2) * 280 + hi - lo]
                link(nc.vector.tensor_tensor(gt, bank[n % 4][:, 0:hi - lo], gt, ALU.mult))
                nc.vector.sem_inc(pj_free_dve, 1)
                link(nc.vector.tensor_tensor(merged[:, cb, lo:hi], merged[:, cb, lo:hi], gt, ALU.add))
                nc.vector.sem_inc(half_merged, 1)
                nc.vector.sem_inc(merged_ready, 1)
            def second_norm(t):
                r = ROWS[t]
                if t >= 2:
                    dve.wait_ge(x2_stored[t - 2], 16)
                    dve.wait_ge(tr_ready, T_X2 + 2 * (t - 2) + 2)
                dve.wait_ge(rstd2_ready, t + 1)
                nc.vector.scalar_tensor_tensor(x2row[0:r, t % 2, :], X[0:r, t, :], rstd[0:r, t:t + 1], g2b[0:r, :],
                                               ALU.mult, ALU.mult).then_inc(x2_ready, 1)

            dve.wait_ge(xres_in, 16 * (NT + 2))
            dve.wait_ge(g2_in, 16)
            for t in range(NT + 1):
                if t < NT:
                    r = ROWS[t]
                    for c in range(2):
                        n = J_WO + 2 * t + c
                        dve.wait_ge(pj_ready, n + 1)
                        v = X[0:r, t, 512 * c:512 * (c + 1)]
                        link(nc.vector.tensor_tensor(v, bank[n % 4][0:r, :], v, ALU.add))
                        nc.vector.sem_inc(pj_free_dve, 1)
                    nc.vector.sem_inc(h_ready, 1)
                if t:
                    second_norm(t - 1)

            def per_row(v, n):
                return v.rearrange("p (t o) -> p t o", o=1).broadcast_to([P, v.shape[1], n])

            def counting(m, n):
                return iota[:, 0:n].rearrange("p (o e) -> p o e", o=1).broadcast_to([P, m, n])

            def tt(o, x, y, op):
                link(nc.vector.tensor_tensor(o, x, y, op))

            def ts(o, x, c1, c2, op0, op1=None):
                if op1 is None:
                    link(nc.vector.tensor_scalar(o, x, c1, None, op0))
                else:
                    link(nc.vector.tensor_scalar(o, x, c1, c2, op0, op1))

            def stt(o, x, c1, y, op0, op1):
                link(nc.vector.scalar_tensor_tensor(o, x, c1, y, op0, op1))

            def red(o, x, op):
                link(nc.vector.tensor_reduce(o, x, AX.X, op))

            def first_of(o, eq, n):
                stt(eq, counting(NT, n), -100.0, eq, ALU.add, ALU.mult)
                red(v_first, eq, ALU.min)
                stt(o, counting(NT, n), -100.0, per_row(v_first, n), ALU.add, ALU.is_equal)

            link(nc.vector.memset(marks[:, :, 0:1], 0.0))
            link(nc.vector.memset(go_on, 1.0))
            link(nc.vector.memset(go_on[:, :, 0:1], 0.0))
            link(nc.vector.memset(ones, 1.0))
            ts(by_cap, iota[:, 0:NE], -float(CAP), float(CAP * (NE - 1)), ALU.mult, ALU.add)

            dve.wait_ge(logits_ready, 1)
            g = rl[:, :, 0:NG]
            d = gx[:, 0:NG * NT].rearrange("p (t g) -> p t g", t=NT)
            red(v_max, g, ALU.max)
            tt(d, g, per_row(v_max, NG), ALU.subtract)
            nc.vector.sem_inc(rvals_ready, 1)
            tt(g_eq, g, per_row(v_max, NG), ALU.is_equal)
            first_of(g_eq, g_eq, NG)
            masked, eq = (tabs[:, i * NT * NE:(i + 1) * NT * NE].rearrange("p (t e) -> p t e", t=NT) for i in range(2))
            ts(g_eq, g_eq, -1.0, BIG, ALU.add, ALU.mult)
            tt(masked.rearrange("p t (g e) -> p t g e", g=NG),
               rl[:, :, NG:].rearrange("p t (g e) -> p t g e", g=NG),
               g_eq.rearrange("p t (g o) -> p t g o", o=1).broadcast_to([P, NT, NG, EPG]), ALU.add)
            for c in range(2):
                red(v_top[c], masked, ALU.max)
                tt(eq, masked, per_row(v_top[c], NE), ALU.is_equal)
                first_of(oh[:, c], eq, NE)
                if c == 0:
                    stt(masked, oh[:, 0], -BIG, masked, ALU.mult, ALU.add)
            ex = gx[:, 40:40 + NT]
            tt(ex, v_top[1], v_top[0], ALU.subtract)
            nc.vector.sem_inc(rvals_ready, 1)
            for c in range(2):
                tt(oh[:, c], oh[:, c], per_row(valid, NE), ALU.mult)
            tt(marks[:, :, 1:].rearrange("p e t -> p t e"), oh[:, 0], oh[:, 1], ALU.add)
            link(nc.vector.tensor_tensor_scan(earlier.rearrange("p e t -> p (e t)"), go_on.rearrange("p e t -> p (e t)"),
                                              marks.rearrange("p e t -> p (e t)"), 0.0, ALU.mult, ALU.subtract))
            nc.vector.sem_inc(onehot_ready, 1)
            dve.wait_ge(rexp_ready, 2)
            red(v_gp, d, ALU.add)
            ts(ew[0], ex, 1.0, None, ALU.add)
            tt(ew[0], ew[0], v_gp, ALU.mult)
            link(nc.vector.reciprocal(ew[0], ew[0]))
            tt(ew[1], ew[0], ex, ALU.mult)
            dve.wait_ge(pos_ready, 1)
            pos = bank[0][:, 0:NT * NE].rearrange("p (t e) -> p t e", t=NT)
            cnt = bank[0][:, NT * NE:(NT + 1) * NE]
            cmp = tabs[:, 0:8 * NE].rearrange("p (e k) -> p e k", k=8)
            tt(cmp, cnt.rearrange("p (e o) -> p e o", o=1).broadcast_to([P, NE, 8]),
               thr.rearrange("p (o k) -> p o k", o=1).broadcast_to([P, NE, 8]), ALU.is_gt)
            red(blocks, cmp, ALU.add)
            link(nc.vector.tensor_tensor_scan(upto, ones, blocks, 0.0, ALU.mult, ALU.add))
            tt(over_base, upto, blocks, ALU.subtract)
            stt(over_base, over_base, float(CAP), by_cap, ALU.mult, ALU.add)
            own, past = (tabs[:, 8 * NE + i * NT * NE:8 * NE + (i + 1) * NT * NE].rearrange("p (t e) -> p t e", t=NT)
                         for i in range(2))
            stt(own, counting(NT, NE), float(CAP), pos, ALU.mult, ALU.add)
            stt(past, pos, float(CAP), over_base.rearrange("p (o e) -> p o e", o=1).broadcast_to([P, NT, NE]),
                ALU.is_ge, ALU.mult)
            tt(own, own, past, ALU.add)
            picked = tabs[:, 640:640 + 2 * NT * NE].rearrange("p (c t e) -> p c t e", c=2, t=NT)
            for c in range(2):
                tt(picked[:, c], oh[:, c], own, ALU.mult)
            red(v_slot, picked.rearrange("p c t e -> p (c t) e"), ALU.add)
            link(nc.vector.tensor_copy(slot_i[:, :], v_slot))
            for t in (NT - 2, NT - 1):
                dve.wait_ge(x2_stored[t], 16)
            for i, (op, arg, dst, n) in enumerate(((ALU.bitwise_and, CAP - 1, at_slot, CAP),
                                                   (ALU.logical_shift_right, CAP.bit_length() - 1, at_block, NBLK))):
                link(nc.vector.tensor_scalar(slot_part[i][:, :], slot_i[:, :], arg, None, op))
                link(nc.vector.tensor_copy(v_slot, slot_part[i][:, :]))
                tt(dst, counting(2 * NT, n), per_row(v_slot, n), ALU.is_equal)
            for c in range(2):
                tt(at_block[:, c * NT:(c + 1) * NT], at_block[:, c * NT:(c + 1) * NT], per_row(rid, NBLK), ALU.mult)
            nc.vector.sem_inc(slots_ready, 1)
            m17 = rt[0:1, 0:MAX_OVER * NE].rearrange("p (b e) -> p b e", b=MAX_OVER)
            tt(m17, upto[0:1].rearrange("p (o e) -> p o e", o=1).broadcast_to([1, MAX_OVER, NE]),
               iota[0:1, 0:MAX_OVER].rearrange("p (b o) -> p b o", o=1).broadcast_to([1, MAX_OVER, NE]), ALU.is_le)
            o17 = ones[0:1, 0:MAX_OVER]
            red(o17, m17, ALU.add)
            ts(o17, o17, float(NE - 1), None, ALU.min)
            link(nc.vector.tensor_copy(over_i[0:1, 0:MAX_OVER], o17))
            link(nc.vector.tensor_copy(over_i[0:1, MAX_OVER:MAX_OVER + 1], upto[0:1, NE - 1:NE]))
            dve.wait_ge(idx_ready, 1)
            nc.vector.tensor_copy(idxs[:, :], bank[1][0:CAP, 0:NBLK]).then_inc(idx_in, 1)

            def hidden(q, done):
                nc.vector.tensor_tensor(hid[:, q, :], sil[:, q, :], bank[4 * q + 1][:, P:2 * P], ALU.mult)\
                    .then_inc(done, 1)

            def copy_hidden(q, done):
                nc.vector.tensor_copy(hidT[:, q, :], bank[4 * q + 2][:, 0:P]).then_inc(done, 1)

            with dve.Fori(0, NE // 2) as i:
                for q in range(2):
                    dve.wait_ge(silu_ready, i * 2 + q + 1)
                    hidden(q, hid_ready)
                    dve.wait_ge(hT_ready, i * 2 + q + 1)
                    copy_hidden(q, hidT_ready)
            over = dve.value_load(over_i[0:1, MAX_OVER:MAX_OVER + 1], min_val=0, max_val=MAX_OVER)
            with dve.If(over > 0):
                with dve.Fori(0, MAX_OVER) as b:
                    dve.wait_ge(o_step, b * 10 + 4)
                    hidden(0, o_step)
                    dve.wait_ge(o_step, b * 10 + 6)
                    copy_hidden(0, o_step)
            for t in range(NT):
                r = ROWS[t]
                for c in range(2):
                    n = 2 * t + c
                    dve.wait_ge(comb_in[n], 16)
                    link(nc.vector.scalar_tensor_tensor(X[0:r, t, :], arena[0:r, n * D:(n + 1) * D],
                                                        ew[c][0:r, t:t + 1], X[0:r, t, :], ALU.mult, ALU.add))
                nc.vector.sem_inc(final_ready, 1)


_SHAPES = {
    "y_prompt": [SEQ, D], "y_sample": [DEC, D],
    "sk_p": [N_PROMPT, 512], "sv_p": [N_PROMPT, 512], "dk_p": [N_PROMPT, 2, HD], "dv_p": [N_PROMPT, 128],
    "ik_p": [N_PROMPT, HD],
    "sk_s": [DEC, 512], "sv_s": [DEC, 512], "dk_s": [DEC, 2, HD], "dv_s": [DEC, 128], "ik_s": [DEC, HD],
}
_RETURNED = [
    (1, SEQ, D), (1, DEC, D),
    (1, 1, N_PROMPT, NH, HD), (1, 1, N_PROMPT, NH, HD), (1, 1, N_PROMPT, 2, HD), (1, 1, N_PROMPT, 2, HD),
    (1, 1, N_PROMPT, HD),
    (1, 1, DEC, NH, HD), (1, 1, DEC, NH, HD), (1, 1, DEC, 2, HD), (1, 1, DEC, 2, HD), (1, 1, DEC, HD),
]


def kernel(**inputs):
    import numpy as _np
    import concourse.bacc as _bacc
    from concourse import mybir as _mybir
    from concourse.bass_utils import run_bass_kernel_spmd as _run

    shapes = {
        "x_prompt": (SEQ, D), "x_sample": (DEC, D), "cache_sb_k": (PAST, 512), "cache_sb_v": (PAST, 512),
        "cache_dsa_k": (PAST, 2, HD), "cache_dsa_v": (PAST, 128), "cache_idx_k": (PAST, HD),
        "meta_tokens": (N_META, D), "norm1_g": (D,), "w_in": (D, 4936), "dsa_q_norm_g": (HD,),
        "dsa_k_norm_g": (HD,), "w_sb_branch": (512, D), "w_dsa_branch": (512, D), "w_out": (D, D),
        "norm2_g": (D,), "w_group": (D, NG), "w_router": (D, NE), "w_gate": (NE, D, FE), "w_up": (NE, D, FE),
        "w_down": (NE, FE, D),
    }
    nc = _bacc.Bacc("TRN2", target_bir_lowering=False, num_devices=1)
    arrays = {n: _np.ascontiguousarray(inputs[n]).reshape(s) for n, s in shapes.items()}
    arrays["consts"] = constants()
    arrays = {f"in_{n}": v for n, v in arrays.items()}
    args = {n[3:]: nc.dram_tensor(n, v.shape, _mybir.dt.from_np(v.dtype), kind="ExternalInput").ap()
            for n, v in arrays.items()}
    outs = {n: nc.dram_tensor(f"out_{n}", s, _mybir.dt.float32, kind="ExternalOutput").ap()
            for n, s in _SHAPES.items()}
    build(nc, args, outs)
    r = _run(nc, [arrays], core_ids=[0])
    return tuple(r.results[0][f"out_{n}"].reshape(s) for n, s in zip(_SHAPES, _RETURNED))
```
